# Optimizing a Trainium2 kernel written in Bass

```python
import jax, jax.numpy as jnp
from jax import lax
import numpy as np
import math

D_MODEL = 1024
BATCH = 1
SEQ = 512
DEPTH = 1

N_META = 16
D_MIX = D_MODEL
HEAD_DIM = 64
D_ATTN = D_MIX // 2
N_ATTN_HEADS = D_ATTN // HEAD_DIM
D_CONV = D_MIX - D_ATTN
N_CONV_GROUPS = D_CONV // HEAD_DIM
CONV_WIDTH = 3
D_FF = 4 * D_MODEL
Q_BLOCK = 128
EPS = 1e-5
NEG_INF = -1e30
D_IN_PROJ = 3 * D_ATTN + N_ATTN_HEADS + 3 * D_CONV


def rms_norm(x, g):
    xf = x.astype(jnp.float32)
    y = xf * lax.rsqrt(jnp.mean(xf * xf, axis=-1, keepdims=True) + EPS)
    return (y * g.astype(jnp.float32)).astype(x.dtype)

def head_rms_norm(y, n_groups, g):
    b, l, c = y.shape
    yf = y.astype(jnp.float32).reshape(b, l, n_groups, c // n_groups)
    yf = yf * lax.rsqrt(jnp.mean(yf * yf, axis=-1, keepdims=True) + EPS)
    return (yf.reshape(b, l, c) * g.astype(jnp.float32)).astype(y.dtype)

def forgetting_attention(q, k, v, log_f):
    L = q.shape[1]
    cum = jnp.cumsum(log_f.astype(jnp.float32), axis=1).transpose(0, 2, 1)
    scale = HEAD_DIM ** -0.5
    n_blocks = (L - N_META) // Q_BLOCK
    bounds = [(0, N_META)] + [(N_META + i * Q_BLOCK, N_META + (i + 1) * Q_BLOCK)
                              for i in range(n_blocks)]
    outs = []
    for lo, hi in bounds:
        qb, kb, vb = q[:, lo:hi], k[:, :hi], v[:, :hi]
        s = jnp.einsum('bqhd,bkhd->bhqk', qb, kb,
                       preferred_element_type=jnp.float32) * scale
        decay = cum[:, :, lo:hi, None] - cum[:, :, None, :hi]
        causal = jnp.arange(hi)[None, :] <= jnp.arange(lo, hi)[:, None]
        s = jnp.where(causal, s + decay, NEG_INF)
        p = jax.nn.softmax(s, axis=-1)
        outs.append(jnp.einsum('bhqk,bkhd->bqhd', p.astype(vb.dtype), vb))
    return jnp.concatenate(outs, axis=1)

def causal_depthwise_conv(u, w):
    L = u.shape[1]
    up = jnp.pad(u, ((0, 0), (CONV_WIDTH - 1, 0), (0, 0)))
    y = w[0] * up[:, 0:L]
    for kk in range(1, CONV_WIDTH):
        y = y + w[kk] * up[:, kk:kk + L]
    return y

def first_inputs(seed: int = 0) -> dict:
    key = jax.random.key(seed)
    ks = jax.random.split(key, 14)
    f32 = jnp.float32
    x = jax.random.normal(ks[0], (BATCH, SEQ, D_MODEL), f32)
    meta_tokens = jax.random.normal(ks[1], (N_META, D_MODEL), f32)
    norm_mix_g = 1.0 + 0.02 * jax.random.normal(ks[2], (DEPTH, D_MODEL), f32)
    w_in = jax.random.normal(ks[3], (DEPTH, D_MODEL, D_IN_PROJ), f32) * D_MODEL ** -0.5
    b_f = (jnp.linspace(1.0, 6.0, N_ATTN_HEADS, dtype=f32)[None, :]
           + 0.1 * jax.random.normal(ks[4], (DEPTH, N_ATTN_HEADS), f32))
    conv_w = jax.random.normal(ks[5], (DEPTH, CONV_WIDTH, D_CONV), f32) * CONV_WIDTH ** -0.5
    out_norm_g = 1.0 + 0.02 * jax.random.normal(ks[6], (DEPTH, D_MIX), f32)
    w_out = jax.random.normal(ks[7], (DEPTH, D_MIX, D_MODEL), f32) * D_MIX ** -0.5
    norm_mlp_g = 1.0 + 0.02 * jax.random.normal(ks[8], (DEPTH, D_MODEL), f32)
    w_ff1 = jax.random.normal(ks[9], (DEPTH, D_MODEL, D_FF), f32) * D_MODEL ** -0.5
    w_ff2 = jax.random.normal(ks[10], (DEPTH, D_FF, D_MODEL), f32) * D_FF ** -0.5
    final_norm_g = 1.0 + 0.02 * jax.random.normal(ks[11], (D_MODEL,), f32)
    return {"x": x, "meta_tokens": meta_tokens, "norm_mix_g": norm_mix_g, "w_in": w_in,
            "b_f": b_f, "conv_w": conv_w, "out_norm_g": out_norm_g, "w_out": w_out,
            "norm_mlp_g": norm_mlp_g, "w_ff1": w_ff1, "w_ff2": w_ff2,
            "final_norm_g": final_norm_g}

def first_block(x, meta_tokens, norm_mix_g, w_in, b_f, conv_w, out_norm_g, w_out,
              norm_mlp_g, w_ff1, w_ff2, final_norm_g):
    B = x.shape[0]
    meta = jnp.broadcast_to(meta_tokens.astype(x.dtype)[None], (B, N_META, D_MODEL))
    h = jnp.concatenate([meta, x], axis=1)
    L = h.shape[1]
    split_at = [D_ATTN, 2 * D_ATTN, 3 * D_ATTN, 3 * D_ATTN + N_ATTN_HEADS,
                3 * D_ATTN + N_ATTN_HEADS + D_CONV, 3 * D_ATTN + N_ATTN_HEADS + 2 * D_CONV]
    for layer in range(DEPTH):
        xn = rms_norm(h, norm_mix_g[layer])
        proj = jnp.einsum('bld,de->ble', xn, w_in[layer])
        q, k, v, f_logit, b_gate, c_gate, u = jnp.split(proj, split_at, axis=-1)
        log_f = jax.nn.log_sigmoid(f_logit.astype(jnp.float32) + b_f[layer].astype(jnp.float32))
        hs = (B, L, N_ATTN_HEADS, HEAD_DIM)
        y_attn = forgetting_attention(q.reshape(hs), k.reshape(hs), v.reshape(hs), log_f)
        y_attn = y_attn.reshape(B, L, D_ATTN)
        y_conv = b_gate * causal_depthwise_conv(c_gate * u, conv_w[layer].astype(u.dtype))
        y = jnp.concatenate([head_rms_norm(y_attn, N_ATTN_HEADS, out_norm_g[layer, :D_ATTN]),
                             head_rms_norm(y_conv, N_CONV_GROUPS, out_norm_g[layer, D_ATTN:])],
                            axis=-1)
        h = h + jnp.einsum('ble,ed->bld', y, w_out[layer])
        hn = rms_norm(h, norm_mlp_g[layer])
        a = jnp.square(jax.nn.relu(jnp.einsum('bld,df->blf', hn, w_ff1[layer])))
        h = h + jnp.einsum('blf,fd->bld', a, w_ff2[layer])
    h = rms_norm(h, final_norm_g)
    return h[:, N_META:]


DEPTH_2 = 2

N_A_LAYERS = DEPTH_2 // 2
N_B_LAYERS = DEPTH_2 - N_A_LAYERS
PLE_DIM = 256
SSM_DIM = D_MODEL
SSM_GROUP_DIM = 16
SSM_GROUPS = SSM_DIM // SSM_GROUP_DIM
SSM_STATE = 64
SSM_CHUNK = 128
N_HEADS = 8
REL_BUCKETS = 32
REL_MAX_EXACT = REL_BUCKETS // 2
REL_MAX_DIST = 128
D_FF_2 = 2816
NEG_INF_2 = -1e30
EPS_2 = 1e-6


def rms_norm_2(x, g):
    xf = x.astype(jnp.float32)
    y = xf * lax.rsqrt(jnp.mean(xf * xf, axis=-1, keepdims=True) + EPS_2)
    return (y * g.astype(jnp.float32)).astype(x.dtype)

def _ssm_combine(e_i, e_j):
    ar_i, ai_i, br_i, bi_i = e_i
    ar_j, ai_j, br_j, bi_j = e_j
    return (ar_j * ar_i - ai_j * ai_i,
            ar_j * ai_i + ai_j * ar_i,
            ar_j * br_i - ai_j * bi_i + br_j,
            ar_j * bi_i + ai_j * br_i + bi_j)

def s5_mixer(h, w_in, log_dt, lam_re, lam_im, b_re, b_im, c_re, c_im, d_skip, w_glu):
    f32 = jnp.float32
    bsz, seqlen, _ = h.shape
    u = h @ w_in
    dt = jnp.exp(log_dt.astype(f32))[:, None]
    lr = lam_re.astype(f32)
    li = lam_im.astype(f32)
    mag = jnp.exp(lr * dt)
    ab_r = mag * jnp.cos(li * dt)
    ab_i = mag * jnp.sin(li * dt)
    den = lr * lr + li * li
    f_r = ((ab_r - 1.0) * lr + ab_i * li) / den
    f_i = (ab_i * lr - (ab_r - 1.0) * li) / den
    br = b_re.astype(f32)
    bi = b_im.astype(f32)
    bb_r = f_r[..., None] * br - f_i[..., None] * bi
    bb_i = f_r[..., None] * bi + f_i[..., None] * br
    cr = c_re.astype(f32)
    ci = c_im.astype(f32)
    n_chunks = seqlen // SSM_CHUNK
    uc = u.astype(f32).reshape(bsz, n_chunks, SSM_CHUNK, SSM_GROUPS, SSM_GROUP_DIM)
    uc = uc.transpose(1, 2, 0, 3, 4)
    a_shape = (SSM_CHUNK, bsz, SSM_GROUPS, SSM_STATE)
    a_r = jnp.broadcast_to(ab_r, a_shape)
    a_i = jnp.broadcast_to(ab_i, a_shape)

    def chunk_step(carry, u_chunk):
        x_r0, x_i0 = carry
        bu_r = jnp.einsum("tbgc,gpc->tbgp", u_chunk, bb_r)
        bu_i = jnp.einsum("tbgc,gpc->tbgp", u_chunk, bb_i)
        pw_r, pw_i, s_r, s_i = lax.associative_scan(
            _ssm_combine, (a_r, a_i, bu_r, bu_i), axis=0)
        x_r = s_r + pw_r * x_r0 - pw_i * x_i0
        x_i = s_i + pw_r * x_i0 + pw_i * x_r0
        y = (jnp.einsum("tbgp,gcp->tbgc", x_r, cr)
             - jnp.einsum("tbgp,gcp->tbgc", x_i, ci))
        return (x_r[-1], x_i[-1]), y

    zeros = jnp.zeros((bsz, SSM_GROUPS, SSM_STATE), f32)
    _, ys = lax.scan(chunk_step, (zeros, zeros), uc)
    y = ys.transpose(2, 0, 1, 3, 4).reshape(bsz, seqlen, SSM_DIM)
    y = y + d_skip.astype(f32) * u.astype(f32)
    g = jax.nn.gelu(y).astype(h.dtype)
    val, gate = jnp.split(g @ w_glu, 2, axis=-1)
    return val * jax.nn.sigmoid(gate)

def t5_causal_bucket(rel):
    n = jnp.maximum(-rel, 0)
    nf = jnp.maximum(n, REL_MAX_EXACT).astype(jnp.float32)
    large = REL_MAX_EXACT + (jnp.log(nf / REL_MAX_EXACT)
                             / math.log(REL_MAX_DIST / REL_MAX_EXACT)
                             * (REL_BUCKETS - REL_MAX_EXACT)).astype(jnp.int32)
    large = jnp.minimum(large, REL_BUCKETS - 1)
    return jnp.where(n < REL_MAX_EXACT, n, large)

def shared_kv(x, kv_norm, kv_w, k_norm):
    bsz, seqlen, _ = x.shape
    kv = rms_norm_2(x, kv_norm) @ kv_w
    nk = 2 * N_HEADS * HEAD_DIM
    k = rms_norm_2(kv[..., :nk].reshape(bsz, seqlen, N_HEADS, 2, HEAD_DIM), k_norm)
    v = kv[..., nk:].reshape(bsz, seqlen, N_HEADS, 2 * HEAD_DIM)
    return k, v

def diff_attention(h, k, v, rel_bias, w_q, q_norm, lq1, lk1, lq2, lk2, subln, w_o, lam_init):
    f32 = jnp.float32
    bsz, seqlen, _ = h.shape
    q = rms_norm_2((h @ w_q).reshape(bsz, seqlen, N_HEADS, 2, HEAD_DIM), q_norm)
    lam = (jnp.exp(jnp.sum(lq1.astype(f32) * lk1.astype(f32)))
           - jnp.exp(jnp.sum(lq2.astype(f32) * lk2.astype(f32))) + lam_init)
    scale = HEAD_DIM ** -0.5
    n_blocks = seqlen // Q_BLOCK
    qb = q.reshape(bsz, n_blocks, Q_BLOCK, N_HEADS, 2, HEAD_DIM).transpose(1, 0, 2, 3, 4, 5)
    k_pos = jnp.arange(seqlen)

    def block(args):
        idx, qc = args
        q_pos = idx * Q_BLOCK + jnp.arange(Q_BLOCK)
        rel = k_pos[None, :] - q_pos[:, None]
        bias = rel_bias[t5_causal_bucket(rel)].astype(f32).transpose(2, 0, 1)
        s = jnp.einsum("bqhcd,bkhcd->bhcqk", qc, k).astype(f32) * scale
        s = s + bias[None, :, None]
        s = jnp.where(rel <= 0, s, NEG_INF_2)
        pm = jax.nn.softmax(s, axis=-1)
        attn = pm[:, :, 0] - lam * pm[:, :, 1]
        return jnp.einsum("bhqk,bkhe->bqhe", attn.astype(v.dtype), v)

    o = lax.map(block, (jnp.arange(n_blocks), qb))
    o = o.transpose(1, 0, 2, 3, 4).reshape(bsz, seqlen, N_HEADS, 2 * HEAD_DIM)
    o = rms_norm_2(o, subln) * (1.0 - lam_init)
    return o.reshape(bsz, seqlen, N_HEADS * 2 * HEAD_DIM) @ w_o

def conv_ffn(h, w_up, conv_w, conv_b, w_down):
    up = h @ w_up
    seqlen = up.shape[1]
    padded = jnp.pad(up, ((0, 0), (CONV_WIDTH - 1, 0), (0, 0)))
    c = conv_b
    for j in range(CONV_WIDTH):
        c = c + conv_w[j] * padded[:, j:j + seqlen]
    g, val = jnp.split(c, 2, axis=-1)
    return (jax.nn.gelu(g) * val) @ w_down

def second_inputs(seed: int = 0) -> dict:
    key = jax.random.key(seed)
    ks = iter(jax.random.split(key, 40))
    f32 = jnp.float32

    def nrm(shape, scale):
        return jax.random.normal(next(ks), shape, f32) * scale

    def gain(shape):
        return 1.0 + nrm(shape, 0.05)

    na, nb = N_A_LAYERS, N_B_LAYERS
    lam_im = jnp.pi * jnp.arange(SSM_STATE, dtype=f32)
    return {
        "x": nrm((BATCH, SEQ, D_MODEL), 1.0),
        "p": nrm((DEPTH_2, BATCH, SEQ, PLE_DIM), 1.0),
        "ssm_norm": gain((na, D_MODEL)),
        "ssm_w_in": nrm((na, D_MODEL, SSM_DIM), D_MODEL ** -0.5),
        "ssm_log_dt": jax.random.uniform(next(ks), (na, SSM_GROUPS), f32,
                                         math.log(1e-3), math.log(1e-1)),
        "ssm_lambda_re": -0.5 + nrm((na, SSM_GROUPS, SSM_STATE), 0.01),
        "ssm_lambda_im": lam_im + nrm((na, SSM_GROUPS, SSM_STATE), 0.01),
        "ssm_b_re": nrm((na, SSM_GROUPS, SSM_STATE, SSM_GROUP_DIM), SSM_GROUP_DIM ** -0.5),
        "ssm_b_im": nrm((na, SSM_GROUPS, SSM_STATE, SSM_GROUP_DIM), SSM_GROUP_DIM ** -0.5),
        "ssm_c_re": nrm((na, SSM_GROUPS, SSM_GROUP_DIM, SSM_STATE), SSM_STATE ** -0.5),
        "ssm_c_im": nrm((na, SSM_GROUPS, SSM_GROUP_DIM, SSM_STATE), SSM_STATE ** -0.5),
        "ssm_d": nrm((na, SSM_DIM), 0.5),
        "ssm_w_glu": nrm((na, SSM_DIM, 2 * D_MODEL), SSM_DIM ** -0.5),
        "kv_norm": gain((D_MODEL,)),
        "kv_w": nrm((D_MODEL, 2 * N_HEADS * HEAD_DIM + N_HEADS * 2 * HEAD_DIM), D_MODEL ** -0.5),
        "k_norm": gain((HEAD_DIM,)),
        "attn_norm": gain((nb, D_MODEL)),
        "attn_w_q": nrm((nb, D_MODEL, 2 * N_HEADS * HEAD_DIM), D_MODEL ** -0.5),
        "q_norm": gain((nb, HEAD_DIM)),
        "lambda_q1": nrm((nb, HEAD_DIM), 0.1),
        "lambda_k1": nrm((nb, HEAD_DIM), 0.1),
        "lambda_q2": nrm((nb, HEAD_DIM), 0.1),
        "lambda_k2": nrm((nb, HEAD_DIM), 0.1),
        "subln": gain((nb, 2 * HEAD_DIM)),
        "attn_w_o": nrm((nb, N_HEADS * 2 * HEAD_DIM, D_MODEL), (N_HEADS * 2 * HEAD_DIM) ** -0.5),
        "rel_bias": nrm((REL_BUCKETS, N_HEADS), 0.5),
        "ffn_norm": gain((DEPTH_2, D_MODEL)),
        "ffn_w_up": nrm((DEPTH_2, D_MODEL, 2 * D_FF_2), D_MODEL ** -0.5),
        "ffn_conv_w": nrm((DEPTH_2, CONV_WIDTH, 2 * D_FF_2), CONV_WIDTH ** -0.5),
        "ffn_conv_b": nrm((DEPTH_2, 2 * D_FF_2), 0.02),
        "ffn_w_down": nrm((DEPTH_2, D_FF_2, D_MODEL), D_FF_2 ** -0.5),
        "ple_norm": gain((DEPTH_2, D_MODEL)),
        "ple_w_gate": nrm((DEPTH_2, D_MODEL, D_MODEL), D_MODEL ** -0.5),
        "ple_w_proj": nrm((DEPTH_2, PLE_DIM, D_MODEL), PLE_DIM ** -0.5),
    }

def second_block(x, p, ssm_norm, ssm_w_in, ssm_log_dt, ssm_lambda_re, ssm_lambda_im,
              ssm_b_re, ssm_b_im, ssm_c_re, ssm_c_im, ssm_d, ssm_w_glu,
              kv_norm, kv_w, k_norm, attn_norm, attn_w_q, q_norm,
              lambda_q1, lambda_k1, lambda_q2, lambda_k2, subln, attn_w_o, rel_bias,
              ffn_norm, ffn_w_up, ffn_conv_w, ffn_conv_b, ffn_w_down,
              ple_norm, ple_w_gate, ple_w_proj):
    k = v = None
    for i in range(DEPTH_2):
        if i < N_A_LAYERS:
            h = rms_norm_2(x, ssm_norm[i])
            x = x + s5_mixer(h, ssm_w_in[i], ssm_log_dt[i], ssm_lambda_re[i], ssm_lambda_im[i],
                             ssm_b_re[i], ssm_b_im[i], ssm_c_re[i], ssm_c_im[i],
                             ssm_d[i], ssm_w_glu[i])
        else:
            if i == N_A_LAYERS:
                k, v = shared_kv(x, kv_norm, kv_w, k_norm)
            j = i - N_A_LAYERS
            lam_init = 0.8 - 0.6 * math.exp(-0.3 * i)
            h = rms_norm_2(x, attn_norm[j])
            x = x + diff_attention(h, k, v, rel_bias, attn_w_q[j], q_norm[j],
                                   lambda_q1[j], lambda_k1[j], lambda_q2[j], lambda_k2[j],
                                   subln[j], attn_w_o[j], lam_init)
        h = rms_norm_2(x, ffn_norm[i])
        x = x + conv_ffn(h, ffn_w_up[i], ffn_conv_w[i], ffn_conv_b[i], ffn_w_down[i])
        gate = jax.nn.sigmoid(rms_norm_2(x, ple_norm[i]) @ ple_w_gate[i])
        x = x + gate * (p[i] @ ple_w_proj[i])
    return x


def setup_inputs(seed=0):
    out = dict(first_inputs(seed))
    for name, value in second_inputs(seed + 1).items():
        if name != "x":
            out[name + "_2"] = value
    return out


def reference(
    x, meta_tokens, norm_mix_g, w_in, b_f, conv_w, out_norm_g, w_out, norm_mlp_g, w_ff1, w_ff2,
    final_norm_g, p_2, ssm_norm_2, ssm_w_in_2, ssm_log_dt_2, ssm_lambda_re_2, ssm_lambda_im_2,
    ssm_b_re_2, ssm_b_im_2, ssm_c_re_2, ssm_c_im_2, ssm_d_2, ssm_w_glu_2, kv_norm_2, kv_w_2,
    k_norm_2, attn_norm_2, attn_w_q_2, q_norm_2, lambda_q1_2, lambda_k1_2, lambda_q2_2,
    lambda_k2_2, subln_2, attn_w_o_2, rel_bias_2, ffn_norm_2, ffn_w_up_2, ffn_conv_w_2,
    ffn_conv_b_2, ffn_w_down_2, ple_norm_2, ple_w_gate_2, ple_w_proj_2,
):
    x = first_block(
        x, meta_tokens, norm_mix_g, w_in, b_f, conv_w, out_norm_g, w_out, norm_mlp_g, w_ff1,
        w_ff2, final_norm_g,
    )
    return second_block(
        x, p_2, ssm_norm_2, ssm_w_in_2, ssm_log_dt_2, ssm_lambda_re_2, ssm_lambda_im_2,
        ssm_b_re_2, ssm_b_im_2, ssm_c_re_2, ssm_c_im_2, ssm_d_2, ssm_w_glu_2, kv_norm_2, kv_w_2,
        k_norm_2, attn_norm_2, attn_w_q_2, q_norm_2, lambda_q1_2, lambda_k1_2, lambda_q2_2,
        lambda_k2_2, subln_2, attn_w_o_2, rel_bias_2, ffn_norm_2, ffn_w_up_2, ffn_conv_w_2,
        ffn_conv_b_2, ffn_w_down_2, ple_norm_2, ple_w_gate_2, ple_w_proj_2,
    )


_drawn_inputs = setup_inputs


def setup_inputs(seed=0):
    import zlib

    import numpy as np

    out = dict(_drawn_inputs(seed))
    spreads = {}
    factors = {'out_norm_g': 3.296,
     'norm_mlp_g': 3.592,
     'ssm_norm_2': 5.74,
     'ssm_lambda_re_2': 64.0,
     'k_norm_2': 5.32,
     'attn_norm_2': 4.479,
     'q_norm_2': 3.967,
     'lambda_q1_2': 3.354,
     'lambda_k1_2': 6.48,
     'lambda_k2_2': 7.095,
     'ffn_conv_b_2': 2.773,
     'ple_norm_2': 5.587,
     'subln_2': 3.409}
    for name, (base, spread) in spreads.items():
        noise = np.random.default_rng([zlib.crc32(name.encode()), seed]).standard_normal(out[name].shape)
        drawn = base * np.exp(spread * noise) if base else spread * noise
        out[name] = __import__('jax').numpy.asarray(drawn.astype(out[name].dtype))
    for name, factor in factors.items():
        out[name] = (out[name] * factor).astype(out[name].dtype)
    return out
```

```python
from contextlib import ExitStack

import numpy as np

import concourse.bass as bass
from concourse import mybir

F32 = mybir.dt.float32
F32R = mybir.dt.float32r
BF16 = mybir.dt.bfloat16
ACT = mybir.ActivationFunctionType
ALU = mybir.AluOpType
AX_X = mybir.AxisListType.X

P = 128
D = 1024
KT = D // P
SEQ = 512
META = 16
TOK = META + SEQ
HALF = TOK // 2
HD = 64
FFT = 22
FFG = [8, 8, 6]
NEG = -1e30
LAM = 0.8 - 0.6 * float(np.exp(-0.3))
PI = float(np.pi)

U_QKVB = 0
U_CU = 16
U_OUT1 = 24
U_FF = 32
U_SSM = 96
U_GLU = 104
U_FFNA = 120
U_PPA = 188
U_GATEA = 190
U_Q = 198
U_KV = 206
U_WO = 222
U_FFNB = 230
U_PPB = 298
U_GATEB = 300
NU = 308


def column_map():
    at, cols = 0, {}
    for name, n in (
        ("norm_mix", 8), ("out_norm", 8), ("norm_mlp", 8), ("final_norm", 8), ("conv_w", 12), ("b_f", 1),
        ("ssm_norm", 8), ("kv_norm", 8), ("attn_norm", 8), ("k_norm", 1), ("q_norm", 1), ("subln", 1),
        ("ffn_norm0", 8), ("ffn_norm1", 8), ("ple_norm0", 8), ("ple_norm1", 8),
        ("ffn_w0", 132), ("ffn_w1", 132), ("ffn_b0", 44), ("ffn_b1", 44),
        ("lam_re", 32), ("lam_im", 32), ("log_dt", 32), ("ssm_d", 32), ("lambdas", 4),
    ):
        cols[name] = at
        at += n
    return cols, at


COL, NCOL = column_map()


class Unit:

    def __init__(self, c, i=0, step=4):
        self.c, self.i, self.step = c, i, step

    def n(self, k=0):
        return self.c + k + self.step * self.i

    def ahead(self, k):
        return Unit(self.c + k, self.i, self.step)

    @property
    def slot(self):
        return self.c % 4

    @property
    def round(self):
        return self.c // 2 + self.step // 2 * self.i


class Count:

    def __init__(self, sem):
        self.sem, self.base, self.i, self.rate = sem, 0, 0, 0

    def did(self, ins):
        ins.then_inc(self.sem, 1)
        self.base += 1
        return self.base + self.rate * self.i

    def loop(self, i, rate, first=0):
        self.i, self.rate, self.entered = i, rate, self.base
        self.base -= rate * first

    def leave(self, trips, first=0):
        got = self.base - self.entered + self.rate * first
        assert got == self.rate, ("rate", got, self.rate)
        self.base = self.entered + self.rate * (trips - first)
        self.i, self.rate = 0, 0


def ge(eng, sem, value):
    if not (isinstance(value, int) and value <= 0):
        eng.wait_ge(sem, value)


def one(t, k):
    return t[:, bass.ds(k, 1), :] if not isinstance(k, int) else t[:, k:k + 1, :]


def program(nc, A, out, stop=99):
    with ExitStack() as ctx:
        build(nc, A, out, ctx, stop)


def build(nc, A, out, ctx, stop):
    def sb(name, shape, dt=F32, c=ctx):
        return c.enter_context(nc.sbuf_tensor(name, shape, dt))

    def sem(name):
        return ctx.enter_context(nc.semaphore(name))

    h = sb("h", [P, KT, TOK])
    a_hi = sb("a_hi", [P, KT, SEQ], F32R)
    a_lo = sb("a_lo", [P, KT, SEQ], F32R)
    raw = sb("raw", [P, 2, KT * P])
    w_hi = sb("w_hi", [P, 4, KT * P], F32R)
    w_lo = sb("w_lo", [P, 4, KT * P], F32R)
    vecs = sb("vecs", [P, NCOL])
    ones = sb("ones", [P, P])
    blk = sb("blk", [P, P])
    ident = sb("ident", [P, P])
    flip_r = sb("flip_r", [P, P], F32R)
    ident_b = sb("ident_b", [P, P], BF16)
    mask_b = sb("mask_b", [P, P], BF16)
    zero = sb("zero", [P, P])
    eps5 = sb("eps5", [P, 1])
    eps6 = sb("eps6", [P, 1])
    eps_o = sb("eps_o", [P, 1])
    neg_lam = sb("neg_lam", [P, 1])
    rel = sb("rel", [32, 8])
    rt = sb("rt", [P, TOK])
    rstd = sb("rstd", [P, TOK])
    sq = sb("sq", [P, 2, TOK])
    t0 = sb("t0", [P, 2, TOK])
    t1 = sb("t1", [P, 2, TOK])
    t2 = sb("t2", [P, 2, TOK])
    small = sb("small", [P, 4, 8])

    with ExitStack() as c:
        x_hi = sb("x_hi", [P, KT, TOK], F32R, c)
        x_lo = sb("x_lo", [P, KT, TOK], F32R, c)
    with ExitStack() as c:
        qs = sb("qs", [P, 2, 2, SEQ], F32, c)
        ks = sb("ks", [P, 2, TOK], F32, c)
        vs = sb("vs", [P, 2, TOK], F32, c)
        vp = sb("vp", [P, 2, 4, 2, P], F32, c)
        vm = sb("vm", [META, 2, 2, P], F32, c)
        pt = sb("pt", [P, 2, 4, P], F32, c)
        ptm = sb("ptm", [META, 2, P], F32, c)
    with ExitStack() as c:
        e_r = sb("e_r", [P, 32, P], F32, c)
        e_i = sb("e_i", [P, 32, P], F32, c)
    with ExitStack() as c:
        qs2 = sb("qs2", [P, 2, 2, SEQ], F32, c)
        ks2 = sb("ks2", [P, 2, SEQ], F32, c)
        vs2 = sb("vs2", [P, 2, SEQ], F32, c)
        vtok = sb("vtok", [P, 2, 4, P], F32, c)
        pt2 = sb("pt2", [P, 2, 4, P], F32, c)
        b_hi = sb("b_hi", [P, 2, SEQ], F32R, c)
        b_lo = sb("b_lo", [P, 2, SEQ], F32R, c)
    sb("region_x", [P, 2 * KT * TOK])
    with ExitStack() as c:
        qkvb = sb("qkvb", [P, 16, TOK], F32, c)
        aug_q = sb("aug_q", [P, 2, 2, SEQ], F32, c)
        aug_k = sb("aug_k", [P, TOK], F32, c)
        cum8 = sb("cum8", [40, TOK], F32, c)
        wf = sb("wf", [P, KT, 8], F32, c)
        mask = sb("mask", [P, P], F32, c)
        flip = sb("flip", [P, P], F32, c)
        wf_hi = sb("wf_hi", [P, KT, 8], F32R, c)
        wf_lo = sb("wf_lo", [P, KT, 8], F32R, c)

    with ExitStack() as c:
        u_t = sb("u_t", [P, 32, P], F32, c)
        c_raw = sb("c_raw", [P, 2, 32, 16], F32, c)
        bb = sb("bb", [P, 2, 32, 16], F32, c)
        pw_up = sb("pw_up", [P, 3, 32, 5], F32, c)
        pw_dn = sb("pw_dn", [P, 2, 32, 4], F32, c)
        sp_ = sb("sp_", [P, 16, 32], F32, c)
        v_b = sb("v_b", [P, 2, 2, 4, 4, 2, 16], F32, c)
        v_l = sb("v_l", [P, 2, 4, P], F32, c)
        c_p = sb("c_p", [P, 2, 2, 4, 5, 2, 16], F32, c)
        t_l = sb("t_l", [P, 4, P], F32, c)
        x_s = sb("x_s", [P, 2, 4, P + 1], F32, c)
        cmp_ = sb("cmp_", [P, 2, 320], F32, c)
    with ExitStack() as c:
        q2 = sb("q2", [P, 8, SEQ], F32, c)
        k2 = sb("k2", [P, 8, SEQ], F32, c)
        v2 = sb("v2", [P, 8, SEQ], F32, c)
        b_raw = sb("b_raw", [P, 1, SEQ], F32, c)
        tab = sb("tab", [8, 640], F32, c)
        onehot = sb("onehot", [32, 640], F32, c)
        neg_row = sb("neg_row", [8, 640], F32, c)
    with ExitStack() as c:
        pp = sb("pp", [P, 8, SEQ], F32, c)
        p_raw = sb("p_raw", [P, 2, SEQ], F32, c)
        p_hi = sb("p_hi", [P, 2, SEQ], F32R, c)
        p_lo = sb("p_lo", [P, 2, SEQ], F32R, c)
    scratch = nc.dram_tensor("scratch", (8, 640), F32, kind="Internal").ap()

    ps = ctx.enter_context(nc.psum_tensor("ps", [P, 8, SEQ], F32))

    consts_in = sem("consts_in")
    h_in = [sem(f"h_in{k}") for k in range(2)]
    raw_in = [sem(f"raw_in{k}") for k in range(2)]
    hi_ok = sem("hi_ok")
    lo_ok = sem("lo_ok")
    unit_mm = sem("unit_mm")
    unit_ev = sem("unit_ev")
    h_fin = sem("h_fin")
    sq_ok = sem("sq_ok")
    stat_mm = sem("stat_mm")
    xhi_ok = sem("xhi_ok")
    xlo_ok = sem("xlo_ok")
    rt_ok = sem("rt_ok")
    rstd_ok = sem("rstd_ok")
    consts_ok = sem("consts_ok")
    wf_ok = sem("wf_ok")
    wflo_ok = sem("wflo_ok")
    f_mm = sem("f_mm")
    f_act = sem("f_act")
    f_ok = sem("f_ok")
    staged = sem("staged")
    vt_mm = sem("vt_mm")
    vt_ok = sem("vt_ok")
    s_mm = sem("s_mm")
    nb_ok = sem("nb_ok")
    exp_ok = sem("exp_ok")
    nrm_ok = sem("nrm_ok")
    vz_ok = sem("vz_ok")
    qz_ok = sem("qz_ok")
    pt_mm = sem("pt_mm")
    pt_ok = sem("pt_ok")
    pv_mm = sem("pv_mm")
    y_ok = sem("y_ok")
    hn_sq = sem("hn_sq")
    hn_mm = sem("hn_mm")
    hn_rt = sem("hn_rt")
    hn_y = sem("hn_y")
    hn_hi = sem("hn_hi")
    hn_lo = sem("hn_lo")
    ay_ok = sem("ay_ok")
    ahi_ok = sem("ahi_ok")
    alo_ok = sem("alo_ok")
    dve_did = sem("dve_did")
    act_did = sem("act_did")
    pool_did = sem("pool_did")
    pool = Count(pool_did)
    dve = Count(dve_did)
    act = Count(act_did)
    ut_a = sem("ut_a")
    ut_p = sem("ut_p")
    par_v = sem("par_v")
    par_a = sem("par_a")
    bc_in = sem("bc_in")
    vb_ok = sem("vb_ok")
    cp_ok = sem("cp_ok")
    vb_mm = sem("vb_mm")
    g_mm = sem("g_mm")
    vl_ok = sem("vl_ok")
    tl_ok = sem("tl_ok")
    v_mm = sem("v_mm")
    v_ev = sem("v_ev")
    xs_ok = sem("xs_ok")
    y_mm = sem("y_mm")
    ys_ok = sem("ys_ok")
    ge_ok = sem("ge_ok")
    g_hi = sem("g_hi")
    g_lo = sem("g_lo")
    sig_ok = sem("sig_ok")
    c0_ok = sem("c0_ok")
    cg_ok = sem("cg_ok")
    gel_ok = sem("gel_ok")
    p_in = sem("p_in")
    phi_ok = sem("phi_ok")
    plo_ok = sem("plo_ok")
    tab_in = sem("tab_in")
    tab_mm = sem("tab_mm")
    tab_ok = sem("tab_ok")
    tab_out = sem("tab_out")
    b_in = sem("b_in")
    bhi_ok = sem("bhi_ok")
    blo_ok = sem("blo_ok")
    lam_v = sem("lam_v")
    lam_mm = sem("lam_mm")
    lam_a = sem("lam_a")
    v2_ok = sem("v2_ok")
    zz_ok = sem("zz_ok")
    cv_ok = sem("cv_ok")
    sg_ok = sem("sg_ok")
    sgu_ok = sem("sgu_ok")
    o_ok = sem("o_ok")
    fence_at = sem("fence_at")
    stored = sem("stored")

    REAL = slice(META, TOK)
    NLOAD = {1: U_SSM, 2: U_FFNA, 4: U_Q + 2, 5: U_FFNB + 2}.get(stop, NU)

    def vec(name, k=0, lo=0, n=P):
        k = COL[name] + k
        return vecs[lo:lo + n, k:k + 1] if isinstance(k, int) else vecs[lo:lo + n, bass.ds(k, 1)]

    def halves(t):
        return t.rearrange("p (a b) -> p a b", a=2)

    def fence(e, k):
        e.drain().then_inc(fence_at, 1)
        e.wait_ge(fence_at, 4 * k)

    def load_unit(e, u):
        if not (isinstance(u.i, int) and u.n() < 2):
            e.wait_ge(lo_ok, u.n(-1))
        n = u.n()
        src = A["wstream"][bass.ds(n * P, P), :] if not isinstance(n, int) else A["wstream"][n * P:n * P + P, :]
        e.dma_start(raw[:, u.c % 2, :], src).then_inc(raw_in[u.c % 2], 16)

    def split_hi(e, u):
        e.wait_ge(raw_in[u.c % 2], 16 * (u.round + 1))
        if not (isinstance(u.i, int) and u.n() < 4):
            e.wait_ge(unit_mm, u.n(-3))
        e.activation(w_hi[:, u.slot, :], raw[:, u.c % 2, :], ACT.Copy).then_inc(hi_ok, 1)

    def split_lo(e, u):
        e.wait_ge(hi_ok, u.n(1))
        e.tensor_tensor(w_lo[:, u.slot, :], raw[:, u.c % 2, :], w_hi[:, u.slot, :], ALU.subtract)\
            .then_inc(lo_ok, 1)

    def split_ahead(e, u, split):
        if not (isinstance(u.i, int) and u.n() + 2 >= NLOAD):
            split(e, u.ahead(2))

    def products(e, u, bank, hi, lo, k0=0, kt=KT, w0=0, ready=None):
        for k in range(kt):
            w = slice((w0 + k) * P, (w0 + k + 1) * P)
            if ready:
                ready(e, k)
            for n, (wt, x) in enumerate(((w_hi, hi), (w_hi, lo), (w_lo, hi))):
                last = e.matmul(ps[:, bank, :], wt[:, u.slot, w], x[:, k0 + k, 0:SEQ],
                                start=(k == 0 and n == 0), stop=(k == kt - 1 and n == 2))
        return last

    def unit_pe(e, u, hi, lo, ready=None, kt=KT):
        e.wait_ge(lo_ok, u.n(1))
        e.wait_ge(unit_ev, u.n(-3))
        products(e, u, u.slot, hi, lo, kt=kt, ready=ready).then_inc(unit_mm, 1)

    XN = {0: 0, 1: 1, 3: 2, 4: 3, 5: 4, 6: 5, 7: 7, 8: 8}

    def stat_pe(e, n, m, cols=SEQ):
        e.wait_ge(sq_ok, 8 * n + m + 1)
        if n and m == 0:
            e.wait_ge(rt_ok, n)
        for half in range(2 if cols > SEQ else 1):
            w = HALF if cols > SEQ else SEQ
            last = e.matmul(ps[:, 4 + half, 0:w], ones[:, :], sq[:, m % 2, half * HALF:half * HALF + w],
                            start=(m == 0), stop=(m == KT - 1))
        last.then_inc(stat_mm, 1)

    def norm_act(e, n, m, gain, cols=SEQ, x_hi=x_hi):
        src = h[:, m, TOK - cols:TOK]
        if 8 * n + m >= 2:
            e.wait_ge(stat_mm, 8 * n + m - 1)
        e.activation(sq[:, m % 2, 0:cols], src, ACT.Square).then_inc(sq_ok, 1)
        if gain:
            x_act(e, n, m, gain, cols)

    def x_act(e, n, m, gain, cols=SEQ, hi=x_hi):
        src = h[:, m, TOK - cols:TOK]
        e.activation(hi[:, m, 0:cols], src, ACT.Copy, scale=vec(gain, m)).then_inc(xhi_ok, 1)

    def x_dve(e, xn, m, gain, cols=SEQ, hi=x_hi, lo=x_lo):
        src = h[:, m, TOK - cols:TOK]
        e.wait_ge(xhi_ok, 8 * xn + m + 1)
        e.scalar_tensor_tensor(lo[:, m, 0:cols], src, vec(gain, m), hi[:, m, 0:cols], ALU.mult,
                               ALU.subtract).then_inc(xlo_ok, 1)

    def root_act(e, n, eps, cols=SEQ):
        e.wait_ge(stat_mm, 8 * (n + 1))
        if n:
            e.wait_ge(rstd_ok, n)
        if cols > SEQ:
            o, i = halves(rt[:, :]), ps[:, 4:6, 0:HALF]
        else:
            o, i = rt[:, 0:cols], ps[:, 4, 0:cols]
        e.activation(o, i, ACT.Sqrt, bias=eps[:, 0:1], scale=1.0 / D).then_inc(rt_ok, 1)

    def root_dve(e, n, cols=SEQ):
        e.wait_ge(rt_ok, n + 1)
        e.reciprocal(rstd[:, 0:cols], rt[:, 0:cols]).then_inc(rstd_ok, 1)
        e.wait_ge(rstd_ok, n + 1)

    def head_sq(e, k, y):
        if k >= 2:
            e.wait_ge(hn_mm, k - 1)
        e.activation(sq[:, k % 2, 0:SEQ], y, ACT.Square).then_inc(hn_sq, 1)

    def head_pe(e, k, which):
        e.wait_ge(hn_sq, k + 1)
        if k >= 2:
            e.wait_ge(hn_rt, k - 1)
        e.matmul(ps[:, 6 + k % 2, :], which[:, :], sq[:, k % 2, 0:SEQ], start=True, stop=True).then_inc(hn_mm, 1)

    def head_root(e, k, n, eps):
        e.wait_ge(hn_mm, k + 1)
        if k >= 2:
            e.wait_ge(hn_y, k - 1)
        e.activation(t2[:, k % 2, 0:SEQ], ps[:, 6 + k % 2, :], ACT.Sqrt, bias=eps[:, 0:1], scale=1.0 / n)\
            .then_inc(hn_rt, 1)

    def head_scale(e, k, y, gain, to=None, extra=None):
        e.wait_ge(hn_rt, k + 1)
        r = t2[:, k % 2, 0:SEQ]
        n = dve.did(e.reciprocal(r, r))
        if to is None and k >= 2:
            e.wait_ge(hn_lo, HNX(k) - 1)
        e.wait_ge(dve_did, n)
        to = t0[:, k % 2, 0:SEQ] if to is None else to
        e.scalar_tensor_tensor(to, y, gain, r, ALU.mult, ALU.mult).then_inc(hn_y, 1)

    def HNX(k):
        return k if k < 8 else k - 16

    def head_hi(e, k, m):
        e.wait_ge(hn_y, k + 1)
        e.activation(a_hi[:, m, :], t0[:, k % 2, 0:SEQ], ACT.Copy).then_inc(hn_hi, 1)

    def head_lo(e, k, m):
        e.wait_ge(hn_hi, HNX(k) + 1)
        e.wait_ge(hn_y, k + 1)
        e.tensor_tensor(a_lo[:, m, :], t0[:, k % 2, 0:SEQ], a_hi[:, m, :], ALU.subtract).then_inc(hn_lo, 1)

    def wide_pe(e, u):
        e.wait_ge(lo_ok, u.n(1))
        if not (isinstance(u.i, int) and u.n() < 2):
            e.wait_ge(unit_ev, u.n(-1))
        b = 2 * (u.slot % 2)
        for k in range(KT):
            w = slice(k * P, (k + 1) * P)
            if isinstance(u.i, int) and u.n() == 0:
                e.wait_ge(xlo_ok, k + 1)
            for n, (wt, x) in enumerate(((w_hi, x_hi), (w_hi, x_lo), (w_lo, x_hi))):
                for half in range(2):
                    last = e.matmul(ps[:, b + half, 0:HALF], wt[:, u.slot, w],
                                    x[:, k, half * HALF:(half + 1) * HALF],
                                    start=(k == 0 and n == 0), stop=(k == KT - 1 and n == 2))
        last.then_inc(unit_mm, 1)

    def wide_dve(e, u, to):
        e.wait_ge(unit_mm, u.n(1))
        b = 2 * (u.slot % 2)
        e.tensor_tensor(halves(to), ps[:, b:b + 2, 0:HALF], halves(rstd[:, :]), ALU.mult).then_inc(unit_ev, 1)

    def f_pe(e):
        e.wait_ge(wflo_ok, 1)
        for k in range(KT):
            for n, (wt, x) in enumerate(((wf_hi, x_hi), (wf_hi, x_lo), (wf_lo, x_hi))):
                for half in range(2):
                    last = e.matmul(ps[0:8, 6 + half, 0:HALF], wt[:, k, :], x[:, k, half * HALF:(half + 1) * HALF],
                                    start=(k == 0 and n == 0), stop=(k == KT - 1 and n == 2))
        last.then_inc(f_mm, 1)

    def f_dve(e):
        z, az, ls = t0[0:8, 0, :], t0[0:8, 1, :], t1[0:8, 0, :]
        e.wait_ge(f_mm, 1)
        n = dve.did(e.tensor_tensor(halves(az), ps[0:8, 6:8, 0:HALF], halves(rstd[0:8, :]), ALU.mult))
        e.wait_ge(dve_did, n)
        e.tensor_scalar(z, az, vec("b_f", 0, 0, 8), None, ALU.add).then_inc(f_ok, 1)
        e.wait_ge(f_act, 1)
        n = dve.did(e.scalar_tensor_tensor(ls, z, 0.0, t1[0:8, 1, :], ALU.min, ALU.subtract))
        e.wait_ge(dve_did, n)
        e.wait_ge(consts_ok, 1)
        n = dve.did(e.tensor_tensor_scan(cum8[0:8, :], t2[0:8, 0, :], ls, 0.0, ALU.mult, ALU.add))
        e.wait_ge(dve_did, n)
        e.tensor_scalar(aug_k[0:8, :], cum8[0:8, :], -8.0, None, ALU.mult).then_inc(f_ok, 1)
        e.tensor_scalar(cum8[32:40, :], cum8[0:8, :], 8.0, None, ALU.mult).then_inc(f_ok, 1)

    def f_scalar(e):
        e.wait_ge(f_ok, 1)
        n = act.did(e.activation(t0[0:8, 1, :], t0[0:8, 0, :], ACT.Abs))
        e.wait_ge(act_did, n)
        n = act.did(e.activation(t1[0:8, 0, :], t0[0:8, 1, :], ACT.Exp, scale=-1.0))
        e.wait_ge(act_did, n)
        e.activation(t1[0:8, 1, :], t1[0:8, 0, :], ACT.Ln, bias=1.0).then_inc(f_act, 1)

    def conv_dve(e, u, s):
        k = s // 2
        if s % 2 == 0:
            wide_dve(e, u, t0[:, k, :])
            return
        wide_dve(e, u, t1[:, k, :])
        j = 2 * u.i + k
        e.wait_ge(unit_ev, u.n(1))
        n = dve.did(e.tensor_tensor(t2[:, k, :], t0[:, k, :], t1[:, k, :], ALU.mult))
        e.wait_ge(dve_did, n)
        n = dve.did(e.tensor_scalar(t0[:, k, 0:SEQ], t2[:, k, 16:528], vec("conv_w", 8 + j), None, ALU.mult))
        e.wait_ge(dve_did, n)
        n = dve.did(e.scalar_tensor_tensor(t1[:, k, 0:SEQ], t2[:, k, 15:527], vec("conv_w", 4 + j),
                                           t0[:, k, 0:SEQ], ALU.mult, ALU.add))
        e.wait_ge(dve_did, n)
        n = dve.did(e.scalar_tensor_tensor(t0[:, k, 0:SEQ], t2[:, k, 14:526], vec("conv_w", j),
                                           t1[:, k, 0:SEQ], ALU.mult, ALU.add))
        e.wait_ge(dve_did, n)
        b = qkvb[:, bass.ds(12 + j, 1), REAL] if not isinstance(j, int) else qkvb[:, 12 + j:13 + j, REAL]
        n = dve.did(e.tensor_tensor(b, b, t0[:, k:k + 1, 0:SEQ], ALU.mult))

    def tile_of(t, k, cols=slice(None), rows=slice(None)):
        return t[rows, k:k + 1, cols] if isinstance(k, int) else t[rows, bass.ds(k, 1), cols]

    def stage1_pool(e, i):
        for par in range(2):
            p = 2 * i + par
            if not (isinstance(i, int) and i == 0):
                e.wait_ge(y_ok, 2 * i + par - 1)
            k = 8 * p
            for hh in range(2):
                r = slice(HD * hh, HD * hh + HD)
                ge(e, staged, k + hh)
                e.tensor_copy(qs[r, par, hh:hh + 1, :], tile_of(qkvb, p, REAL, r)).then_inc(staged, 1)
            e.wait_ge(staged, k + 2)
            e.tensor_copy(ks[:, par:par + 1, :], tile_of(qkvb, 4 + p)).then_inc(staged, 1)
            e.wait_ge(staged, k + 3)
            e.tensor_copy(vs[:, par:par + 1, :], tile_of(qkvb, 8 + p)).then_inc(staged, 1)
            for hh in range(2):
                hd = 2 * p + hh
                pick = lambda lo, c: (ident[lo:lo + 8, c:c + 1] if isinstance(c, int)
                                      else ident[lo:lo + 8, bass.ds(c, 1)]).to_broadcast([8, SEQ])
                e.wait_ge(staged, k + 4 + 2 * hh)
                e.tensor_copy(aug_q[0:8, par, hh, :], pick(0, hd)).then_inc(staged, 1)
                e.wait_ge(staged, k + 5 + 2 * hh)
                e.tensor_tensor(aug_q[32:40, par, hh, :], cum8[32:40, REAL], pick(32, 32 + hd), ALU.mult)\
                    .then_inc(staged, 1)

    def values_pe(e, i, par):
        p = 2 * i + par
        e.wait_ge(staged, 8 * p + 8)
        for j in range(4):
            e.transpose(ps[:, 4 + par, j * P:(j + 1) * P], vs[:, par, META + j * P:META + (j + 1) * P], ident[:, :])
        e.transpose(ps[0:META, 6 + par, 0:P], vs[:, par, 0:META], ident[:, :]).then_inc(vt_mm, 1)

    def values_act(e, i, par):
        p = 2 * i + par
        e.wait_ge(vt_mm, p + 1)
        e.wait_ge(vz_ok, 1)
        t = ps[:, 4 + par, :].rearrange("p (j c) -> p j c", j=4)
        for hh in range(2):
            c = slice(HD * hh, HD * hh + HD)
            e.activation(vp[:, par, :, hh, c], t[:, :, c], ACT.Copy).then_inc(vt_ok, 1)
            e.activation(vm[:, par, hh, c], ps[0:META, 6 + par, c], ACT.Copy).then_inc(vt_ok, 1)

    def scores1_pe(e, i, par, w):
        qt, hh, sl = w // 2, w % 2, w % 2
        g = 8 * (2 * i + par) + w
        ge(e, exp_ok, g - 1)
        ge(e, pt_ok, 2 * (g - 1))
        A_, B = 2 * sl, 2 * sl + 1
        q = qs[:, par, hh, qt * P:(qt + 1) * P]
        aq = aug_q[:, par, hh, qt * P:(qt + 1) * P]
        N = (qt + 1) * P
        e.matmul(ps[:, A_, SEQ - META:SEQ], q, ks[:, par, 0:META], start=True, stop=False)
        e.matmul(ps[:, A_, SEQ - META:SEQ], aq, aug_k[:, 0:META], start=False, stop=True)
        e.matmul(ps[:, B, 0:N], q, ks[:, par, META:META + N], start=True, stop=False)
        e.matmul(ps[:, B, 0:N], aq, aug_k[:, META:META + N], start=False, stop=False)
        e.matmul(ps[:, B, N - P:N], ident_b[:, :], mask_b[:, :], start=False, stop=True).then_inc(s_mm, 1)

    def turn1_pe(e, i, par, w):
        qt, sl = w // 2, w % 2
        g = 8 * (2 * i + par) + w
        e.wait_ge(nrm_ok, g + 1)
        for j in range(qt + 1):
            e.transpose(ps[:, 4 + sl, j * P:(j + 1) * P], t0[:, sl, META + j * P:META + (j + 1) * P], ident[:, :])
        e.transpose(ps[0:META, 2 * sl, 0:P], t0[:, sl, 0:META], ident[:, :]).then_inc(pt_mm, 1)

    def pv1_pe(e, i, par, w):
        qt, hh, sl = w // 2, w % 2, w % 2
        g = 8 * (2 * i + par) + w
        e.wait_ge(pt_ok, 2 * (g + 1))
        if w == 0:
            e.wait_ge(vt_ok, 4 * (2 * i + par) + 4)
        o = ps[:, 6 + par, qt * P:(qt + 1) * P]
        for j in range(qt + 1):
            e.matmul(o, vp[:, par, j, hh, :], pt[:, sl, j, :], start=(hh == 0 and j == 0), stop=False)
        e.matmul(o, vm[:, par, hh, :], ptm[:, sl, :], start=False, stop=(hh == 1)).then_inc(pv_mm, 1)

    def attention1_pe(e, i):
        for par in range(2):
            values_pe(e, i, par)
            for w in range(8 + 2):
                if w < 8:
                    scores1_pe(e, i, par, w)
                if 1 <= w < 9:
                    turn1_pe(e, i, par, w - 1)
                if w >= 2:
                    pv1_pe(e, i, par, w - 2)

    def scores_flat(sl):
        return ps[:, 2 * sl:2 * sl + 2, :].rearrange("p a b -> p (a b)")

    def attention1_dve(e, i):
        def top(par, w):
            qt, sl = w // 2, w % 2
            g = 8 * (2 * i + par) + w
            e.wait_ge(s_mm, g + 1)
            s = scores_flat(sl)[:, SEQ - META:SEQ + (qt + 1) * P]
            n = dve.did(e.reduce_max(small[:, 0, sl:sl + 1], s, AX_X))
            e.wait_ge(dve_did, n)
            e.tensor_scalar(small[:, 1, sl:sl + 1], small[:, 0, sl:sl + 1], -0.125, None, ALU.mult)\
                .then_inc(nb_ok, 1)

        def normalise(par, w):
            qt, sl = w // 2, w % 2
            g = 8 * (2 * i + par) + w
            N = META + (qt + 1) * P
            e.wait_ge(exp_ok, g + 1)
            n = dve.did(e.reciprocal(small[:, 3, sl:sl + 1], small[:, 2, sl:sl + 1]))
            e.wait_ge(dve_did, n)
            e.tensor_scalar(t0[:, sl, 0:N], t0[:, sl, 0:N], small[:, 3, sl:sl + 1], None, ALU.mult)\
                .then_inc(nrm_ok, 1)

        for par in range(2):
            for w in range(8 + 1):
                if w < 8:
                    top(par, w)
                if w >= 1:
                    normalise(par, w - 1)
            p = 2 * i + par
            e.wait_ge(pv_mm, 8 * p + 8)
            e.tensor_copy(tile_of(qkvb, p, REAL), ps[:, 6 + par:7 + par, :]).then_inc(y_ok, 1)

    def attention1_act(e, i):
        def exps(par, w):
            qt, sl = w // 2, w % 2
            g = 8 * (2 * i + par) + w
            e.wait_ge(nb_ok, g + 1)
            ge(e, pt_mm, g - 1)
            ge(e, nrm_ok, g - 1)
            N = META + (qt + 1) * P
            e.activation(t0[:, sl, 0:N], scores_flat(sl)[:, SEQ - META:SEQ + (qt + 1) * P], ACT.Exp,
                         bias=small[:, 1, sl:sl + 1], scale=0.125,
                         accum_out=small[:, 2, sl:sl + 1]).then_inc(exp_ok, 1)

        def turned(par, w):
            qt, sl = w // 2, w % 2
            g = 8 * (2 * i + par) + w
            N = (qt + 1) * P
            e.wait_ge(pt_mm, g + 1)
            ge(e, pv_mm, g - 1)
            e.activation(pt[:, sl, 0:qt + 1, :].rearrange("p j c -> p (j c)"), ps[:, 4 + sl, 0:N], ACT.Copy)\
                .then_inc(pt_ok, 1)
            e.activation(ptm[:, sl, :], ps[0:META, 2 * sl, 0:P], ACT.Copy).then_inc(pt_ok, 1)

        for par in range(2):
            values_act(e, i, par)
            for w in range(8 + 1):
                if w < 8:
                    exps(par, w)
                if w >= 1:
                    turned(par, w - 1)

    def y_tile(m):
        return qkvb[:, m if m < 4 else m + 8, REAL]

    def relu2_dve(e, u, s):
        e.wait_ge(unit_mm, u.n(1))
        k = s % 2
        e.tensor_tensor(t0[:, k, 0:SEQ], ps[:, u.slot, :], rstd[:, 0:SEQ], ALU.mult).then_inc(unit_ev, 1)
        ge(e, alo_ok, 8 * u.i + s - 1)
        e.wait_ge(unit_ev, u.n(1))
        e.scalar_tensor_tensor(t1[:, k, 0:SEQ], t0[:, k, 0:SEQ], 0.0, t0[:, k, 0:SEQ], ALU.max, ALU.mult)\
            .then_inc(ay_ok, 1)

    def hidden_hi(e, n, m):
        e.wait_ge(ay_ok, n + 1)
        e.activation(a_hi[:, m, :], t1[:, m % 2, 0:SEQ], ACT.Copy).then_inc(ahi_ok, 1)

    def hidden_lo(e, n, m):
        e.wait_ge(ahi_ok, n + 1)
        e.tensor_tensor(a_lo[:, m, :], t1[:, m % 2, 0:SEQ], a_hi[:, m, :], ALU.subtract).then_inc(alo_ok, 1)

    def add_dve(e, u, m, final=False):
        e.wait_ge(unit_mm, u.n(1))
        e.wait_ge(unit_ev, u.n())
        i = e.tensor_tensor(h[:, m, REAL], h[:, m, REAL], ps[:, u.slot, :], ALU.add)
        i.then_inc(unit_ev, 1)


    def units(e, u0, trips, body, first=0, cycle=4, counts=None, rate=0):
        for i in range(first):
            for s in range(cycle):
                body(Unit(u0 + s, i, cycle), s)
        if trips > first:
            with e.Fori(first, trips) as i:
                if counts:
                    counts.loop(i, rate, first)
                for s in range(cycle):
                    body(Unit(u0 + s, i, cycle), s)
            if counts:
                counts.leave(trips, first)

    def spread_u(e, u, m, q, j, who):
        src = t0[32 * q:32 * q + 32, m % 2 if isinstance(m, int) else u.slot % 2, 0:SEQ]
        src = src.rearrange("p (c j) -> p j c", j=4)[:, j:j + 1, :]
        k = 4 * m + q
        dst = u_t[32 * j:32 * j + 32, bass.ds(k, 1), :] if not isinstance(k, int) else u_t[32 * j:32 * j + 32, k:k + 1, :]
        return (e.activation(dst, src, ACT.Copy) if who == "a" else e.tensor_copy(dst, src))

    def cmul(e, n, out_r, out_i, a, b, tmp, sign=1):
        ar, ai = a
        br, bi = b
        ta, tb, tc, td = tmp
        n.did(e.tensor_tensor(ta, ar, br, ALU.mult))
        n.did(e.tensor_tensor(tb, ai, bi, ALU.mult))
        n.did(e.tensor_tensor(tc, ar, bi, ALU.mult))
        k = n.did(e.tensor_tensor(td, ai, br, ALU.mult))
        e.wait_ge(n.sem, k)
        n.did(e.tensor_tensor(out_r, ta, tb, ALU.subtract if sign > 0 else ALU.add))
        k = n.did(e.tensor_tensor(out_i, tc, td, ALU.add if sign > 0 else ALU.subtract))
        e.wait_ge(n.sem, k)

    S = lambda k: sp_[:, k, :]
    T4 = lambda w: [t[:, s, 0:w] for t in (t0, t1) for s in range(2)]
    V_DT, V_MAG, V_TH, V_K, V_R, V_SH, V_SIN, V_COS, V_AR, V_AI, V_FR, V_FI, V_M4, V_T, V_W, V_Z = range(16)

    def system_act(e):
        e.activation(S(V_DT), vecs[:, COL["log_dt"]:COL["log_dt"] + 32], ACT.Exp).then_inc(par_a, 1)
        e.wait_ge(par_v, 1)
        e.activation(S(V_MAG), S(V_T), ACT.Exp).then_inc(par_a, 1)
        e.wait_ge(par_v, 2)
        e.activation(S(V_SH), S(V_R), ACT.Sin, scale=0.5).then_inc(par_a, 1)
        e.activation(S(V_SIN), S(V_R), ACT.Sin).then_inc(par_a, 1)

    def system_dve(e):
        lr = vecs[:, COL["lam_re"]:COL["lam_re"] + 32]
        li = vecs[:, COL["lam_im"]:COL["lam_im"] + 32]

        def do(ins):
            k = dve.did(ins)
            e.wait_ge(dve_did, k)

        tt = lambda o, a, b, op: do(e.tensor_tensor(o, a, b, op))
        ts = lambda o, a, x, y, op0, op1: do(e.tensor_scalar(o, a, x, y, op0, op1))
        e.wait_ge(par_a, 1)
        e.tensor_tensor(S(V_T), lr, S(V_DT), ALU.mult).then_inc(par_v, 1)
        tt(S(V_TH), li, S(V_DT), ALU.mult)
        magic = 1.5 * 2.0 ** 23
        ts(S(V_K), S(V_TH), 1.0 / (2 * PI), magic, ALU.mult, ALU.add)
        ts(S(V_K), S(V_K), magic, None, ALU.subtract, ALU.bypass)
        c1 = 6.28125
        c2 = float(np.float32(2 * np.pi - c1).view(np.uint32) & np.uint32(0xFFFFF000)) and \
            float((np.float32(2 * np.pi - c1).view(np.uint32) & np.uint32(0xFFFFF000)).view(np.float32))
        c3 = float(np.float32(2 * np.pi - c1 - c2))
        src = S(V_TH)
        for c in (c1, c2, c3):
            do(e.scalar_tensor_tensor(S(V_R), S(V_K), -c, src, ALU.mult, ALU.add))
            src = S(V_R)
        lim = float(np.nextafter(np.float32(np.pi), np.float32(0)))
        e.tensor_scalar(S(V_R), S(V_R), lim, -lim, ALU.min, ALU.max).then_inc(par_v, 1)
        e.wait_ge(par_a, 4)
        tt(S(V_COS), S(V_SH), S(V_SH), ALU.mult)
        ts(S(V_COS), S(V_COS), -2.0, 1.0, ALU.mult, ALU.add)
        tt(S(V_AR), S(V_MAG), S(V_COS), ALU.mult)
        tt(S(V_AI), S(V_MAG), S(V_SIN), ALU.mult)
        tt(S(V_T), lr, lr, ALU.mult)
        tt(S(V_W), li, li, ALU.mult)
        tt(S(V_T), S(V_T), S(V_W), ALU.add)
        do(e.reciprocal(S(V_Z), S(V_T)))
        ts(S(V_W), S(V_AR), -1.0, None, ALU.add, ALU.bypass)
        tt(S(V_FR), S(V_W), lr, ALU.mult)
        tt(S(V_T), S(V_AI), li, ALU.mult)
        tt(S(V_FR), S(V_FR), S(V_T), ALU.add)
        tt(S(V_FR), S(V_FR), S(V_Z), ALU.mult)
        tt(S(V_FI), S(V_AI), lr, ALU.mult)
        tt(S(V_T), S(V_W), li, ALU.mult)
        tt(S(V_FI), S(V_FI), S(V_T), ALU.subtract)
        tt(S(V_FI), S(V_FI), S(V_Z), ALU.mult)
        tt(S(V_T), S(V_MAG), S(V_MAG), ALU.mult)
        tt(S(V_M4), S(V_T), S(V_T), ALU.mult)
        small4 = [t[:, s, 0:32] for t in (t0, t1) for s in range(2)]
        up = lambda k, n: pw_up[:, k, :, n]
        do(e.memset(up(0, 0), 1.0))
        do(e.memset(up(1, 0), 0.0))
        do(e.tensor_copy(up(0, 1), S(V_AR)))
        do(e.tensor_copy(up(1, 1), S(V_AI)))
        for n, (a, b) in {2: (1, 1), 3: (2, 1), 4: (2, 2)}.items():
            cmul(e, dve, up(0, n), up(1, n), (up(0, a), up(1, a)), (up(0, b), up(1, b)), small4)
        ts(pw_up[:, 2, :, :], pw_up[:, 1, :, :], -1.0, None, ALU.mult, ALU.bypass)
        for j in range(4):
            do(e.tensor_copy(pw_dn[:, :, :, j], pw_up[:, 0:2, :, 3 - j]))
        e.wait_ge(bc_in, 32)
        br, bi = (t2[:, k, 0:SEQ].rearrange("p (q c) -> p q c", c=16) for k in range(2))
        bc = lambda k: S(k).unsqueeze(2).to_broadcast([P, 32, 16])
        cmul(e, dve, bb[:, 0, :, :], bb[:, 1, :, :], (bc(V_FR), bc(V_FI)), (br, bi),
             [t.rearrange("p (q c) -> p q c", c=16) for t in T4(SEQ)])
        cr, ci = S(V_COS), S(V_SIN)
        for _ in range(2):
            cmul(e, dve, S(V_T), S(V_W), (cr, ci), (cr, ci), small4)
            unit_length(e, S(V_T), S(V_W), S(V_Z), S(V_K))
            do(e.tensor_copy(S(V_COS), S(V_T)))
            do(e.tensor_copy(S(V_SIN), S(V_W)))
        do(e.memset(e_r[:, :, 0:1], 1.0))
        do(e.memset(e_i[:, :, 0:1], 0.0))
        n = 1
        while n < P:
            per = min(32, 512 // n)
            for q in range(0, 32, per):
                w = [t.rearrange("p (q c) -> p q c", c=n) for t in T4(per * n)]
                b = [S(k)[:, q:q + per].unsqueeze(2).to_broadcast([P, per, n]) for k in (V_COS, V_SIN)]
                cmul(e, dve, e_r[:, q:q + per, n:2 * n], e_i[:, q:q + per, n:2 * n],
                     (e_r[:, q:q + per, 0:n], e_i[:, q:q + per, 0:n]), b, w)
            n *= 2
            if n < P:
                cmul(e, dve, S(V_T), S(V_W), (cr, ci), (cr, ci), small4)
                unit_length(e, S(V_T), S(V_W), S(V_Z), S(V_K))
                do(e.tensor_copy(S(V_COS), S(V_T)))
                do(e.tensor_copy(S(V_SIN), S(V_W)))
        e.drain().then_inc(par_v, 1)

    def unit_length(e, r, i, s, w):
        def do(ins):
            e.wait_ge(dve_did, dve.did(ins))
        do(e.tensor_tensor(s, r, r, ALU.mult))
        do(e.tensor_tensor(w, i, i, ALU.mult))
        do(e.tensor_tensor(s, s, w, ALU.add))
        do(e.tensor_scalar(s, s, -0.5, 1.5, ALU.mult, ALU.add))
        do(e.tensor_tensor(r, r, s, ALU.mult))
        do(e.tensor_tensor(i, i, s, ALU.mult))

    def matrices_pool(e, m):
        b = m % 2
        pr_ = slice(4 * m, 4 * m + 4)
        ge(e, y_mm, m - 1)
        for dst, src, pw, n, done in ((v_b, bb, pw_dn, 4, vb_ok), (c_p, c_raw, pw_up, 5, cp_ok)):
            w = [t[:, 0:64 * n].rearrange("p (q j c) -> p q j c", q=4, j=n)
                 for t in (cmp_[:, 0, :], cmp_[:, 1, :], rt, rstd)]
            x = [src[:, k, pr_, :].unsqueeze(2).to_broadcast([P, 4, n, 16]) for k in range(2)]
            y = [pw[:, k, pr_, :].unsqueeze(3).to_broadcast([P, 4, n, 16]) for k in range(3 if n == 5 else 2)]
            im = 2 if n == 5 else 1

            def do(ins):
                e.wait_ge(pool_did, pool.did(ins))

            do(e.tensor_tensor(w[0], x[0], y[0], ALU.mult))
            do(e.tensor_tensor(w[1], x[1], y[1], ALU.mult))
            do(e.tensor_tensor(w[2], x[0], y[im], ALU.mult))
            do(e.tensor_tensor(w[3], x[1], y[0], ALU.mult))
            for g in range(2):
                r = slice(HD * g, HD * g + HD)
                do(e.tensor_tensor(dst[r, b, 0, :, :, g, :], w[0][r], w[1][r], ALU.subtract))
                do(e.tensor_tensor(dst[r, b, 1, :, :, g, :], w[2][r], w[3][r],
                                   ALU.subtract if n == 5 else ALU.add))
            e.drain().then_inc(done, 1)

    def mixer_front_pe(e, m):
        b = m % 2
        e.wait_ge(vb_ok, m + 1)
        ge(e, vl_ok, 2 * m)
        for k in range(2):
            for q in range(4):
                last = e.transpose(ps[:, 4 + k, q * P:(q + 1) * P],
                                   v_b[:, b, k, q, :, :, :].rearrange("p j g c -> p (j g c)"), ident[:, :])
        last.then_inc(vb_mm, 1)
        e.wait_ge(cp_ok, m + 1)
        ge(e, tl_ok, 4 * m)
        for q in range(4):
            for k in range(2):
                last = e.matmul(ps[0:32, 6, q * P:(q + 1) * P], v_b[:, b, k, q, 3, :, :].rearrange("p g c -> p (g c)"),
                                c_p[:, b, k, q, 0:4, :, :].rearrange("p j g c -> p (j g c)"),
                                start=(k == 0), stop=(k == 1))
        last.then_inc(g_mm, 1)
        e.wait_ge(vl_ok, 2 * m + 2)
        ge(e, v_ev, m)
        for k in range(2):
            for q in range(4):
                last = e.matmul(ps[:, k, q * P:(q + 1) * P], v_l[:, k, q, :], u_t[:, 4 * m + q, :],
                                start=True, stop=True)
        last.then_inc(v_mm, 1)

    def mixer_back_pe(e, m):
        b = m % 2
        e.wait_ge(tl_ok, 4 * m + 4)
        e.wait_ge(xs_ok, m + 1)
        ge(e, ys_ok, 4 * m)
        for q in range(4):
            o = ps[:, 2, q * P:(q + 1) * P]
            e.matmul(o, t_l[:, q, :], u_t[:, 4 * m + q, :], start=True, stop=False)
            for k in range(2):
                last = e.matmul(o, c_p[:, b, k, q, 1:5, :, :].rearrange("p j g c -> p (j g c)"),
                                x_s[:, k, q, 0:P], start=False, stop=(k == 1))
        last.then_inc(y_mm, 1)

    def mixer_front_act(e, m):
        e.wait_ge(vb_mm, m + 1)
        ge(e, v_mm, m)
        for k in range(2):
            e.activation(v_l[:, k, :, :].rearrange("p q c -> p (q c)"), ps[:, 4 + k, :], ACT.Copy).then_inc(vl_ok, 1)
        e.wait_ge(g_mm, m + 1)
        ge(e, y_mm, m)
        g = ps[0:32, 6, :].rearrange("p (q c) -> p q c", q=4)
        for j in range(4):
            e.activation(t_l[32 * j:32 * j + 32, :, 32 * j:P], g[:, :, 0:P - 32 * j], ACT.Copy).then_inc(tl_ok, 1)

    def mixer_back_act(e, m):
        e.wait_ge(ys_ok, 4 * m + 4)
        ge(e, g_lo, m - 1)
        for q in range(4):
            for j in range(4):
                dst = sq[32 * q:32 * q + 32, m % 2, 0:SEQ].rearrange("p (c j) -> p j c", j=4)[:, j, :]
                e.activation(dst, u_t[32 * j:32 * j + 32, 4 * m + q, :], ACT.Gelu_apprx_tanh).then_inc(ge_ok, 1)
        e.wait_ge(ge_ok, 16 * m + 16)
        e.activation(a_hi[:, m, :], sq[:, m % 2, 0:SEQ], ACT.Copy).then_inc(g_hi, 1)

    def mixer_dve(e, m):
        e.wait_ge(v_mm, m + 1)
        er, ei = (t[:, 4 * m:4 * m + 4, :].rearrange("p q c -> p (q c)") for t in (e_r, e_i))
        z = [t2[:, k, 0:SEQ] for k in range(2)]
        w = T4(SEQ)
        cmul(e, dve, z[0], z[1], (er, ei), (ps[:, 0, :], ps[:, 1, :]), w, -1)
        e.drain().then_inc(v_ev, 1)
        for k in range(2):
            for q in range(4):
                c = slice(q * P, (q + 1) * P)
                n = dve.did(e.tensor_tensor_scan(t0[:, k, c], S(V_M4)[:, 4 * m + q:4 * m + q + 1].to_broadcast([P, P]),
                                                 t2[:, k, c], 0.0, ALU.mult, ALU.add))
        e.wait_ge(dve_did, n)
        ge(e, y_mm, m)
        q4 = lambda t: t.rearrange("p (q c) -> p q c", q=4)
        x = [x_s[:, k, :, 1:P + 1] for k in range(2)]
        cmul(e, dve, x[0], x[1], (q4(er), q4(ei)), (q4(t0[:, 0, 0:SEQ]), q4(t0[:, 1, 0:SEQ])),
             [q4(t) for t in (t1[:, 0, 0:SEQ], t1[:, 1, 0:SEQ], t2[:, 0, 0:SEQ], t2[:, 1, 0:SEQ])])
        e.drain().then_inc(xs_ok, 1)

    def mixer_out_dve(e, m):
        e.wait_ge(y_mm, m + 1)
        for q in range(4):
            e.scalar_tensor_tensor(u_t[:, 4 * m + q, :], u_t[:, 4 * m + q, :], vec("ssm_d", 4 * m + q),
                                   ps[:, 2, q * P:(q + 1) * P], ALU.mult, ALU.add).then_inc(ys_ok, 1)

    def mixer_lo_dve(e, m):
        e.wait_ge(g_hi, m + 1)
        e.tensor_tensor(a_lo[:, m, :], sq[:, m % 2, 0:SEQ], a_hi[:, m, :], ALU.subtract).then_inc(g_lo, 1)

    def glu_act(e, u, m):
        e.wait_ge(unit_mm, u.n(2))
        e.activation(t0[:, m % 2, 0:SEQ], ps[:, (u.slot + 1) % 4, :], ACT.Sigmoid).then_inc(sig_ok, 1)

    def glu_dve(e, u, m):
        e.wait_ge(sig_ok, m + 1)
        e.tensor_tensor(t1[:, m % 2, 0:SEQ], ps[:, u.slot, :], t0[:, m % 2, 0:SEQ], ALU.mult).then_inc(unit_ev, 1)
        e.wait_ge(unit_ev, u.n(1))
        e.tensor_tensor(h[:, m, REAL], h[:, m, REAL], t1[:, m % 2, 0:SEQ], ALU.add).then_inc(unit_ev, 1)

    A0 = 32

    def pair_n(layer, j):
        return FFT * layer + j

    def up_act(e, layer, j0, u, s):
        k, j = s // 2, j0 + 2 * u.i + s // 2
        G = pair_n(layer, j)
        split_ahead(e, u, split_hi)
        if s % 2 == 0:
            ge(e, gel_ok, G)
        else:
            e.wait_ge(alo_ok, A0 + G)
        e.wait_ge(unit_ev, u.n(1))
        c = 2 * j + s % 2
        e.activation(t1[:, s % 2, 0:SEQ], t0[:, s % 2, 2:SEQ + 2], ACT.Identity, bias=vec(f"ffn_b{layer}", c),
                     scale=vec(f"ffn_w{layer}", 88 + c)).then_inc(c0_ok, 1)
        if s % 2:
            e.wait_ge(cg_ok, G + 1)
            e.activation(t2[:, k, 0:SEQ], t1[:, 0, 0:SEQ], ACT.Gelu_apprx_tanh).then_inc(gel_ok, 1)
            e.wait_ge(ay_ok, A0 + G + 1)
            e.activation(tile_of(a_hi, 2 * u.i + k), t1[:, 1:2, 0:SEQ], ACT.Copy).then_inc(ahi_ok, 1)

    def up_dve(e, layer, j0, u, s):
        k, j = s // 2, j0 + 2 * u.i + s // 2
        G = pair_n(layer, j)
        c = 2 * j + s % 2
        split_ahead(e, u, split_lo)
        e.wait_ge(unit_mm, u.n(1))
        e.tensor_tensor(t0[:, s % 2, 2:SEQ + 2], ps[:, u.slot, :], rstd[:, 0:SEQ], ALU.mult).then_inc(unit_ev, 1)
        e.wait_ge(c0_ok, 2 * G + s % 2 + 1)
        e.wait_ge(unit_ev, u.n(1))
        y = t1[:, s % 2, 0:SEQ]
        n = dve.did(e.scalar_tensor_tensor(y, t0[:, s % 2, 1:SEQ + 1], vec(f"ffn_w{layer}", 44 + c), y, ALU.mult, ALU.add))
        e.wait_ge(dve_did, n)
        e.scalar_tensor_tensor(y, t0[:, s % 2, 0:SEQ], vec(f"ffn_w{layer}", c), y, ALU.mult, ALU.add)\
            .then_inc(cg_ok if s % 2 == 0 else cv_ok, 1)
        if s % 2 == 0:
            e.wait_ge(cg_ok, G + 1)
        if s % 2:
            e.wait_ge(cv_ok, G + 1)
            e.wait_ge(gel_ok, G + 1)
            e.tensor_tensor(y, y, t2[:, k, 0:SEQ], ALU.mult).then_inc(ay_ok, 1)
            e.wait_ge(ahi_ok, A0 + G + 1)
            e.wait_ge(ay_ok, A0 + G + 1)
            a = 2 * u.i + k
            e.tensor_tensor(tile_of(a_lo, a), t1[:, 1:2, 0:SEQ], tile_of(a_hi, a), ALU.subtract).then_inc(alo_ok, 1)

    def ffn(e, who, layer, u0, n):
        j0, u = 0, u0
        gain = f"ple_norm{layer}"
        for gi, g in enumerate(FFG):
            first = 1 if layer == 0 and j0 == 0 else 0
            if who == "act":
                units(e, u, g // 2, lambda v, s: up_act(e, layer, j0, v, s), first)
            elif who == "dve":
                units(e, u, g // 2, lambda v, s: up_dve(e, layer, j0, v, s), first, counts=dve, rate=4)
            else:
                if j0 == 0:
                    def up0(v, s):
                        ready = None
                        if isinstance(v.i, int) and v.i == 0 and s == 0:
                            ready = lambda e, k: e.wait_ge(xlo_ok, 8 * XN[n - 1] + k + 1)
                        unit_pe(e, v, x_hi, x_lo, ready)
                    units(e, u, g // 2, up0, 1)
                else:
                    units(e, u, g // 2, lambda v, s: unit_pe(e, v, x_hi, x_lo))
            u += 2 * g
            last = gi == len(FFG) - 1
            for m in range(KT):
                v = Unit(u + m)
                if who == "act":
                    split_ahead(e, v, split_hi)
                    if last:
                        e.wait_ge(unit_ev, v.n(1))
                        norm_act(e, n, m, None)
                elif who == "dve":
                    split_ahead(e, v, split_lo)
                    add_dve(e, v, m)
                else:
                    ready = (lambda e, k: e.wait_ge(alo_ok, A0 + pair_n(layer, j0) + k + 1)) if m == 0 else None
                    unit_pe(e, v, a_hi, a_lo, ready, kt=g)
                    if last and m:
                        stat_pe(e, n, m - 1)
            u += KT
            j0 += g
        if who == "act":
            root_act(e, n, eps6)
            for m in range(KT):
                x_act(e, n, m, gain)
        elif who == "dve":
            root_dve(e, n)
            for m in range(KT):
                x_dve(e, XN[n], m, gain)
        else:
            stat_pe(e, n, KT - 1)

    def side(e, who, layer, u0, n):
        if who == "act":
            e.wait_ge(p_in, 16 * (layer + 1))
            e.activation(p_hi[:, :, :], p_raw[:, :, :], ACT.Copy).then_inc(phi_ok, 1)
            for s in range(2):
                split_ahead(e, Unit(u0 + s), split_hi)
            for m in range(KT):
                u = Unit(u0 + 2 + m)
                split_ahead(e, u, split_hi)
                e.wait_ge(unit_ev, u.n(1))
                ge(e, sgu_ok, 8 * layer + m - 1)
                e.activation(t1[:, m % 2, 0:SEQ], t0[:, m % 2, 0:SEQ], ACT.Sigmoid).then_inc(sg_ok, 1)
        elif who == "dve":
            e.wait_ge(phi_ok, layer + 1)
            e.tensor_tensor(p_lo[:, :, :], p_raw[:, :, :], p_hi[:, :, :], ALU.subtract).then_inc(plo_ok, 1)
            for s in range(2):
                u = Unit(u0 + s)
                split_ahead(e, u, split_lo)
                e.wait_ge(unit_mm, u.n(1))
                e.tensor_copy(pp[:, 4 * s:4 * s + 4, :], ps[:, 0:4, :]).then_inc(unit_ev, 1)
            for m in range(KT + 1):
                if m < KT:
                    u = Unit(u0 + 2 + m)
                    split_ahead(e, u, split_lo)
                    e.wait_ge(unit_mm, u.n(1))
                    ge(e, sg_ok, 8 * layer + m - 1)
                    e.tensor_tensor(t0[:, m % 2, 0:SEQ], ps[:, u.slot, :], rstd[:, 0:SEQ], ALU.mult).then_inc(unit_ev, 1)
                if m:
                    j = m - 1
                    e.wait_ge(sg_ok, 8 * layer + j + 1)
                    e.wait_ge(unit_ev, u0 + 2)
                    e.tensor_tensor(t2[:, j % 2, 0:SEQ], t1[:, j % 2, 0:SEQ], pp[:, j, :], ALU.mult).then_inc(sgu_ok, 1)
                    e.wait_ge(sgu_ok, 8 * layer + j + 1)
                    e.tensor_tensor(h[:, j, REAL], h[:, j, REAL], t2[:, j % 2, 0:SEQ], ALU.add).then_inc(h_fin, 1)
        else:
            e.wait_ge(plo_ok, layer + 1)
            for s in range(2):
                u = Unit(u0 + s)
                e.wait_ge(lo_ok, u.n(1))
                e.wait_ge(unit_ev, u.n())
                for q in range(4):
                    last = products(e, u, q, p_hi, p_lo, kt=2, w0=2 * q)
                last.then_inc(unit_mm, 1)
            e.wait_ge(unit_ev, u0 + 2)
            for m in range(KT):
                ready = (lambda e, k: e.wait_ge(xlo_ok, 8 * XN[n] + k + 1)) if m == 0 else None
                unit_pe(e, Unit(u0 + 2 + m), x_hi, x_lo, ready)


    def normed(e, who, u0, k0, store, gain, hi, lo, first_ready):
        for m in range(8 + 1):
            if m < 8:
                u = Unit(u0 + m)
                if who == "act":
                    split_ahead(e, u, split_hi)
                    e.wait_ge(unit_ev, u.n(1))
                    head_sq(e, k0 + m, store[:, m, :])
                elif who == "dve":
                    split_ahead(e, u, split_lo)
                    e.wait_ge(unit_mm, u.n(1))
                    e.tensor_tensor(store[:, m, :], ps[:, u.slot, :], rstd[:, 0:SEQ], ALU.mult).then_inc(unit_ev, 1)
                else:
                    unit_pe(e, u, hi, lo, first_ready if m == 0 else None)
            if m:
                j = m - 1
                if who == "act":
                    head_root(e, k0 + j, HD, eps6)
                elif who == "dve":
                    head_scale(e, k0 + j, store[:, j, :], gain, store[:, j, :])
                else:
                    head_pe(e, k0 + j, blk)

    def stage2_pool(e, p):
        par = p % 2
        k = 4 * p
        ge(e, o_ok, p - 1)
        for c in range(2):
            r = slice(HD * c, HD * c + HD)
            e.wait_ge(staged, 32 + k + c)
            e.tensor_copy(qs2[r, par, c, :], q2[r, p, :]).then_inc(staged, 1)
        e.wait_ge(staged, 32 + k + 2)
        e.tensor_copy(ks2[:, par, :], k2[:, p, :]).then_inc(staged, 1)
        e.wait_ge(staged, 32 + k + 3)
        e.tensor_copy(vs2[:, par, :], v2[:, p, :]).then_inc(staged, 1)

    def bias_load(e, p):
        ge(e, blo_ok, p)
        src = bass.AP(scratch.tensor, scratch.offset + p * 640 + 1, [[1, P], [1, SEQ]])
        e.dma_start(b_raw[:, 0, :], src).then_inc(b_in, 16)

    def attention2(e, who):
        def pe_scores(g):
            p, qt, sl = g // 4, g % 4, g % 2
            N = (qt + 1) * P
            if qt == 0:
                e.wait_ge(staged, 32 + 4 * p + 4)
                e.wait_ge(blo_ok, p + 1)
                ge(e, o_ok, p - 1)
                for j in range(4):
                    last = e.transpose(ps[:, 6 + p % 2, j * P:(j + 1) * P], vs2[:, p % 2, j * P:(j + 1) * P], ident[:, :])
                last.then_inc(vt_mm, 1)
            ge(e, exp_ok, 32 + 2 * (g - 1))
            for c in range(2):
                o = ps[:, 2 * sl + c, 0:N]
                e.matmul(o, qs2[:, p % 2, c, qt * P:(qt + 1) * P], ks2[:, p % 2, 0:N], start=True, stop=False)
                for n, t in enumerate((b_hi, b_lo)):
                    last = e.matmul(o, flip_r[:, :], t[:, p % 2, SEQ - N:SEQ], start=False, stop=(n == 1))
            last.then_inc(s_mm, 1)

        def pe_turn(g):
            p, qt, sl = g // 4, g % 4, g % 2
            e.wait_ge(nrm_ok, 32 + g + 1)
            if qt == 0:
                e.wait_ge(v2_ok, p + 1)
            for j in range(qt + 1):
                last = e.transpose(ps[:, 4 + sl, j * P:(j + 1) * P], t0[:, sl, j * P:(j + 1) * P], ident[:, :])
            last.then_inc(pt_mm, 1)

        def pe_pv(g):
            p, qt, sl = g // 4, g % 4, g % 2
            e.wait_ge(pt_ok, 64 + g + 1)
            if qt == 0:
                ge(e, o_ok, p - 1)
            for j in range(qt + 1):
                last = e.matmul(ps[:, 6 + p % 2, qt * P:(qt + 1) * P], vtok[:, p % 2, j, :], pt2[:, sl, j, :],
                                start=(j == 0), stop=(j == qt))
            last.then_inc(pv_mm, 1)

        def dve_top(g):
            p, qt, sl = g // 4, g % 4, g % 2
            N = (qt + 1) * P
            if qt == 0:
                e.wait_ge(bhi_ok, p + 1)
                e.tensor_tensor(b_lo[:, p % 2, :], b_raw[:, 0, :], b_hi[:, p % 2, :], ALU.subtract).then_inc(blo_ok, 1)
            e.wait_ge(s_mm, 32 + g + 1)
            for c in range(2):
                n = dve.did(e.reduce_max(small[:, 0, 2 * sl + c:2 * sl + c + 1], ps[:, 2 * sl + c, 0:N], AX_X))
            e.wait_ge(dve_did, n)
            e.tensor_scalar(small[:, 1, 2 * sl:2 * sl + 2], small[:, 0, 2 * sl:2 * sl + 2], -0.125, None, ALU.mult)\
                .then_inc(nb_ok, 1)

        def dve_mix(g):
            p, qt, sl = g // 4, g % 4, g % 2
            N = (qt + 1) * P
            e.wait_ge(exp_ok, 32 + 2 * g + 2)
            r = small[:, 3, 2 * sl:2 * sl + 2]
            n = dve.did(e.reciprocal(r, small[:, 2, 2 * sl:2 * sl + 2]))
            e.wait_ge(dve_did, n)
            n = dve.did(e.tensor_tensor(small[:, 3, 2 * sl + 1:2 * sl + 2], small[:, 3, 2 * sl + 1:2 * sl + 2],
                                        neg_lam[:, :], ALU.mult))
            n = dve.did(e.tensor_scalar(t0[:, sl, 0:N], t0[:, sl, 0:N], small[:, 3, 2 * sl:2 * sl + 1], None, ALU.mult))
            e.wait_ge(dve_did, n)
            e.scalar_tensor_tensor(t0[:, sl, 0:N], t1[:, sl, 0:N], small[:, 3, 2 * sl + 1:2 * sl + 2],
                                   t0[:, sl, 0:N], ALU.mult, ALU.add).then_inc(nrm_ok, 1)

        def dve_out(p):
            e.wait_ge(pv_mm, 32 + 4 * p + 4)
            e.wait_ge(staged, 32 + 4 * p + 4)
            e.tensor_copy(q2[:, p, :], ps[:, 6 + p % 2, :]).then_inc(o_ok, 1)

        def act_exp(g):
            p, qt, sl = g // 4, g % 4, g % 2
            N = (qt + 1) * P
            if qt == 0:
                e.wait_ge(b_in, 16 * (p + 1))
                ge(e, s_mm, 32 + 4 * (p - 1))
                e.activation(b_hi[:, p % 2, :], b_raw[:, 0, :], ACT.Copy).then_inc(bhi_ok, 1)
            e.wait_ge(nb_ok, 32 + g + 1)
            ge(e, pt_mm, 32 + g - 1)
            for c, t in enumerate((t0, t1)):
                e.activation(t[:, sl, 0:N], ps[:, 2 * sl + c, 0:N], ACT.Exp,
                             bias=small[:, 1, 2 * sl + c:2 * sl + c + 1], scale=0.125,
                             accum_out=small[:, 2, 2 * sl + c:2 * sl + c + 1]).then_inc(exp_ok, 1)

        def act_turn(g):
            p, qt, sl = g // 4, g % 4, g % 2
            N = (qt + 1) * P
            if qt == 0:
                e.wait_ge(vt_mm, 4 + p + 1)
                e.activation(vtok[:, p % 2, :, :].rearrange("p j c -> p (j c)"), ps[:, 6 + p % 2, :], ACT.Copy)\
                    .then_inc(v2_ok, 1)
            e.wait_ge(pt_mm, 32 + g + 1)
            ge(e, pv_mm, 32 + g - 1)
            e.activation(pt2[:, sl, 0:qt + 1, :].rearrange("p j c -> p (j c)"), ps[:, 4 + sl, 0:N], ACT.Copy)\
                .then_inc(pt_ok, 1)

        for g in range(32 + 2):
            if who == "pe":
                if g < 32:
                    pe_scores(g)
                if 1 <= g < 33:
                    pe_turn(g - 1)
                if g >= 2:
                    pe_pv(g - 2)
            elif who == "dve":
                if g < 32:
                    dve_top(g)
                if 1 <= g < 33:
                    dve_mix(g - 1)
                if g >= 5 and (g - 5) % 4 == 0:
                    dve_out((g - 5) // 4)
            else:
                if g < 32:
                    act_exp(g)
                if 1 <= g < 33:
                    act_turn(g - 1)

    block = ctx.enter_context(nc.Block())

    @block.sync
    def _(sp):
        sp.dma_start(vecs[:, :], A["vecs"]).then_inc(consts_in, 16)
        sp.dma_start(h[:, 0:4, :], A["xT"][:, 0:4, :]).then_inc(h_in[0], 16)
        load_unit(sp, Unit(0))
        sp.dma_start(h[:, 4:8, :], A["xT"][:, 4:8, :]).then_inc(h_in[1], 16)
        load_unit(sp, Unit(1))
        for name, t in (("ones", ones), ("blk", blk), ("ident", ident), ("flip", flip), ("mask", mask), ("zero", zero)):
            sp.dma_start(t[:, :], A[name]).then_inc(consts_in, 16)
        sp.dma_start(wf[:, :, :], A["wf"]).then_inc(consts_in, 16)
        sp.dma_start(rel[:, :], A["rel"]).then_inc(consts_in, 16)
        for s in range(2, 4):
            load_unit(sp, Unit(s))
        with sp.Fori(1, NLOAD // 4) as i:
            for s in range(4):
                load_unit(sp, Unit(s, i))
        if stop in (99, 7, 4):
            sp.wait_ge(h_fin, 8 * (2 if stop == 4 else 3))
        elif stop == 1:
            sp.wait_ge(h_fin, 8)
        else:
            sp.wait_ge(fence_at, {2: 20, 5: 32}[stop])
        sp.dma_start(out, h[:, :, REAL]).then_inc(stored, 16)
        sp.wait_ge(stored, 16)

    @block.gpsimd
    def _(e):
        e.memset(eps5[:, :], 1e-5).then_inc(consts_ok, 1)
        e.memset(eps6[:, :], 1e-6).then_inc(consts_ok, 1)
        e.memset(eps_o[:, :], 1e-6 / (1.0 - LAM) ** 2).then_inc(consts_ok, 1)
        e.memset(aug_q[:, :, :, :], 0.0).then_inc(consts_ok, 1)
        e.memset(aug_k[:, :], 0.0).then_inc(consts_ok, 1)
        e.wait_ge(consts_ok, 5)
        e.memset(aug_k[32:40, :], 1.0).then_inc(consts_ok, 1)
        fence(e, 1)
        e.memset(qs[:, :, :, :], 0.0).then_inc(qz_ok, 1)
        e.wait_ge(qz_ok, 1)
        for i in range(2):
            stage1_pool(e, i)
        fence(e, 2)
        if stop == 1:
            return

        def spread(u, s):
            e.wait_ge(unit_ev, u.n(1))
            m = u.n(-U_SSM)
            for q in range(4):
                for j in (2, 3):
                    ge(e, ut_p, 8 * m + 2 * q + j - 2)
                    spread_u(e, u, m, q, j, "p").then_inc(ut_p, 1)

        units(e, U_SSM, 2, spread, 1)
        fence(e, 3)
        e.wait_ge(par_v, 3)
        for m in range(8):
            matrices_pool(e, m)
        fence(e, 4)
        e.dma_start(onehot[:, :], A["onehot"]).then_inc(tab_in, 16)
        e.dma_start(neg_row[:, :], A["neg_row"]).then_inc(tab_in, 16)
        e.dma_start(p_raw[:, :, :], A["pT"][:, 0, :, :]).then_inc(p_in, 16)
        fence(e, 5)
        if stop in (2, 4):
            return
        fence(e, 6)
        e.wait_ge(tab_ok, 2)
        e.dma_start(scratch, tab[0:8, :]).then_inc(tab_out, 16)
        e.memset(qs2[:, :, :, :], 0.0).then_inc(zz_ok, 1)
        e.wait_ge(zz_ok, 1)
        e.wait_ge(tab_out, 16)
        for p in range(8):
            bias_load(e, p)
            stage2_pool(e, p)
        fence(e, 7)
        fence(e, 8)
        e.dma_start(p_raw[:, :, :], A["pT"][:, 1, :, :]).then_inc(p_in, 16)

    @block.scalar
    def _(e):
        for m in range(KT):
            if m % 4 == 0:
                e.wait_ge(h_in[m // 4], 16)
            if m == 0:
                e.wait_ge(consts_in, 16 * 9)
            norm_act(e, 0, m, "norm_mix", TOK)
            if m in (1, 3):
                split_hi(e, Unit(m // 2))
        e.wait_ge(consts_ok, 6)
        root_act(e, 0, eps5, TOK)
        e.activation(wf_hi[:, :, :], wf[:, :, :], ACT.Copy).then_inc(wf_ok, 1)
        e.activation(ident_b[:, :], ident[:, :], ACT.Copy).then_inc(wf_ok, 1)
        e.activation(mask_b[:, :], mask[:, :], ACT.Copy).then_inc(wf_ok, 1)
        e.activation(flip_r[:, :], flip[:, :], ACT.Copy).then_inc(wf_ok, 1)
        units(e, U_QKVB, 4, lambda u, s: split_ahead(e, u, split_hi), 1)
        f_scalar(e)
        units(e, U_CU, 2, lambda u, s: split_ahead(e, u, split_hi))
        fence(e, 1)
        for i in range(2):
            attention1_act(e, i)
        fence(e, 2)
        for m in range(8 + 2):
            if m < 8:
                head_sq(e, m, y_tile(m))
            if 1 <= m < 9:
                head_root(e, m - 1, HD, eps5)
            if m >= 2:
                head_hi(e, m - 2, m - 2)
        for m in range(KT):
            u = Unit(U_OUT1 + m)
            split_ahead(e, u, split_hi)
            e.wait_ge(unit_ev, u.n(1))
            norm_act(e, 1, m, "norm_mlp")
        root_act(e, 1, eps5)

        def ff(u, s):
            split_ahead(e, u, split_hi)
            if s < 8:
                hidden_hi(e, 8 * u.i + s, s)

        units(e, U_FF, 3, ff, cycle=16)
        for s in range(16):
            u = Unit(U_FF + 48 + s)
            split_ahead(e, u, split_hi)
            if s < 8:
                hidden_hi(e, 24 + s, s)
            else:
                e.wait_ge(unit_ev, u.n(1))
                norm_act(e, 2, s - 8, None)
        root_act(e, 2, eps5)
        if stop == 1:
            return
        for m in range(KT):
            e.wait_ge(h_fin, m + 1)
            norm_act(e, 3, m, "ssm_norm")
        root_act(e, 3, eps6)
        e.dma_start(c_raw[:, :, :, :], A["ssm_bc"][:, 2:4, :, :]).then_inc(bc_in, 16)

        def spread(u, s):
            split_ahead(e, u, split_hi)
            e.wait_ge(unit_ev, u.n(1))
            m = u.n(-U_SSM)
            for q in range(4):
                for j in (0, 1):
                    spread_u(e, u, m, q, j, "a").then_inc(ut_a, 1)

        units(e, U_SSM, 2, spread, 1)
        fence(e, 3)
        e.dma_start(t2[:, :, 0:SEQ], A["ssm_bc"][:, 0:2, :, :].rearrange("p a b c -> p a (b c)")).then_inc(bc_in, 16)
        system_act(e)
        for m in range(8 + 1):
            if m < 8:
                mixer_front_act(e, m)
            if m:
                mixer_back_act(e, m - 1)
        fence(e, 4)
        for m in range(KT):
            u = Unit(U_GLU + 2 * m)
            split_ahead(e, u, split_hi)
            split_ahead(e, u.ahead(1), split_hi)
            glu_act(e, u, m)
            e.wait_ge(unit_ev, u.n(2))
            norm_act(e, 4, m, "ffn_norm0")
        root_act(e, 4, eps6)
        fence(e, 5)
        if stop == 2:
            return
        ffn(e, "act", 0, U_FFNA, 5)
        side(e, "act", 0, U_PPA, 5)
        if stop == 4:
            return
        for m in range(KT):
            e.wait_ge(h_fin, 8 + m + 1)
            if m == 0:
                e.wait_ge(unit_mm, U_Q)
            norm_act(e, 6, m, "kv_norm")
        for m in range(KT):
            x_act(e, 6, m, "attn_norm", hi=a_hi)
        root_act(e, 6, eps6)
        normed(e, "act", U_Q, 8, q2, None, None, None, None)
        normed(e, "act", U_KV, 16, k2, None, None, None, None)
        units(e, U_KV + 8, 2, lambda u, s: split_ahead(e, u, split_hi))
        e.wait_ge(lam_mm, 1)
        e.activation(small[:, 1, 0:2], ps[:, 5, 0:2], ACT.Exp).then_inc(lam_a, 1)
        fence(e, 6)
        attention2(e, "act")
        fence(e, 7)
        for m in range(8 + 2):
            if m < 8:
                head_sq(e, 24 + m, q2[:, m, :])
            if 1 <= m < 9:
                head_root(e, 24 + m - 1, P * (1 - LAM) ** 2, eps_o)
            if m >= 2:
                head_hi(e, 24 + m - 2, m - 2)
        for m in range(KT):
            u = Unit(U_WO + m)
            split_ahead(e, u, split_hi)
            e.wait_ge(unit_ev, u.n(1))
            norm_act(e, 7, m, "ffn_norm1")
        root_act(e, 7, eps6)
        fence(e, 8)
        if stop == 5:
            return
        ffn(e, "act", 1, U_FFNB, 8)
        side(e, "act", 1, U_PPB, 8)

    @block.vector
    def _(e):
        e.wait_ge(consts_in, 16 * 9)
        n = dve.did(e.memset(t2[0:8, 0, :], 1.0))
        for m in range(KT):
            x_dve(e, 0, m, "norm_mix", TOK)
            if m in (2, 4):
                split_lo(e, Unit(m // 2 - 1))
        e.wait_ge(wf_ok, 1)
        e.tensor_tensor(wf_lo[:, :, :], wf[:, :, :], wf_hi[:, :, :], ALU.subtract).then_inc(wflo_ok, 1)
        root_dve(e, 0, TOK)

        def qkvb_dve(u, s):
            split_ahead(e, u, split_lo)
            t = u.n()
            wide_dve(e, u, tile_of(qkvb, t).rearrange("p a b -> p (a b)"))

        units(e, U_QKVB, 4, qkvb_dve, 1)
        f_dve(e)

        def conv(u, s):
            split_ahead(e, u, split_lo)
            conv_dve(e, u, s)

        units(e, U_CU, 2, conv, counts=dve, rate=10)
        fence(e, 1)
        n = dve.did(e.memset(vp[:, :, :, :, :], 0.0))
        e.memset(vm[:, :, :, :], 0.0).then_inc(vz_ok, 1)
        for i in range(2):
            attention1_dve(e, i)
        fence(e, 2)
        for m in range(8 + 2):
            if 1 <= m < 9:
                head_scale(e, m - 1, y_tile(m - 1), vec("out_norm", m - 1))
            if m >= 2:
                head_lo(e, m - 2, m - 2)
        for m in range(KT):
            u = Unit(U_OUT1 + m)
            split_ahead(e, u, split_lo)
            add_dve(e, u, m)
            if m:
                x_dve(e, 1, m - 1, "norm_mlp")
        x_dve(e, 1, KT - 1, "norm_mlp")
        root_dve(e, 1)

        def ff(u, s):
            split_ahead(e, u, split_lo)
            if s < 8:
                relu2_dve(e, u, s)
                if s:
                    hidden_lo(e, 8 * u.i + s - 1, s - 1)
                if s == 7:
                    hidden_lo(e, 8 * u.i + 7, 7)
            else:
                add_dve(e, u, s - 8)

        units(e, U_FF, 3, ff, first=1, cycle=16)
        for s in range(16):
            ff(Unit(U_FF + s, 3, 16), s)
        root_dve(e, 2)
        for m in range(KT):
            e.scalar_tensor_tensor(h[:, m, REAL], h[:, m, REAL], vec("final_norm", m), rstd[:, 0:SEQ],
                                   ALU.mult, ALU.mult).then_inc(h_fin, 1)
        if stop == 1:
            return
        for m in range(KT):
            x_dve(e, 2, m, "ssm_norm")
        root_dve(e, 3)

        def project_u(u, s):
            split_ahead(e, u, split_lo)
            e.wait_ge(unit_mm, u.n(1))
            m = u.n(-U_SSM)
            ge(e, ut_a, 8 * (m - 1))
            ge(e, ut_p, 8 * (m - 1))
            e.tensor_tensor(t0[:, s % 2, 0:SEQ], ps[:, u.slot, :], rstd[:, 0:SEQ], ALU.mult).then_inc(unit_ev, 1)

        units(e, U_SSM, 2, project_u, 1)
        fence(e, 3)
        for t in (v_b, c_p):
            dve.did(e.memset(t[:], 0.0))
        dve.did(e.memset(t_l[:, :, :], 0.0))
        n = dve.did(e.memset(x_s[:, :, :, 0:1], 0.0))
        e.wait_ge(dve_did, n)
        system_dve(e)
        for m in range(8 + 1):
            if m < 8:
                mixer_dve(e, m)
            if m >= 2:
                mixer_lo_dve(e, m - 2)
            if m:
                mixer_out_dve(e, m - 1)
        mixer_lo_dve(e, 7)
        fence(e, 4)
        for m in range(KT):
            u = Unit(U_GLU + 2 * m)
            split_ahead(e, u, split_lo)
            split_ahead(e, u.ahead(1), split_lo)
            glu_dve(e, u, m)
            if m:
                x_dve(e, 3, m - 1, "ffn_norm0")
        x_dve(e, 3, KT - 1, "ffn_norm0")
        root_dve(e, 4)
        fence(e, 5)
        if stop == 2:
            return
        n = dve.did(e.memset(t0[:, :, 0:2], 0.0))
        e.wait_ge(dve_did, n)
        ffn(e, "dve", 0, U_FFNA, 5)
        side(e, "dve", 0, U_PPA, 5)
        if stop == 4:
            return
        for m in range(KT):
            x_dve(e, 5, m, "kv_norm")
        for m in range(KT):
            x_dve(e, 6, m, "attn_norm", hi=a_hi, lo=a_lo)
        root_dve(e, 6)
        c = COL["lambdas"]
        e.tensor_tensor(small[:, 0, 0:2], vecs[:, c:c + 4:2], vecs[:, c + 1:c + 4:2], ALU.mult).then_inc(lam_v, 1)
        normed(e, "dve", U_Q, 8, q2, vec("q_norm"), None, None, None)
        normed(e, "dve", U_KV, 16, k2, vec("k_norm"), None, None, None)

        def project_v(u, s):
            split_ahead(e, u, split_lo)
            e.wait_ge(unit_mm, u.n(1))
            e.tensor_tensor(tile_of(v2, u.n(-U_KV - 8)), ps[:, u.slot:u.slot + 1, :],
                            rstd[:, 0:SEQ].unsqueeze(1), ALU.mult).then_inc(unit_ev, 1)

        units(e, U_KV + 8, 2, project_v)
        e.wait_ge(tab_mm, 1)
        for lo, n in ((0, SEQ), (SEQ, P)):
            e.scalar_tensor_tensor(tab[0:8, lo:lo + n], ps[0:8, 6 + lo // SEQ, 0:n], 8.0, neg_row[:, lo:lo + n],
                                   ALU.mult, ALU.add).then_inc(tab_ok, 1)
        e.wait_ge(lam_a, 1)
        n = dve.did(e.tensor_tensor(small[:, 2, 0:1], small[:, 1, 1:2], small[:, 1, 0:1], ALU.subtract))
        e.wait_ge(dve_did, n)
        n = dve.did(e.tensor_scalar(neg_lam[:, :], small[:, 2, 0:1], -LAM, None, ALU.add))
        fence(e, 6)
        attention2(e, "dve")
        fence(e, 7)
        for m in range(8 + 2):
            if 1 <= m < 9:
                head_scale(e, 24 + m - 1, q2[:, m - 1, :], vec("subln"))
            if m >= 2:
                head_lo(e, 24 + m - 2, m - 2)
        for m in range(KT):
            u = Unit(U_WO + m)
            split_ahead(e, u, split_lo)
            add_dve(e, u, m)
            if m:
                x_dve(e, 7, m - 1, "ffn_norm1")
        x_dve(e, 7, KT - 1, "ffn_norm1")
        root_dve(e, 7)
        fence(e, 8)
        if stop == 5:
            return
        n = dve.did(e.memset(t0[:, :, 0:2], 0.0))
        e.wait_ge(dve_did, n)
        ffn(e, "dve", 1, U_FFNB, 8)
        side(e, "dve", 1, U_PPB, 8)

    @block.tensor
    def _(e):
        e.wait_ge(consts_in, 16 * 9)
        for m in range(KT):
            stat_pe(e, 0, m, TOK)
        units(e, U_QKVB, 4, lambda u, s: wide_pe(e, u), 1)
        f_pe(e)
        units(e, U_CU, 2, lambda u, s: wide_pe(e, u))
        fence(e, 1)
        for i in range(2):
            attention1_pe(e, i)
        fence(e, 2)
        for m in range(8):
            head_pe(e, m, blk)
        e.wait_ge(unit_ev, U_OUT1)
        for m in range(KT):
            ready = (lambda e, k: e.wait_ge(hn_lo, k + 1)) if m == 0 else None
            unit_pe(e, Unit(U_OUT1 + m), a_hi, a_lo, ready)
            if m:
                stat_pe(e, 1, m - 1)
        stat_pe(e, 1, KT - 1)

        def ff(u, s):
            ready = None
            if s == 0 and isinstance(u.i, int) and u.i == 0:
                ready = lambda e, k: e.wait_ge(xlo_ok, 8 + k + 1)
            if s == 8:
                ready = lambda e, k: e.wait_ge(alo_ok, 8 * u.i + k + 1)
            if s < 8:
                unit_pe(e, u, x_hi, x_lo, ready)
            else:
                unit_pe(e, u, a_hi, a_lo, ready)

        units(e, U_FF, 3, ff, first=1, cycle=16)
        for s in range(16):
            ff(Unit(U_FF + s, 3, 16), s)
            if s > 8:
                stat_pe(e, 2, s - 9)
        stat_pe(e, 2, KT - 1)
        if stop == 1:
            return
        for m in range(KT):
            stat_pe(e, 3, m)

        def project_u(u, s):
            ready = None
            if isinstance(u.i, int) and s == 0:
                ready = lambda e, k: e.wait_ge(xlo_ok, 16 + k + 1)
            unit_pe(e, u, x_hi, x_lo, ready)

        units(e, U_SSM, 2, project_u, 1)
        fence(e, 3)
        for m in range(8 + 1):
            if m < 8:
                mixer_front_pe(e, m)
            if m:
                mixer_back_pe(e, m - 1)
        fence(e, 4)
        for m in range(2 * KT):
            ready = (lambda e, k: e.wait_ge(g_lo, k + 1)) if m == 0 else None
            unit_pe(e, Unit(U_GLU + m), a_hi, a_lo, ready)
            if m % 2 and m > 2:
                stat_pe(e, 4, m // 2 - 1)
        stat_pe(e, 4, KT - 1)
        fence(e, 5)
        if stop == 2:
            return
        ffn(e, "pe", 0, U_FFNA, 5)
        side(e, "pe", 0, U_PPA, 5)
        if stop == 4:
            return
        for m in range(KT):
            stat_pe(e, 6, m)
        e.wait_ge(lam_v, 1)
        e.matmul(ps[:, 5, 0:2], ones[:, :], small[:, 0, 0:2], start=True, stop=True).then_inc(lam_mm, 1)
        normed(e, "pe", U_Q, 8, None, None, a_hi, a_lo, lambda e, k: e.wait_ge(xlo_ok, 48 + k + 1))
        normed(e, "pe", U_KV, 16, None, None, x_hi, x_lo, None)
        units(e, U_KV + 8, 2, lambda u, s: unit_pe(e, u, x_hi, x_lo))
        e.wait_ge(hn_rt, 24)
        e.wait_ge(tab_in, 32)
        e.matmul(ps[0:8, 6, :], rel[:, :], onehot[:, 0:SEQ], start=True, stop=True)
        e.matmul(ps[0:8, 7, 0:P], rel[:, :], onehot[:, SEQ:640], start=True, stop=True).then_inc(tab_mm, 1)
        fence(e, 6)
        attention2(e, "pe")
        fence(e, 7)
        for m in range(8):
            head_pe(e, 24 + m, ones)
        for m in range(KT):
            ready = (lambda e, k: e.wait_ge(hn_lo, 8 + k + 1)) if m == 0 else None
            unit_pe(e, Unit(U_WO + m), a_hi, a_lo, ready)
            if m:
                stat_pe(e, 7, m - 1)
        stat_pe(e, 7, KT - 1)
        fence(e, 8)
        if stop == 5:
            return
        ffn(e, "pe", 1, U_FFNB, 8)
        side(e, "pe", 1, U_PPB, 8)


def lay_out(x):
    f = np.float32

    def cols(v, parts=P):
        return np.ascontiguousarray(np.asarray(v, f).reshape(-1, parts).T)

    V = np.zeros((P, NCOL), f)

    def put(name, m, parts=P):
        V[:parts, COL[name]:COL[name] + m.shape[1]] = m

    put("norm_mix", cols(x["norm_mix_g"])); put("out_norm", cols(x["out_norm_g"]))
    put("norm_mlp", cols(x["norm_mlp_g"])); put("final_norm", cols(x["final_norm_g"]))
    put("conv_w", cols(x["conv_w"])); put("b_f", np.asarray(x["b_f"], f).reshape(8, 1), 8)
    put("ssm_norm", cols(x["ssm_norm_2"])); put("kv_norm", cols(x["kv_norm_2"]))
    put("attn_norm", cols(x["attn_norm_2"]))
    for n in ("k_norm", "q_norm"):
        put(n, np.tile(np.asarray(x[n + "_2"], f).reshape(1, HD), (1, 2)).T)
    put("subln", cols(x["subln_2"]))
    order = np.arange(2 * FFT).reshape(2, FFT).T.ravel()
    for n in range(2):
        put(f"ffn_norm{n}", cols(x["ffn_norm_2"][n])); put(f"ple_norm{n}", cols(x["ple_norm_2"][n]))
        for tap in range(3):
            V[:, COL[f"ffn_w{n}"] + 44 * tap:COL[f"ffn_w{n}"] + 44 * tap + 44] = \
                cols(x["ffn_conv_w_2"][n][tap])[:, order]
        V[:, COL[f"ffn_b{n}"]:COL[f"ffn_b{n}"] + 44] = cols(x["ffn_conv_b_2"][n])[:, order]
    put("lam_re", cols(x["ssm_lambda_re_2"])); put("lam_im", cols(x["ssm_lambda_im_2"]))
    put("log_dt", cols(np.repeat(np.asarray(x["ssm_log_dt_2"], f).reshape(-1), HD)))
    dsk = np.asarray(x["ssm_d_2"], f).reshape(32, 32).T
    put("ssm_d", np.tile(dsk, (4, 1)))
    put("lambdas", np.stack([np.asarray(x[n + "_2"], f).reshape(HD) for n in
                             ("lambda_q1", "lambda_k1", "lambda_q2", "lambda_k2")], 1), HD)

    def tiles(w, ks, ms):
        w = np.asarray(w, f)
        t = w.reshape(w.shape[0] // P, P, w.shape[1] // P, P)
        o = np.zeros((len(ms), P, 8, P), f)
        o[:, :, :len(ks)] = t[list(ks)][:, :, list(ms)].transpose(2, 1, 0, 3)
        return o

    w_in = np.asarray(x["w_in"], f)[0]
    q, k, v, fg, b, c, u = np.split(w_in, [512, 1024, 1536, 1544, 2056, 2568], axis=1)
    K8 = range(8)
    out = [tiles(m, K8, range(4)) for m in (q, k, v, b)]
    out.append(tiles(np.concatenate([c, u], 1), K8, [0, 4, 1, 5, 2, 6, 3, 7]))
    out.append(tiles(x["w_out"][0], K8, K8))
    for g in range(4):
        out.append(tiles(x["w_ff1"][0], K8, range(8 * g, 8 * g + 8)))
        out.append(tiles(x["w_ff2"][0], range(8 * g, 8 * g + 8), K8))
    out.append(tiles(x["ssm_w_in_2"][0], K8, K8))
    out.append(tiles(x["ssm_w_glu_2"][0], K8, [m + 8 * s for m in range(8) for s in range(2)]))

    def tail(n):
        j0 = 0
        for g in FFG:
            out.append(tiles(x["ffn_w_up_2"][n], K8, [j + FFT * s for j in range(j0, j0 + g) for s in range(2)]))
            out.append(tiles(x["ffn_w_down_2"][n], range(j0, j0 + g), K8))
            j0 += g
        side = np.asarray(x["ple_w_proj_2"][n], f).reshape(2, P, 2, 4, P)
        out.append(side.transpose(2, 1, 3, 0, 4).reshape(2, P, 8, P))
        out.append(tiles(x["ple_w_gate_2"][n], K8, K8))

    tail(0)
    out.append(tiles(x["attn_w_q_2"][0], K8, K8))
    kv = np.asarray(x["kv_w_2"], f)
    out.append(tiles(kv[:, :D], K8, K8)); out.append(tiles(kv[:, D:], K8, K8))
    out.append(tiles(x["attn_w_o_2"][0], K8, K8))
    tail(1)
    W = np.concatenate(out)
    assert W.shape[0] == NU

    hx = np.concatenate([np.asarray(x["meta_tokens"], f), np.asarray(x["x"], f)[0]], 0)
    eye = np.eye(P, dtype=f)
    grp = lambda a: np.asarray(a, f)[0].reshape(32, P, 16).transpose(1, 0, 2)
    grc = lambda a: np.asarray(a, f)[0].transpose(0, 2, 1).reshape(32, P, 16).transpose(1, 0, 2)
    dist = SEQ - np.arange(640)
    far = np.maximum(dist, 16).astype(f)
    big = 16 + (np.log(far / f(16)) / f(np.log(8.0)) * f(16)).astype(np.int32)
    bucket = np.where(dist < 16, np.maximum(dist, 0), np.minimum(big, 31))
    onehot = (bucket[None] == np.arange(32)[:, None]).astype(f) * (dist >= 0)
    neg_row = np.tile(np.where(dist < 0, f(NEG), f(0)), (8, 1))
    i = np.arange(P)
    return {
        "wstream": W.reshape(NU * P, 8 * P), "xT": np.ascontiguousarray(hx.T.reshape(8, P, TOK).transpose(1, 0, 2)),
        "vecs": V, "ones": np.ones((P, P), f), "ident": eye, "flip": np.ascontiguousarray(eye[::-1]), "zero": np.zeros((P, P), f),
        "blk": np.kron(np.eye(2), np.ones((HD, HD))).astype(f),
        "mask": np.where(i[None, :] > i[:, None], NEG, 0.0).astype(f),
        "wf": np.ascontiguousarray(fg.reshape(8, P, 8).transpose(1, 0, 2)),
        "ssm_bc": np.ascontiguousarray(np.stack([grp(x["ssm_b_re_2"]), grp(x["ssm_b_im_2"]),
                                                 grc(x["ssm_c_re_2"]), grc(x["ssm_c_im_2"])], 1)),
        "pT": np.ascontiguousarray(np.asarray(x["p_2"], f)[:, 0].transpose(0, 2, 1).reshape(2, 2, P, SEQ)
                                   .transpose(2, 0, 1, 3)),
        "rel": np.asarray(x["rel_bias_2"], f), "onehot": onehot, "neg_row": neg_row,
    }


def kernel(**inputs):
    import concourse.bacc as bacc
    from concourse.bass_utils import run_bass_kernel_spmd

    nc = bacc.Bacc("TRN2", target_bir_lowering=False, num_devices=1)
    arrays = lay_out(inputs)
    A = {n: nc.dram_tensor(f"in_{n}", a.shape, mybir.dt.from_np(a.dtype), kind="ExternalInput").ap()
         for n, a in arrays.items()}
    out = nc.dram_tensor("out", (P, KT, SEQ), F32, kind="ExternalOutput").ap()
    program(nc, A, out)
    got = run_bass_kernel_spmd(nc, [{f"in_{n}": a for n, a in arrays.items()}], core_ids=[0]).results[0]["out"]
    return np.ascontiguousarray(got.transpose(2, 1, 0).reshape(1, SEQ, D))
```

```python
from contextlib import ExitStack

import numpy as np

import concourse.bass as bass
from concourse import mybir

F32 = mybir.dt.float32
F32R = mybir.dt.float32r
BF16 = mybir.dt.bfloat16
ACT = mybir.ActivationFunctionType
ALU = mybir.AluOpType
AX_X = mybir.AxisListType.X

P = 128
D = 1024
KT = D // P
SEQ = 512
META = 16
TOK = META + SEQ
HALF = TOK // 2
HD = 64
FFT = 22
FFG = [8, 8, 6]
NEG = -1e30
LAM = 0.8 - 0.6 * float(np.exp(-0.3))
PI = float(np.pi)

U_QKVB = 0
U_CU = 16
U_OUT1 = 24
U_FF = 32
U_SSM = 96
U_GLU = 104
U_FFNA = 120
U_PPA = 188
U_GATEA = 190
U_Q = 198
U_KV = 206
U_WO = 222
U_FFNB = 230
U_PPB = 298
U_GATEB = 300
NU = 308


def column_map():
    at, cols = 0, {}
    for name, n in (
        ("norm_mix", 8), ("out_norm", 8), ("norm_mlp", 8), ("final_norm", 8), ("conv_w", 12), ("b_f", 1),
        ("ssm_norm", 8), ("kv_norm", 8), ("attn_norm", 8), ("k_norm", 1), ("q_norm", 1), ("subln", 1),
        ("ffn_norm0", 8), ("ffn_norm1", 8), ("ple_norm0", 8), ("ple_norm1", 8),
        ("ffn_w0", 132), ("ffn_w1", 132), ("ffn_b0", 44), ("ffn_b1", 44),
        ("lam_re", 32), ("lam_im", 32), ("log_dt", 32), ("ssm_d", 32), ("lambdas", 4),
    ):
        cols[name] = at
        at += n
    return cols, at


COL, NCOL = column_map()


class Unit:

    def __init__(self, c, i=0, step=4):
        self.c, self.i, self.step = c, i, step

    def n(self, k=0):
        return self.c + k + self.step * self.i

    def ahead(self, k):
        return Unit(self.c + k, self.i, self.step)

    @property
    def slot(self):
        return self.c % 4

    @property
    def round(self):
        return self.c // 2 + self.step // 2 * self.i


class Count:

    def __init__(self, sem):
        self.sem, self.base, self.i, self.rate = sem, 0, 0, 0

    def did(self, ins):
        ins.then_inc(self.sem, 1)
        self.base += 1
        return self.base + self.rate * self.i

    def loop(self, i, rate, first=0):
        self.i, self.rate, self.entered = i, rate, self.base
        self.base -= rate * first

    def leave(self, trips, first=0):
        got = self.base - self.entered + self.rate * first
        assert got == self.rate, ("rate", got, self.rate)
        self.base = self.entered + self.rate * (trips - first)
        self.i, self.rate = 0, 0


def ge(eng, sem, value):
    if not (isinstance(value, int) and value <= 0):
        eng.wait_ge(sem, value)


def one(t, k):
    return t[:, bass.ds(k, 1), :] if not isinstance(k, int) else t[:, k:k + 1, :]


def program(nc, A, out, stop=99):
    with ExitStack() as ctx:
        build(nc, A, out, ctx, stop)


def build(nc, A, out, ctx, stop):
    def sb(name, shape, dt=F32, c=ctx):
        return c.enter_context(nc.sbuf_tensor(name, shape, dt))

    def sem(name):
        return ctx.enter_context(nc.semaphore(name))

    h = sb("h", [P, KT, TOK])
    with ExitStack() as c:
        a_hi = sb("a_hi", [P, KT, SEQ], F32R, c)
        a_lo = sb("a_lo", [P, KT, SEQ], F32R, c)
    with ExitStack() as c:
        u_t = sb("u_t", [P, 32, P], F32, c)
    sb("region_a", [P, 2 * KT * SEQ])
    sp_ = sb("sp_", [P, 16, 32])
    pw_up = sb("pw_up", [P, 3, 32, 5])
    pw_dn = sb("pw_dn", [P, 2, 32, 4])
    raw = sb("raw", [P, 2, KT * P])
    w_hi = sb("w_hi", [P, 4, KT * P], F32R)
    w_lo = sb("w_lo", [P, 4, KT * P], F32R)
    vecs = sb("vecs", [P, NCOL])
    ones = sb("ones", [P, P])
    ident = sb("ident", [P, P])
    flip_r = sb("flip_r", [P, P], F32R)
    ident_b = sb("ident_b", [P, P], BF16)
    mask_b = sb("mask_b", [P, P], BF16)
    win = sb("win", [P, 64])
    eps5 = sb("eps5", [P, 1])
    eps6 = sb("eps6", [P, 1])
    eps_o = sb("eps_o", [P, 1])
    neg_lam = sb("neg_lam", [P, 1])
    rel = sb("rel", [33, 8])
    rt = sb("rt", [P, TOK])
    rstd = sb("rstd", [P, TOK])
    sq = sb("sq", [P, 2, TOK])
    t0 = sb("t0", [P, 2, TOK])
    t1 = sb("t1", [P, 2, TOK])
    t2 = sb("t2", [P, 2, TOK])
    small = sb("small", [P, 4, 8])

    with ExitStack() as c:
        x_hi = sb("x_hi", [P, KT, TOK], F32R, c)
        x_lo = sb("x_lo", [P, KT, TOK], F32R, c)
    with ExitStack() as c:
        qs = sb("qs", [P, 2, 2, SEQ], F32, c)
        ks = sb("ks", [P, 2, TOK], F32, c)
        vs = sb("vs", [P, 2, TOK], F32, c)
        vp = sb("vp", [P, 2, 4, 2, P], F32, c)
        vm = sb("vm", [META, 2, 2, P], F32, c)
        pt = sb("pt", [P, 2, 4, P], F32, c)
        ptm = sb("ptm", [META, 2, P], F32, c)
    with ExitStack() as c:
        v_b1 = sb("v_b1", [P, 2, 4, 4, 2, 16], F32, c)
        c_p1 = sb("c_p1", [P, 2, 4, 5, 2, 16], F32, c)
        c_p2 = sb("c_p2", [P, 2, 4, 5, 2, 16], F32, c)
        v_l = sb("v_l", [P, 2, 4, P], F32, c)
        t_l = sb("t_l", [P, 4, P], F32, c)
        x_s = sb("x_s", [P, 2, 4, P + 1], F32, c)
    with ExitStack() as c:
        qs2 = sb("qs2", [P, 2, 2, SEQ], F32, c)
        ks2 = sb("ks2", [P, 2, SEQ], F32, c)
        vs2 = sb("vs2", [P, 2, SEQ], F32, c)
        vtok = sb("vtok", [P, 2, 4, P], F32, c)
        pt2 = sb("pt2", [P, 2, 4, P], F32, c)
        b_hi = sb("b_hi", [P, 2, SEQ], F32R, c)
        b_lo = sb("b_lo", [P, 2, SEQ], F32R, c)
    sb("region_x", [P, 2 * KT * TOK])
    with ExitStack() as c:
        qkvb = sb("qkvb", [P, 16, TOK], F32, c)
        aug_q = sb("aug_q", [P, 2, 2, SEQ], F32, c)
        aug_k = sb("aug_k", [P, TOK], F32, c)
        cum8 = sb("cum8", [40, TOK], F32, c)
        spread1 = sb("spread1", [16, KT * P], F32, c)
        wf = sb("wf", [P, KT, 8], F32, c)
        mask = sb("mask", [P, P], F32, c)
        flip = sb("flip", [P, P], F32, c)
        wf_hi = sb("wf_hi", [P, KT, 8], F32R, c)
        wf_lo = sb("wf_lo", [P, KT, 8], F32R, c)

    with ExitStack() as c:
        e_r = sb("e_r", [P, 32, P], F32, c)
        e_i = sb("e_i", [P, 32, P], F32, c)
        c_raw = sb("c_raw", [P, 2, 32, 16], F32, c)
        bb = sb("bb", [P, 2, 32, 16], F32, c)
        with ExitStack() as cc:
            b_in_ = sb("b_in_", [P, 2, 32, 16], F32, cc)
            ctmp = sb("ctmp", [P, 4, SEQ], F32, cc)
        with ExitStack() as cc:
            v_b0 = sb("v_b0", [P, 2, 4, 4, 2, 16], F32, cc)
            c_p0 = sb("c_p0", [P, 2, 4, 5, 2, 16], F32, cc)
            cmp_ = sb("cmp_", [P, 4, 320], F32, cc)
    with ExitStack() as c:
        q2 = sb("q2", [P, 8, SEQ], F32, c)
        k2 = sb("k2", [P, 8, SEQ], F32, c)
        v2 = sb("v2", [P, 8, SEQ], F32, c)
        spread2 = sb("spread2", [16, KT * P], F32, c)
        with ExitStack() as cc:
            b_raw = sb("b_raw", [P, 1, SEQ], F32, cc)
        tab = sb("tab", [8, 640], F32, c)
    with ExitStack() as c:
        pp = sb("pp", [P, 8, SEQ], F32, c)
        p_raw = sb("p_raw", [P, 2, SEQ], F32, c)
        p_hi = sb("p_hi", [P, 2, SEQ], F32R, c)
        p_lo = sb("p_lo", [P, 2, SEQ], F32R, c)
    V_B, C_P = (v_b0, v_b1), (c_p0, c_p1, c_p2)
    onehot = t1.rearrange("p a b -> p (a b)")[0:33, 0:640]
    scratch = nc.dram_tensor("scratch", (8, 640), F32, kind="Internal").ap()

    ps = ctx.enter_context(nc.psum_tensor("ps", [P, 8, SEQ], F32))

    consts_in = sem("consts_in")
    h_in = [sem(f"h_in{k}") for k in range(2)]
    raw_in = [sem(f"raw_in{k}") for k in range(2)]
    hi_ok = sem("hi_ok")
    lo_ok = sem("lo_ok")
    unit_mm = sem("unit_mm")
    unit_ev = sem("unit_ev")
    h_fin = sem("h_fin")
    sq_ok = sem("sq_ok")
    stat_mm = sem("stat_mm")
    xhi_ok = sem("xhi_ok")
    xlo_ok = sem("xlo_ok")
    rt_ok = sem("rt_ok")
    rstd_ok = sem("rstd_ok")
    consts_ok = sem("consts_ok")
    wf_ok = sem("wf_ok")
    wflo_ok = sem("wflo_ok")
    f_mm = sem("f_mm")
    f_act = sem("f_act")
    f_ok = sem("f_ok")
    staged = sem("staged")
    vt_mm = sem("vt_mm")
    vt_ok = sem("vt_ok")
    s_mm = sem("s_mm")
    nb_ok = sem("nb_ok")
    exp_ok = sem("exp_ok")
    nrm_ok = sem("nrm_ok")
    vz_ok = sem("vz_ok")
    qz_ok = sem("qz_ok")
    pt_mm = sem("pt_mm")
    pt_ok = sem("pt_ok")
    pv_mm = sem("pv_mm")
    y_ok = sem("y_ok")
    hn_sq = sem("hn_sq")
    hn_mm = sem("hn_mm")
    hn_rt = sem("hn_rt")
    hn_inv = sem("hn_inv")
    hn_b = sem("hn_b")
    hn_y = sem("hn_y")
    hn_hi = sem("hn_hi")
    hn_lo = sem("hn_lo")
    ay_ok = sem("ay_ok")
    ahi_ok = sem("ahi_ok")
    alo_ok = sem("alo_ok")
    dve_did = sem("dve_did")
    act_did = sem("act_did")
    pool_did = sem("pool_did")
    pool = Count(pool_did)
    dve = Count(dve_did)
    act = Count(act_did)
    ut_a = sem("ut_a")
    ut_p = sem("ut_p")
    par_v = sem("par_v")
    par_a = sem("par_a")
    bc_in = sem("bc_in")
    den_ok = sem("den_ok")
    inv_ok = sem("inv_ok")
    dt_ok = sem("dt_ok")
    pads_ok = sem("pads_ok")
    tables_ok = sem("tables_ok")
    vb_ok = sem("vb_ok")
    cp_ok = sem("cp_ok")
    vb_mm = sem("vb_mm")
    g_mm = sem("g_mm")
    vl_ok = sem("vl_ok")
    tl_ok = sem("tl_ok")
    v_mm = sem("v_mm")
    v_ev = sem("v_ev")
    xs_ok = sem("xs_ok")
    y_mm = sem("y_mm")
    ys_ok = sem("ys_ok")
    ge_ok = sem("ge_ok")
    g_hi = sem("g_hi")
    g_lo = sem("g_lo")
    sig_ok = sem("sig_ok")
    c0_ok = sem("c0_ok")
    cg_ok = sem("cg_ok")
    gel_ok = sem("gel_ok")
    p_in = sem("p_in")
    phi_ok = sem("phi_ok")
    plo_ok = sem("plo_ok")
    tab_in = sem("tab_in")
    tab_mm = sem("tab_mm")
    tab_ok = sem("tab_ok")
    tab_out = sem("tab_out")
    b_in = sem("b_in")
    bhi_ok = sem("bhi_ok")
    blo_ok = sem("blo_ok")
    lam_v = sem("lam_v")
    lam_mm = sem("lam_mm")
    lam_a = sem("lam_a")
    v2_ok = sem("v2_ok")
    zz_ok = sem("zz_ok")
    cv_ok = sem("cv_ok")
    sg_ok = sem("sg_ok")
    sgu_ok = sem("sgu_ok")
    o_ok = sem("o_ok")
    fence_at = sem("fence_at")
    stored = sem("stored")

    REAL = slice(META, TOK)
    NLOAD = {1: U_SSM, 2: U_FFNA, 4: U_Q + 2, 5: U_FFNB + 2}.get(stop, NU)

    def vec(name, k=0, lo=0, n=P):
        k = COL[name] + k
        return vecs[lo:lo + n, k:k + 1] if isinstance(k, int) else vecs[lo:lo + n, bass.ds(k, 1)]

    def halves(t):
        return t.rearrange("p (a b) -> p a b", a=2)

    def fence(e, k):
        e.drain().then_inc(fence_at, 1)
        e.wait_ge(fence_at, 4 * k)

    def load_unit(e, u):
        if not (isinstance(u.i, int) and u.n() < 2):
            e.wait_ge(lo_ok, u.n(-1))
        n = u.n()
        src = A["wstream"][bass.ds(n * P, P), :] if not isinstance(n, int) else A["wstream"][n * P:n * P + P, :]
        e.dma_start(raw[:, u.c % 2, :], src).then_inc(raw_in[u.c % 2], 16)

    def split_hi(e, u):
        e.wait_ge(raw_in[u.c % 2], 16 * (u.round + 1))
        if not (isinstance(u.i, int) and u.n() < 4):
            e.wait_ge(unit_mm, u.n(-3))
        e.activation(w_hi[:, u.slot, :], raw[:, u.c % 2, :], ACT.Copy).then_inc(hi_ok, 1)

    def split_lo(e, u):
        e.wait_ge(hi_ok, u.n(1))
        e.tensor_tensor(w_lo[:, u.slot, :], raw[:, u.c % 2, :], w_hi[:, u.slot, :], ALU.subtract)\
            .then_inc(lo_ok, 1)

    def split_ahead(e, u, split):
        if not (isinstance(u.i, int) and u.n() + 2 >= NLOAD):
            split(e, u.ahead(2))

    def products(e, u, bank, hi, lo, k0=0, kt=KT, w0=0, ready=None):
        for k in range(kt):
            w = slice((w0 + k) * P, (w0 + k + 1) * P)
            if ready:
                ready(e, k)
            for n, (wt, x) in enumerate(((w_hi, hi), (w_hi, lo), (w_lo, hi))):
                last = e.matmul(ps[:, bank, :], wt[:, u.slot, w], x[:, k0 + k, 0:SEQ],
                                start=(k == 0 and n == 0), stop=(k == kt - 1 and n == 2))
        return last

    def unit_pe(e, u, hi, lo, ready=None, kt=KT):
        e.wait_ge(lo_ok, u.n(1))
        e.wait_ge(unit_ev, u.n(-3))
        products(e, u, u.slot, hi, lo, kt=kt, ready=ready).then_inc(unit_mm, 1)

    XN = {0: 0, 1: 1, 3: 2, 4: 3, 5: 4, 6: 5, 7: 7, 8: 8}

    def stat_pe(e, n, m, cols=SEQ):
        e.wait_ge(sq_ok, 8 * n + m + 1)
        if n and m == 0:
            e.wait_ge(rt_ok, n)
        for half in range(2 if cols > SEQ else 1):
            w = HALF if cols > SEQ else SEQ
            last = e.matmul(ps[:, 4 + half, 0:w], ones[:, :], sq[:, m % 2, half * HALF:half * HALF + w],
                            start=(m == 0), stop=(m == KT - 1))
        last.then_inc(stat_mm, 1)

    def norm_act(e, n, m, gain, cols=SEQ, x_hi=x_hi):
        src = h[:, m, TOK - cols:TOK]
        if 8 * n + m >= 2:
            e.wait_ge(stat_mm, 8 * n + m - 1)
        e.activation(sq[:, m % 2, 0:cols], src, ACT.Square).then_inc(sq_ok, 1)
        if gain:
            x_act(e, n, m, gain, cols)

    def x_act(e, n, m, gain, cols=SEQ, hi=x_hi):
        src = h[:, m, TOK - cols:TOK]
        e.activation(hi[:, m, 0:cols], src, ACT.Copy, scale=vec(gain, m)).then_inc(xhi_ok, 1)

    def x_dve(e, xn, m, gain, cols=SEQ, hi=x_hi, lo=x_lo):
        src = h[:, m, TOK - cols:TOK]
        e.wait_ge(xhi_ok, 8 * xn + m + 1)
        e.scalar_tensor_tensor(lo[:, m, 0:cols], src, vec(gain, m), hi[:, m, 0:cols], ALU.mult,
                               ALU.subtract).then_inc(xlo_ok, 1)

    def root_act(e, n, eps, cols=SEQ):
        e.wait_ge(stat_mm, 8 * (n + 1))
        if n:
            e.wait_ge(rstd_ok, n)
        if cols > SEQ:
            o, i = halves(rt[:, :]), ps[:, 4:6, 0:HALF]
        else:
            o, i = rt[:, 0:cols], ps[:, 4, 0:cols]
        e.activation(o, i, ACT.Sqrt, bias=eps[:, 0:1], scale=1.0 / D).then_inc(rt_ok, 1)

    def root_dve(e, n, cols=SEQ):
        e.wait_ge(rt_ok, n + 1)
        e.reciprocal(rstd[:, 0:cols], rt[:, 0:cols]).then_inc(rstd_ok, 1)
        e.wait_ge(rstd_ok, n + 1)

    roots = t2[0:16, 0, 0:SEQ]

    def head_sq(e, k, y):
        if k >= 2:
            e.wait_ge(hn_mm, k - 1)
        e.activation(sq[:, k % 2, 0:SEQ], y, ACT.Square).then_inc(hn_sq, 1)

    def head_pe(e, k, w=0):
        m = k % 8
        e.wait_ge(hn_sq, k + 1)
        if m == 0:
            ge(e, hn_rt, k // 8)
        e.matmul(ps[0:16, 5, :], win[:, 32 * w + 15 - 2 * m:32 * w + 31 - 2 * m], sq[:, k % 2, 0:SEQ],
                 start=(m == 0), stop=(m == 7)).then_inc(hn_mm, 1)

    def head_root(e, b, n, eps):
        e.wait_ge(hn_mm, 8 * b + 8)
        ge(e, hn_b, 8 * b)
        e.activation(roots, ps[0:16, 5, :], ACT.Sqrt, bias=eps[0:16, 0:1], scale=1.0 / n).then_inc(hn_rt, 1)

    def head_inverse(e, b):
        e.wait_ge(hn_rt, b + 1)
        e.reciprocal(roots, roots).then_inc(hn_inv, 1)

    def head_spread(e, k):
        m = k % 8
        e.wait_ge(hn_inv, k // 8 + 1)
        ge(e, hn_y, k - 1)
        e.matmul(ps[:, 6 + k % 2, :], (spread1 if k < 8 else spread2)[:, m * P:(m + 1) * P],
                 roots, start=True, stop=True).then_inc(hn_b, 1)

    def head_scale(e, k, y, gain, to=None):
        e.wait_ge(hn_b, k + 1)
        if to is None and k >= 2:
            e.wait_ge(hn_lo, HNX(k) - 1)
        to = t0[:, k % 2, 0:SEQ] if to is None else to
        e.scalar_tensor_tensor(to, y, gain, ps[:, 6 + k % 2, :], ALU.mult, ALU.mult).then_inc(hn_y, 1)

    def HNX(k):
        return k if k < 8 else k - 16

    def head_hi(e, k, m):
        e.wait_ge(hn_y, k + 1)
        e.activation(a_hi[:, m, :], t0[:, k % 2, 0:SEQ], ACT.Copy).then_inc(hn_hi, 1)

    def head_lo(e, k, m):
        e.wait_ge(hn_hi, HNX(k) + 1)
        e.wait_ge(hn_y, k + 1)
        e.tensor_tensor(a_lo[:, m, :], t0[:, k % 2, 0:SEQ], a_hi[:, m, :], ALU.subtract).then_inc(hn_lo, 1)

    def wide_pe(e, u):
        e.wait_ge(lo_ok, u.n(1))
        if not (isinstance(u.i, int) and u.n() < 2):
            e.wait_ge(unit_ev, u.n(-1))
        b = 2 * (u.slot % 2)
        for k in range(KT):
            w = slice(k * P, (k + 1) * P)
            if isinstance(u.i, int) and u.n() == 0:
                e.wait_ge(xlo_ok, k + 1)
            for n, (wt, x) in enumerate(((w_hi, x_hi), (w_hi, x_lo), (w_lo, x_hi))):
                for half in range(2):
                    last = e.matmul(ps[:, b + half, 0:HALF], wt[:, u.slot, w],
                                    x[:, k, half * HALF:(half + 1) * HALF],
                                    start=(k == 0 and n == 0), stop=(k == KT - 1 and n == 2))
        last.then_inc(unit_mm, 1)

    def wide_dve(e, u, to):
        e.wait_ge(unit_mm, u.n(1))
        b = 2 * (u.slot % 2)
        e.tensor_tensor(halves(to), ps[:, b:b + 2, 0:HALF], halves(rstd[:, :]), ALU.mult).then_inc(unit_ev, 1)

    def f_pe(e):
        e.wait_ge(wflo_ok, 1)
        for k in range(KT):
            for n, (wt, x) in enumerate(((wf_hi, x_hi), (wf_hi, x_lo), (wf_lo, x_hi))):
                for half in range(2):
                    last = e.matmul(ps[0:8, 6 + half, 0:HALF], wt[:, k, :], x[:, k, half * HALF:(half + 1) * HALF],
                                    start=(k == 0 and n == 0), stop=(k == KT - 1 and n == 2))
        last.then_inc(f_mm, 1)

    def f_dve(e):
        z, az, ls = t0[0:8, 0, :], t0[0:8, 1, :], t1[0:8, 0, :]
        e.wait_ge(f_mm, 1)
        n = dve.did(e.tensor_tensor(halves(az), ps[0:8, 6:8, 0:HALF], halves(rstd[0:8, :]), ALU.mult))
        e.wait_ge(dve_did, n)
        e.tensor_scalar(z, az, vec("b_f", 0, 0, 8), None, ALU.add).then_inc(f_ok, 1)
        e.wait_ge(f_act, 1)
        n = dve.did(e.scalar_tensor_tensor(ls, z, 0.0, t1[0:8, 1, :], ALU.min, ALU.subtract))
        e.wait_ge(dve_did, n)
        e.wait_ge(consts_ok, 1)
        n = dve.did(e.tensor_tensor_scan(cum8[0:8, :], t2[0:8, 0, :], ls, 0.0, ALU.mult, ALU.add))
        e.wait_ge(dve_did, n)
        e.tensor_scalar(aug_k[0:8, :], cum8[0:8, :], -8.0, None, ALU.mult).then_inc(f_ok, 1)
        e.tensor_scalar(cum8[32:40, :], cum8[0:8, :], 8.0, None, ALU.mult).then_inc(f_ok, 1)

    def f_scalar(e):
        e.wait_ge(f_ok, 1)
        n = act.did(e.activation(t0[0:8, 1, :], t0[0:8, 0, :], ACT.Abs))
        e.wait_ge(act_did, n)
        n = act.did(e.activation(t1[0:8, 0, :], t0[0:8, 1, :], ACT.Exp, scale=-1.0))
        e.wait_ge(act_did, n)
        e.activation(t1[0:8, 1, :], t1[0:8, 0, :], ACT.Ln, bias=1.0).then_inc(f_act, 1)

    def conv_dve(e, u, s):
        k = s // 2
        if s % 2 == 0:
            wide_dve(e, u, t0[:, k, :])
            return
        wide_dve(e, u, t1[:, k, :])
        j = 2 * u.i + k
        e.wait_ge(unit_ev, u.n(1))
        n = dve.did(e.tensor_tensor(t2[:, k, :], t0[:, k, :], t1[:, k, :], ALU.mult))
        e.wait_ge(dve_did, n)
        n = dve.did(e.tensor_scalar(t0[:, k, 0:SEQ], t2[:, k, 16:528], vec("conv_w", 8 + j), None, ALU.mult))
        e.wait_ge(dve_did, n)
        n = dve.did(e.scalar_tensor_tensor(t1[:, k, 0:SEQ], t2[:, k, 15:527], vec("conv_w", 4 + j),
                                           t0[:, k, 0:SEQ], ALU.mult, ALU.add))
        e.wait_ge(dve_did, n)
        n = dve.did(e.scalar_tensor_tensor(t0[:, k, 0:SEQ], t2[:, k, 14:526], vec("conv_w", j),
                                           t1[:, k, 0:SEQ], ALU.mult, ALU.add))
        e.wait_ge(dve_did, n)
        b = qkvb[:, bass.ds(12 + j, 1), REAL] if not isinstance(j, int) else qkvb[:, 12 + j:13 + j, REAL]
        n = dve.did(e.tensor_tensor(b, b, t0[:, k:k + 1, 0:SEQ], ALU.mult))

    def tile_of(t, k, cols=slice(None), rows=slice(None)):
        return t[rows, k:k + 1, cols] if isinstance(k, int) else t[rows, bass.ds(k, 1), cols]

    def stage1_pool(e, i):
        for par in range(2):
            p = 2 * i + par
            if not (isinstance(i, int) and i == 0):
                e.wait_ge(y_ok, 2 * i + par - 1)
            k = 8 * p
            for hh in range(2):
                r = slice(HD * hh, HD * hh + HD)
                ge(e, staged, k + hh)
                e.tensor_copy(qs[r, par, hh:hh + 1, :], tile_of(qkvb, p, REAL, r)).then_inc(staged, 1)
            e.wait_ge(staged, k + 2)
            e.tensor_copy(ks[:, par:par + 1, :], tile_of(qkvb, 4 + p)).then_inc(staged, 1)
            e.wait_ge(staged, k + 3)
            e.tensor_copy(vs[:, par:par + 1, :], tile_of(qkvb, 8 + p)).then_inc(staged, 1)
            for hh in range(2):
                hd = 2 * p + hh
                pick = lambda lo, c: (ident[lo:lo + 8, c:c + 1] if isinstance(c, int)
                                      else ident[lo:lo + 8, bass.ds(c, 1)]).to_broadcast([8, SEQ])
                e.wait_ge(staged, k + 4 + 2 * hh)
                e.tensor_copy(aug_q[0:8, par, hh, :], pick(0, hd)).then_inc(staged, 1)
                e.wait_ge(staged, k + 5 + 2 * hh)
                e.tensor_tensor(aug_q[32:40, par, hh, :], cum8[32:40, REAL], pick(32, 32 + hd), ALU.mult)\
                    .then_inc(staged, 1)

    def values_pe(e, i, par):
        p = 2 * i + par
        e.wait_ge(staged, 8 * p + 8)
        for j in range(4):
            e.transpose(ps[:, 4 + par, j * P:(j + 1) * P], vs[:, par, META + j * P:META + (j + 1) * P], ident[:, :])
        e.transpose(ps[0:META, 6 + par, 0:P], vs[:, par, 0:META], ident[:, :]).then_inc(vt_mm, 1)

    def values_act(e, i, par):
        p = 2 * i + par
        e.wait_ge(vt_mm, p + 1)
        e.wait_ge(vz_ok, 1)
        t = ps[:, 4 + par, :].rearrange("p (j c) -> p j c", j=4)
        for hh in range(2):
            c = slice(HD * hh, HD * hh + HD)
            e.activation(vp[:, par, :, hh, c], t[:, :, c], ACT.Copy).then_inc(vt_ok, 1)
            e.activation(vm[:, par, hh, c], ps[0:META, 6 + par, c], ACT.Copy).then_inc(vt_ok, 1)

    def scores1_pe(e, i, par, w):
        qt, hh, sl = w // 2, w % 2, w % 2
        g = 8 * (2 * i + par) + w
        ge(e, exp_ok, g - 1)
        ge(e, pt_ok, 2 * (g - 1))
        A_, B = 2 * sl, 2 * sl + 1
        q = qs[:, par, hh, qt * P:(qt + 1) * P]
        aq = aug_q[:, par, hh, qt * P:(qt + 1) * P]
        N = (qt + 1) * P
        e.matmul(ps[:, A_, SEQ - META:SEQ], q, ks[:, par, 0:META], start=True, stop=False)
        e.matmul(ps[:, A_, SEQ - META:SEQ], aq, aug_k[:, 0:META], start=False, stop=True)
        e.matmul(ps[:, B, 0:N], q, ks[:, par, META:META + N], start=True, stop=False)
        e.matmul(ps[:, B, 0:N], aq, aug_k[:, META:META + N], start=False, stop=False)
        e.matmul(ps[:, B, N - P:N], ident_b[:, :], mask_b[:, :], start=False, stop=True).then_inc(s_mm, 1)

    def turn1_pe(e, i, par, w):
        qt, sl = w // 2, w % 2
        g = 8 * (2 * i + par) + w
        e.wait_ge(nrm_ok, g + 1)
        for j in range(qt + 1):
            e.transpose(ps[:, 4 + sl, j * P:(j + 1) * P], t0[:, sl, META + j * P:META + (j + 1) * P], ident[:, :])
        e.transpose(ps[0:META, 2 * sl, 0:P], t0[:, sl, 0:META], ident[:, :]).then_inc(pt_mm, 1)

    def pv1_pe(e, i, par, w):
        qt, hh, sl = w // 2, w % 2, w % 2
        g = 8 * (2 * i + par) + w
        e.wait_ge(pt_ok, 2 * (g + 1))
        if w == 0:
            e.wait_ge(vt_ok, 4 * (2 * i + par) + 4)
        o = ps[:, 6 + par, qt * P:(qt + 1) * P]
        for j in range(qt + 1):
            e.matmul(o, vp[:, par, j, hh, :], pt[:, sl, j, :], start=(hh == 0 and j == 0), stop=False)
        e.matmul(o, vm[:, par, hh, :], ptm[:, sl, :], start=False, stop=(hh == 1)).then_inc(pv_mm, 1)

    def attention1_pe(e, i):
        for par in range(2):
            values_pe(e, i, par)
            for w in range(8 + 2):
                if w < 8:
                    scores1_pe(e, i, par, w)
                if 1 <= w < 9:
                    turn1_pe(e, i, par, w - 1)
                if w >= 2:
                    pv1_pe(e, i, par, w - 2)

    def scores_flat(sl):
        return ps[:, 2 * sl:2 * sl + 2, :].rearrange("p a b -> p (a b)")

    def attention1_dve(e, i):
        def top(par, w):
            qt, sl = w // 2, w % 2
            g = 8 * (2 * i + par) + w
            e.wait_ge(s_mm, g + 1)
            s = scores_flat(sl)[:, SEQ - META:SEQ + (qt + 1) * P]
            n = dve.did(e.reduce_max(small[:, 0, sl:sl + 1], s, AX_X))
            e.wait_ge(dve_did, n)
            e.tensor_scalar(small[:, 1, sl:sl + 1], small[:, 0, sl:sl + 1], -0.125, None, ALU.mult)\
                .then_inc(nb_ok, 1)

        def normalise(par, w):
            qt, sl = w // 2, w % 2
            g = 8 * (2 * i + par) + w
            N = META + (qt + 1) * P
            e.wait_ge(exp_ok, g + 1)
            n = dve.did(e.reciprocal(small[:, 3, sl:sl + 1], small[:, 2, sl:sl + 1]))
            e.wait_ge(dve_did, n)
            e.tensor_scalar(t0[:, sl, 0:N], t0[:, sl, 0:N], small[:, 3, sl:sl + 1], None, ALU.mult)\
                .then_inc(nrm_ok, 1)

        for par in range(2):
            for w in range(8 + 1):
                if w >= 1:
                    normalise(par, w - 1)
                if w < 8:
                    top(par, w)
            p = 2 * i + par
            e.wait_ge(pv_mm, 8 * p + 8)
            e.tensor_copy(tile_of(qkvb, p, REAL), ps[:, 6 + par:7 + par, :]).then_inc(y_ok, 1)

    def attention1_act(e, i):
        def exps(par, w):
            qt, sl = w // 2, w % 2
            g = 8 * (2 * i + par) + w
            e.wait_ge(nb_ok, g + 1)
            ge(e, pt_mm, g - 1)
            ge(e, nrm_ok, g - 1)
            N = META + (qt + 1) * P
            e.activation(t0[:, sl, 0:N], scores_flat(sl)[:, SEQ - META:SEQ + (qt + 1) * P], ACT.Exp,
                         bias=small[:, 1, sl:sl + 1], scale=0.125,
                         accum_out=small[:, 2, sl:sl + 1]).then_inc(exp_ok, 1)

        def turned(par, w):
            qt, sl = w // 2, w % 2
            g = 8 * (2 * i + par) + w
            N = (qt + 1) * P
            e.wait_ge(pt_mm, g + 1)
            ge(e, pv_mm, g - 1)
            e.activation(pt[:, sl, 0:qt + 1, :].rearrange("p j c -> p (j c)"), ps[:, 4 + sl, 0:N], ACT.Copy)\
                .then_inc(pt_ok, 1)
            e.activation(ptm[:, sl, :], ps[0:META, 2 * sl, 0:P], ACT.Copy).then_inc(pt_ok, 1)

        for par in range(2):
            values_act(e, i, par)
            for w in range(8 + 1):
                if w < 8:
                    exps(par, w)
                if w >= 1:
                    turned(par, w - 1)

    def y_tile(m):
        return qkvb[:, m if m < 4 else m + 8, REAL]

    def relu2_dve(e, u, s):
        e.wait_ge(unit_mm, u.n(1))
        k = s % 2
        e.tensor_tensor(t0[:, k, 0:SEQ], ps[:, u.slot, :], rstd[:, 0:SEQ], ALU.mult).then_inc(unit_ev, 1)
        ge(e, alo_ok, 8 * u.i + s - 1)
        e.wait_ge(unit_ev, u.n(1))
        e.scalar_tensor_tensor(t1[:, k, 0:SEQ], t0[:, k, 0:SEQ], 0.0, t0[:, k, 0:SEQ], ALU.max, ALU.mult)\
            .then_inc(ay_ok, 1)

    def hidden_hi(e, n, m):
        e.wait_ge(ay_ok, n + 1)
        e.activation(a_hi[:, m, :], t1[:, m % 2, 0:SEQ], ACT.Copy).then_inc(ahi_ok, 1)

    def hidden_lo(e, n, m):
        e.wait_ge(ahi_ok, n + 1)
        e.tensor_tensor(a_lo[:, m, :], t1[:, m % 2, 0:SEQ], a_hi[:, m, :], ALU.subtract).then_inc(alo_ok, 1)

    def add_dve(e, u, m, final=False):
        e.wait_ge(unit_mm, u.n(1))
        e.wait_ge(unit_ev, u.n())
        i = e.tensor_tensor(h[:, m, REAL], h[:, m, REAL], ps[:, u.slot, :], ALU.add)
        i.then_inc(unit_ev, 1)


    def units(e, u0, trips, body, first=0, cycle=4, counts=None, rate=0):
        for i in range(first):
            for s in range(cycle):
                body(Unit(u0 + s, i, cycle), s)
        if trips > first:
            with e.Fori(first, trips) as i:
                if counts:
                    counts.loop(i, rate, first)
                for s in range(cycle):
                    body(Unit(u0 + s, i, cycle), s)
            if counts:
                counts.leave(trips, first)

    def spread_u(e, u, m, q, j, who):
        src = t0[32 * q:32 * q + 32, m % 2 if isinstance(m, int) else u.slot % 2, 0:SEQ]
        src = src.rearrange("p (c j) -> p j c", j=4)[:, j:j + 1, :]
        k = 4 * m + q
        dst = u_t[32 * j:32 * j + 32, bass.ds(k, 1), :] if not isinstance(k, int) else u_t[32 * j:32 * j + 32, k:k + 1, :]
        return (e.activation(dst, src, ACT.Copy) if who == "a" else e.tensor_copy(dst, src))

    def cmul(e, n, out_r, out_i, a, b, tmp, sign=1):
        ar, ai = a
        br, bi = b
        ta, tb, tc, td = tmp
        n.did(e.tensor_tensor(ta, ar, br, ALU.mult))
        n.did(e.tensor_tensor(tb, ai, bi, ALU.mult))
        n.did(e.tensor_tensor(tc, ar, bi, ALU.mult))
        k = n.did(e.tensor_tensor(td, ai, br, ALU.mult))
        e.wait_ge(n.sem, k)
        n.did(e.tensor_tensor(out_r, ta, tb, ALU.subtract if sign > 0 else ALU.add))
        k = n.did(e.tensor_tensor(out_i, tc, td, ALU.add if sign > 0 else ALU.subtract))
        e.wait_ge(n.sem, k)

    S = lambda k: sp_[:, k, :]
    T4 = lambda w: [t[:, s, 0:w] for t in (t0, t1) for s in range(2)]
    V_DT, V_MAG, V_TH, V_K, V_R, V_SH, V_SIN, V_COS, V_AR, V_AI, V_FR, V_FI, V_M4, V_T, V_W, V_Z = range(16)

    def system_dve(e):
        e.wait_ge(den_ok, 1)
        e.reciprocal(S(V_Z), S(V_T)).then_inc(inv_ok, 1)

    def system_pool(e):
        lr = vecs[:, COL["lam_re"]:COL["lam_re"] + 32]
        li = vecs[:, COL["lam_im"]:COL["lam_im"] + 32]

        def do(ins):
            e.wait_ge(pool_did, pool.did(ins))

        tt = lambda o, a, b, op: do(e.tensor_tensor(o, a, b, op))
        ts = lambda o, a, x, y, op0, op1: do(e.tensor_scalar(o, a, x, y, op0, op1))
        e.wait_ge(consts_in, 16 * 9)
        e.wait_ge(consts_ok, 6)
        tt(S(V_T), lr, lr, ALU.mult)
        tt(S(V_W), li, li, ALU.mult)
        e.tensor_tensor(S(V_T), S(V_T), S(V_W), ALU.add).then_inc(den_ok, 1)
        e.wait_ge(dt_ok, 1)
        e.tensor_tensor(S(V_SH), lr, S(V_DT), ALU.mult).then_inc(par_v, 1)
        tt(S(V_TH), li, S(V_DT), ALU.mult)
        magic = 1.5 * 2.0 ** 23
        ts(S(V_K), S(V_TH), 1.0 / (2 * PI), magic, ALU.mult, ALU.add)
        ts(S(V_K), S(V_K), magic, None, ALU.subtract, ALU.bypass)
        c1 = 6.28125
        c2 = float((np.float32(2 * np.pi - c1).view(np.uint32) & np.uint32(0xFFFFF000)).view(np.float32))
        c3 = float(np.float32(2 * np.pi - c1 - c2))
        do(e.tensor_copy(S(V_R), S(V_TH)))
        for c in (c1, c2, c3):
            ts(S(V_W), S(V_K), -c, None, ALU.mult, ALU.bypass)
            tt(S(V_R), S(V_R), S(V_W), ALU.add)
        lim = float(np.nextafter(np.float32(np.pi), np.float32(0)))
        e.tensor_scalar(S(V_R), S(V_R), lim, -lim, ALU.min, ALU.max).then_inc(par_v, 1)
        e.wait_ge(par_a, 3)
        tt(S(V_COS), S(V_COS), S(V_COS), ALU.mult)
        ts(S(V_COS), S(V_COS), -2.0, 1.0, ALU.mult, ALU.add)
        tt(S(V_AR), S(V_MAG), S(V_COS), ALU.mult)
        tt(S(V_AI), S(V_MAG), S(V_SIN), ALU.mult)
        e.wait_ge(inv_ok, 1)
        ts(S(V_W), S(V_AR), -1.0, None, ALU.add, ALU.bypass)
        tt(S(V_FR), S(V_W), lr, ALU.mult)
        tt(S(V_T), S(V_AI), li, ALU.mult)
        tt(S(V_FR), S(V_FR), S(V_T), ALU.add)
        tt(S(V_FR), S(V_FR), S(V_Z), ALU.mult)
        tt(S(V_FI), S(V_AI), lr, ALU.mult)
        tt(S(V_T), S(V_W), li, ALU.mult)
        tt(S(V_FI), S(V_FI), S(V_T), ALU.subtract)
        tt(S(V_FI), S(V_FI), S(V_Z), ALU.mult)
        tt(S(V_T), S(V_MAG), S(V_MAG), ALU.mult)
        tt(S(V_M4), S(V_T), S(V_T), ALU.mult)
        up = lambda k, n: pw_up[:, k, :, n]
        do(e.memset(up(0, 0), 1.0))
        do(e.memset(up(1, 0), 0.0))
        do(e.tensor_copy(up(0, 1), S(V_AR)))
        do(e.tensor_copy(up(1, 1), S(V_AI)))
        small4 = [S(k) for k in (V_TH, V_K, V_R, V_SH)]
        for n, (a, b) in {2: (1, 1), 3: (2, 1), 4: (2, 2)}.items():
            cmul(e, pool, up(0, n), up(1, n), (up(0, a), up(1, a)), (up(0, b), up(1, b)), small4)
        ts(pw_up[:, 2, :, :], pw_up[:, 1, :, :], -1.0, None, ALU.mult, ALU.bypass)
        for j in range(4):
            do(e.tensor_copy(pw_dn[:, :, :, j], pw_up[:, 0:2, :, 3 - j]))

    def tables_pool(e):
        small4 = [S(k) for k in (V_TH, V_K, V_R, V_SH)]

        def do(ins):
            e.wait_ge(pool_did, pool.did(ins))

        e.wait_ge(bc_in, 32)
        bc = lambda k: S(k).unsqueeze(2).to_broadcast([P, 32, 16])
        cmul(e, pool, bb[:, 0, :, :], bb[:, 1, :, :], (bc(V_FR), bc(V_FI)), (b_in_[:, 0, :, :], b_in_[:, 1, :, :]),
             [ctmp[:, k, :].rearrange("p (q c) -> p q c", c=16) for k in range(4)])

        def square():
            c, i = S(V_COS), S(V_SIN)
            cmul(e, pool, S(V_T), S(V_W), (c, i), (c, i), small4)
            unit_length(e, S(V_T), S(V_W), S(V_Z), S(V_K))
            do(e.tensor_copy(c, S(V_T)))
            do(e.tensor_copy(i, S(V_W)))

        square()
        square()
        do(e.memset(e_r[:, :, 0:1], 1.0))
        do(e.memset(e_i[:, :, 0:1], 0.0))
        n = 1
        while n < P:
            per = min(32, SEQ // n)
            for q in range(0, 32, per):
                w = [ctmp[:, k, 0:per * n].rearrange("p (q c) -> p q c", c=n) for k in range(4)]
                b = [S(k)[:, q:q + per].unsqueeze(2).to_broadcast([P, per, n]) for k in (V_COS, V_SIN)]
                cmul(e, pool, e_r[:, q:q + per, n:2 * n], e_i[:, q:q + per, n:2 * n],
                     (e_r[:, q:q + per, 0:n], e_i[:, q:q + per, 0:n]), b, w)
            n *= 2
            if n < P:
                square()
        e.memset(v_b0[:, :, :, :, :, :], 0.0).then_inc(pads_ok, 1)
        e.memset(c_p0[:, :, :, :, :, :], 0.0).then_inc(pads_ok, 1)
        e.wait_ge(pads_ok, 2)

    def unit_length(e, r, i, s, w):
        def do(ins):
            e.wait_ge(pool_did, pool.did(ins))
        do(e.tensor_tensor(s, r, r, ALU.mult))
        do(e.tensor_tensor(w, i, i, ALU.mult))
        do(e.tensor_tensor(s, s, w, ALU.add))
        do(e.tensor_scalar(s, s, -0.5, 1.5, ALU.mult, ALU.add))
        do(e.tensor_tensor(r, r, s, ALU.mult))
        do(e.tensor_tensor(i, i, s, ALU.mult))

    def matrices_pool(e, m):
        b = m % 2
        pr_ = slice(4 * m, 4 * m + 4)
        ge(e, g_mm, m - 1)
        ge(e, y_mm, m - 2)
        for dst, src, pw, n, done in ((V_B[b], bb, pw_dn, 4, vb_ok), (C_P[m % 3], c_raw, pw_up, 5, cp_ok)):
            w = [cmp_[:, k, 0:64 * n].rearrange("p (q j c) -> p q j c", q=4, j=n) for k in range(4)]
            x = [src[:, k, pr_, :].unsqueeze(2).to_broadcast([P, 4, n, 16]) for k in range(2)]
            y = [pw[:, k, pr_, :].unsqueeze(3).to_broadcast([P, 4, n, 16]) for k in range(3 if n == 5 else 2)]
            im = 2 if n == 5 else 1

            def do(ins):
                e.wait_ge(pool_did, pool.did(ins))

            do(e.tensor_tensor(w[0], x[0], y[0], ALU.mult))
            do(e.tensor_tensor(w[1], x[1], y[1], ALU.mult))
            do(e.tensor_tensor(w[2], x[0], y[im], ALU.mult))
            do(e.tensor_tensor(w[3], x[1], y[0], ALU.mult))
            for g in range(2):
                r = slice(HD * g, HD * g + HD)
                do(e.tensor_tensor(dst[r, 0, :, :, g, :], w[0][r], w[1][r], ALU.subtract))
                do(e.tensor_tensor(dst[r, 1, :, :, g, :], w[2][r], w[3][r],
                                   ALU.subtract if n == 5 else ALU.add))
            e.drain().then_inc(done, 1)

    VB = ((0, 1), (3, 7))

    def mixer_front_pe(e, m):
        b = m % 2
        e.wait_ge(vb_ok, m + 1)
        ge(e, vl_ok, 2 * m)
        for k in range(2):
            for q in range(4):
                last = e.transpose(ps[:, 4 + k, q * P:(q + 1) * P],
                                   V_B[b][:, k, q, :, :, :].rearrange("p j g c -> p (j g c)"), ident[:, :])
        last.then_inc(vb_mm, 1)
        e.wait_ge(cp_ok, m + 1)
        ge(e, tl_ok, 4 * m)
        for q in range(4):
            for k in range(2):
                last = e.matmul(ps[0:32, 6, q * P:(q + 1) * P], V_B[b][:, k, q, 3, :, :].rearrange("p g c -> p (g c)"),
                                C_P[m % 3][:, k, q, 0:4, :, :].rearrange("p j g c -> p (j g c)"),
                                start=(k == 0), stop=(k == 1))
        last.then_inc(g_mm, 1)
        e.wait_ge(vl_ok, 2 * m + 2)
        ge(e, v_ev, m - 1)
        for k in range(2):
            for q in range(4):
                last = e.matmul(ps[:, VB[m % 2][k], q * P:(q + 1) * P], v_l[:, k, q, :], u_t[:, 4 * m + q, :],
                                start=True, stop=True)
        last.then_inc(v_mm, 1)

    def mixer_back_pe(e, m):
        b = m % 2
        e.wait_ge(tl_ok, 4 * m + 4)
        e.wait_ge(xs_ok, m + 1)
        ge(e, ys_ok, 4 * m)
        for q in range(4):
            o = ps[:, 2, q * P:(q + 1) * P]
            e.matmul(o, t_l[:, q, :], u_t[:, 4 * m + q, :], start=True, stop=False)
            for k in range(2):
                last = e.matmul(o, C_P[m % 3][:, k, q, 1:5, :, :].rearrange("p j g c -> p (j g c)"),
                                x_s[:, k, q, 0:P], start=False, stop=(k == 1))
        last.then_inc(y_mm, 1)

    def mixer_front_act(e, m):
        e.wait_ge(vb_mm, m + 1)
        ge(e, v_mm, m)
        for k in range(2):
            e.activation(v_l[:, k, :, :].rearrange("p q c -> p (q c)"), ps[:, 4 + k, :], ACT.Copy).then_inc(vl_ok, 1)
        e.wait_ge(g_mm, m + 1)
        ge(e, y_mm, m)
        g = ps[0:32, 6, :].rearrange("p (q c) -> p q c", q=4)
        for j in range(4):
            e.activation(t_l[32 * j:32 * j + 32, :, 32 * j:P], g[:, :, 0:P - 32 * j], ACT.Copy).then_inc(tl_ok, 1)

    def mixer_back_act(e, m):
        e.wait_ge(ys_ok, 4 * m + 4)
        ge(e, g_lo, m - 1)
        for q in range(4):
            for j in range(4):
                dst = sq[32 * q:32 * q + 32, m % 2, 0:SEQ].rearrange("p (c j) -> p j c", j=4)[:, j, :]
                e.activation(dst, u_t[32 * j:32 * j + 32, 4 * m + q, :], ACT.Gelu_apprx_tanh).then_inc(ge_ok, 1)
        e.wait_ge(ge_ok, 16 * m + 16)
        e.activation(a_hi[:, m, :], sq[:, m % 2, 0:SEQ], ACT.Copy).then_inc(g_hi, 1)

    def mixer_dve(e, m):
        e.wait_ge(v_mm, m + 1)
        er, ei = (t[:, 4 * m:4 * m + 4, :].rearrange("p q c -> p (q c)") for t in (e_r, e_i))
        z = [t2[:, k, 0:SEQ] for k in range(2)]
        w = T4(SEQ)
        cmul(e, dve, z[0], z[1], (er, ei), (ps[:, VB[m % 2][0], :], ps[:, VB[m % 2][1], :]), w, -1)
        e.drain().then_inc(v_ev, 1)
        for k in range(2):
            for q in range(4):
                c = slice(q * P, (q + 1) * P)
                n = dve.did(e.tensor_tensor_scan(t0[:, k, c], S(V_M4)[:, 4 * m + q:4 * m + q + 1].to_broadcast([P, P]),
                                                 t2[:, k, c], 0.0, ALU.mult, ALU.add))
        e.wait_ge(dve_did, n)
        ge(e, y_mm, m)
        q4 = lambda t: t.rearrange("p (q c) -> p q c", q=4)
        x = [x_s[:, k, :, 1:P + 1] for k in range(2)]
        cmul(e, dve, x[0], x[1], (q4(er), q4(ei)), (q4(t0[:, 0, 0:SEQ]), q4(t0[:, 1, 0:SEQ])),
             [q4(t) for t in (t1[:, 0, 0:SEQ], t1[:, 1, 0:SEQ], t2[:, 0, 0:SEQ], t2[:, 1, 0:SEQ])])
        e.drain().then_inc(xs_ok, 1)

    def mixer_out_dve(e, m):
        e.wait_ge(y_mm, m + 1)
        for q in range(4):
            e.scalar_tensor_tensor(u_t[:, 4 * m + q, :], u_t[:, 4 * m + q, :], vec("ssm_d", 4 * m + q),
                                   ps[:, 2, q * P:(q + 1) * P], ALU.mult, ALU.add).then_inc(ys_ok, 1)

    def mixer_lo_dve(e, m):
        e.wait_ge(g_hi, m + 1)
        e.tensor_tensor(a_lo[:, m, :], sq[:, m % 2, 0:SEQ], a_hi[:, m, :], ALU.subtract).then_inc(g_lo, 1)

    def glu_act(e, u, m):
        e.wait_ge(unit_mm, u.n(2))
        e.activation(t0[:, m % 2, 0:SEQ], ps[:, (u.slot + 1) % 4, :], ACT.Sigmoid).then_inc(sig_ok, 1)

    def glu_dve(e, u, m):
        e.wait_ge(sig_ok, m + 1)
        e.tensor_tensor(t1[:, m % 2, 0:SEQ], ps[:, u.slot, :], t0[:, m % 2, 0:SEQ], ALU.mult).then_inc(unit_ev, 1)
        e.wait_ge(unit_ev, u.n(1))
        e.tensor_tensor(h[:, m, REAL], h[:, m, REAL], t1[:, m % 2, 0:SEQ], ALU.add).then_inc(unit_ev, 1)

    A0 = 32

    def pair_n(layer, j):
        return FFT * layer + j

    def up_act(e, layer, j0, u, s):
        k, j = s // 2, j0 + 2 * u.i + s // 2
        G = pair_n(layer, j)
        split_ahead(e, u, split_hi)
        if s % 2 == 0:
            ge(e, gel_ok, G)
        else:
            e.wait_ge(alo_ok, A0 + G)
        e.wait_ge(unit_ev, u.n(1))
        c = 2 * j + s % 2
        e.activation(t1[:, s % 2, 0:SEQ], t0[:, s % 2, 2:SEQ + 2], ACT.Identity, bias=vec(f"ffn_b{layer}", c),
                     scale=vec(f"ffn_w{layer}", 88 + c)).then_inc(c0_ok, 1)
        if s % 2:
            e.wait_ge(cg_ok, G + 1)
            e.activation(t2[:, k, 0:SEQ], t1[:, 0, 0:SEQ], ACT.Gelu_apprx_tanh).then_inc(gel_ok, 1)
            e.wait_ge(ay_ok, A0 + G + 1)
            e.activation(tile_of(a_hi, 2 * u.i + k), t1[:, 1:2, 0:SEQ], ACT.Copy).then_inc(ahi_ok, 1)

    def up_dve(e, layer, j0, u, s):
        k, j = s // 2, j0 + 2 * u.i + s // 2
        G = pair_n(layer, j)
        c = 2 * j + s % 2
        split_ahead(e, u, split_lo)
        e.wait_ge(unit_mm, u.n(1))
        e.tensor_tensor(t0[:, s % 2, 2:SEQ + 2], ps[:, u.slot, :], rstd[:, 0:SEQ], ALU.mult).then_inc(unit_ev, 1)
        e.wait_ge(c0_ok, 2 * G + s % 2 + 1)
        e.wait_ge(unit_ev, u.n(1))
        y = t1[:, s % 2, 0:SEQ]
        n = dve.did(e.scalar_tensor_tensor(y, t0[:, s % 2, 1:SEQ + 1], vec(f"ffn_w{layer}", 44 + c), y, ALU.mult, ALU.add))
        e.wait_ge(dve_did, n)
        e.scalar_tensor_tensor(y, t0[:, s % 2, 0:SEQ], vec(f"ffn_w{layer}", c), y, ALU.mult, ALU.add)\
            .then_inc(cg_ok if s % 2 == 0 else cv_ok, 1)
        if s % 2 == 0:
            e.wait_ge(cg_ok, G + 1)
        if s % 2:
            e.wait_ge(cv_ok, G + 1)
            e.wait_ge(gel_ok, G + 1)
            e.tensor_tensor(y, y, t2[:, k, 0:SEQ], ALU.mult).then_inc(ay_ok, 1)
            e.wait_ge(ahi_ok, A0 + G + 1)
            e.wait_ge(ay_ok, A0 + G + 1)
            a = 2 * u.i + k
            e.tensor_tensor(tile_of(a_lo, a), t1[:, 1:2, 0:SEQ], tile_of(a_hi, a), ALU.subtract).then_inc(alo_ok, 1)

    def ffn(e, who, layer, u0, n):
        j0, u = 0, u0
        gain = f"ple_norm{layer}"
        for gi, g in enumerate(FFG):
            first = 1 if layer == 0 and j0 == 0 else 0
            if who == "act":
                units(e, u, g // 2, lambda v, s: up_act(e, layer, j0, v, s), first)
            elif who == "dve":
                units(e, u, g // 2, lambda v, s: up_dve(e, layer, j0, v, s), first, counts=dve, rate=4)
            else:
                if j0 == 0:
                    def up0(v, s):
                        ready = None
                        if isinstance(v.i, int) and v.i == 0 and s == 0:
                            ready = lambda e, k: e.wait_ge(xlo_ok, 8 * XN[n - 1] + k + 1)
                        unit_pe(e, v, x_hi, x_lo, ready)
                    units(e, u, g // 2, up0, 1)
                else:
                    units(e, u, g // 2, lambda v, s: unit_pe(e, v, x_hi, x_lo))
            u += 2 * g
            last = gi == len(FFG) - 1
            for m in range(KT):
                v = Unit(u + m)
                if who == "act":
                    split_ahead(e, v, split_hi)
                    if last:
                        e.wait_ge(unit_ev, v.n(1))
                        norm_act(e, n, m, None)
                elif who == "dve":
                    split_ahead(e, v, split_lo)
                    add_dve(e, v, m)
                else:
                    ready = (lambda e, k: e.wait_ge(alo_ok, A0 + pair_n(layer, j0) + k + 1)) if m == 0 else None
                    unit_pe(e, v, a_hi, a_lo, ready, kt=g)
                    if last and m:
                        stat_pe(e, n, m - 1)
            u += KT
            j0 += g
        if who == "act":
            root_act(e, n, eps6)
            for m in range(KT):
                x_act(e, n, m, gain)
        elif who == "dve":
            root_dve(e, n)
            for m in range(KT):
                x_dve(e, XN[n], m, gain)
        else:
            stat_pe(e, n, KT - 1)

    def side(e, who, layer, u0, n):
        if who == "act":
            e.wait_ge(p_in, 16 * (layer + 1))
            e.activation(p_hi[:, :, :], p_raw[:, :, :], ACT.Copy).then_inc(phi_ok, 1)
            for s in range(2):
                split_ahead(e, Unit(u0 + s), split_hi)
            for m in range(KT):
                u = Unit(u0 + 2 + m)
                split_ahead(e, u, split_hi)
                e.wait_ge(unit_ev, u.n(1))
                ge(e, sgu_ok, 8 * layer + m - 1)
                e.activation(t1[:, m % 2, 0:SEQ], t0[:, m % 2, 0:SEQ], ACT.Sigmoid).then_inc(sg_ok, 1)
        elif who == "dve":
            e.wait_ge(phi_ok, layer + 1)
            e.tensor_tensor(p_lo[:, :, :], p_raw[:, :, :], p_hi[:, :, :], ALU.subtract).then_inc(plo_ok, 1)
            for s in range(2):
                u = Unit(u0 + s)
                split_ahead(e, u, split_lo)
                e.wait_ge(unit_mm, u.n(1))
                e.tensor_copy(pp[:, 4 * s:4 * s + 4, :], ps[:, 0:4, :]).then_inc(unit_ev, 1)
            for m in range(KT + 1):
                if m < KT:
                    u = Unit(u0 + 2 + m)
                    split_ahead(e, u, split_lo)
                    e.wait_ge(unit_mm, u.n(1))
                    ge(e, sg_ok, 8 * layer + m - 1)
                    e.tensor_tensor(t0[:, m % 2, 0:SEQ], ps[:, u.slot, :], rstd[:, 0:SEQ], ALU.mult).then_inc(unit_ev, 1)
                if m:
                    j = m - 1
                    e.wait_ge(sg_ok, 8 * layer + j + 1)
                    e.wait_ge(unit_ev, u0 + 2)
                    e.tensor_tensor(t2[:, j % 2, 0:SEQ], t1[:, j % 2, 0:SEQ], pp[:, j, :], ALU.mult).then_inc(sgu_ok, 1)
                    e.wait_ge(sgu_ok, 8 * layer + j + 1)
                    e.tensor_tensor(h[:, j, REAL], h[:, j, REAL], t2[:, j % 2, 0:SEQ], ALU.add).then_inc(h_fin, 1)
        else:
            e.wait_ge(plo_ok, layer + 1)
            for s in range(2):
                u = Unit(u0 + s)
                e.wait_ge(lo_ok, u.n(1))
                e.wait_ge(unit_ev, u.n())
                for q in range(4):
                    last = products(e, u, q, p_hi, p_lo, kt=2, w0=2 * q)
                last.then_inc(unit_mm, 1)
            e.wait_ge(unit_ev, u0 + 2)
            for m in range(KT):
                ready = (lambda e, k: e.wait_ge(xlo_ok, 8 * XN[n] + k + 1)) if m == 0 else None
                unit_pe(e, Unit(u0 + 2 + m), x_hi, x_lo, ready)


    def normed(e, who, u0, b, store, gain, hi, lo, ready=None):
        def last(m):
            if b > 1:
                k = 8 * (b - 1) + m
                if who == "dve":
                    if m == 0:
                        head_inverse(e, b - 1)
                    head_scale(e, k, gain[0][:, m, :], gain[1], gain[0][:, m, :])
                elif who == "pe":
                    head_spread(e, k)

        if b > 1 and who == "act":
            head_root(e, b - 1, HD, eps6)
        for m in range(8 + 1):
            if m < 8:
                u = Unit(u0 + m)
                if who == "act":
                    split_ahead(e, u, split_hi)
                    if b < 3:
                        e.wait_ge(unit_ev, u.n(1))
                        head_sq(e, 8 * b + m, store[:, m, :])
                elif who == "dve":
                    split_ahead(e, u, split_lo)
                    e.wait_ge(unit_mm, u.n(1))
                    e.tensor_tensor(store[:, m, :], ps[:, u.slot, :], rstd[:, 0:SEQ], ALU.mult).then_inc(unit_ev, 1)
                else:
                    unit_pe(e, u, hi, lo, ready if m == 0 else None)
            if m:
                if who == "pe" and b < 3:
                    head_pe(e, 8 * b + m - 1)
                last(m - 1)

    def stage2_pool(e, p):
        par = p % 2
        k = 4 * p
        ge(e, o_ok, p - 1)
        for c in range(2):
            r = slice(HD * c, HD * c + HD)
            e.wait_ge(staged, 32 + k + c)
            e.tensor_copy(qs2[r, par, c, :], q2[r, p, :]).then_inc(staged, 1)
        e.wait_ge(staged, 32 + k + 2)
        e.tensor_copy(ks2[:, par, :], k2[:, p, :]).then_inc(staged, 1)
        e.wait_ge(staged, 32 + k + 3)
        e.tensor_copy(vs2[:, par, :], v2[:, p, :]).then_inc(staged, 1)

    def bias_load(e, p):
        ge(e, blo_ok, p)
        src = bass.AP(scratch.tensor, scratch.offset + p * 640 + 1, [[1, P], [1, SEQ]])
        e.dma_start(b_raw[:, 0, :], src).then_inc(b_in, 16)

    def attention2(e, who):
        def pe_scores(g):
            p, qt, sl = g // 4, g % 4, g % 2
            N = (qt + 1) * P
            if qt == 0:
                e.wait_ge(staged, 32 + 4 * p + 4)
                e.wait_ge(blo_ok, p + 1)
                ge(e, o_ok, p - 1)
                for j in range(4):
                    last = e.transpose(ps[:, 6 + p % 2, j * P:(j + 1) * P], vs2[:, p % 2, j * P:(j + 1) * P], ident[:, :])
                last.then_inc(vt_mm, 1)
            ge(e, exp_ok, 32 + 2 * (g - 1))
            for c in range(2):
                o = ps[:, 2 * sl + c, 0:N]
                e.matmul(o, qs2[:, p % 2, c, qt * P:(qt + 1) * P], ks2[:, p % 2, 0:N], start=True, stop=False)
                for n, t in enumerate((b_hi, b_lo)):
                    last = e.matmul(o, flip_r[:, :], t[:, p % 2, SEQ - N:SEQ], start=False, stop=(n == 1))
            last.then_inc(s_mm, 1)

        def pe_turn(g):
            p, qt, sl = g // 4, g % 4, g % 2
            e.wait_ge(nrm_ok, 32 + g + 1)
            if qt == 0:
                e.wait_ge(v2_ok, p + 1)
            for j in range(qt + 1):
                last = e.transpose(ps[:, 4 + sl, j * P:(j + 1) * P], t0[:, sl, j * P:(j + 1) * P], ident[:, :])
            last.then_inc(pt_mm, 1)

        def pe_pv(g):
            p, qt, sl = g // 4, g % 4, g % 2
            e.wait_ge(pt_ok, 64 + g + 1)
            if qt == 0:
                ge(e, o_ok, p - 1)
            for j in range(qt + 1):
                last = e.matmul(ps[:, 6 + p % 2, qt * P:(qt + 1) * P], vtok[:, p % 2, j, :], pt2[:, sl, j, :],
                                start=(j == 0), stop=(j == qt))
            last.then_inc(pv_mm, 1)

        def dve_top(g):
            p, qt, sl = g // 4, g % 4, g % 2
            N = (qt + 1) * P
            if qt == 0:
                e.wait_ge(bhi_ok, p + 1)
                e.tensor_tensor(b_lo[:, p % 2, :], b_raw[:, 0, :], b_hi[:, p % 2, :], ALU.subtract).then_inc(blo_ok, 1)
            e.wait_ge(s_mm, 32 + g + 1)
            for c in range(2):
                n = dve.did(e.reduce_max(small[:, 0, 2 * sl + c:2 * sl + c + 1], ps[:, 2 * sl + c, 0:N], AX_X))
            e.wait_ge(dve_did, n)
            e.tensor_scalar(small[:, 1, 2 * sl:2 * sl + 2], small[:, 0, 2 * sl:2 * sl + 2], -0.125, None, ALU.mult)\
                .then_inc(nb_ok, 1)

        def dve_mix(g):
            p, qt, sl = g // 4, g % 4, g % 2
            N = (qt + 1) * P
            e.wait_ge(exp_ok, 32 + 2 * g + 2)
            r = small[:, 3, 2 * sl:2 * sl + 2]
            n = dve.did(e.reciprocal(r, small[:, 2, 2 * sl:2 * sl + 2]))
            e.wait_ge(dve_did, n)
            n = dve.did(e.tensor_tensor(small[:, 3, 2 * sl + 1:2 * sl + 2], small[:, 3, 2 * sl + 1:2 * sl + 2],
                                        neg_lam[:, :], ALU.mult))
            n = dve.did(e.tensor_scalar(t0[:, sl, 0:N], t0[:, sl, 0:N], small[:, 3, 2 * sl:2 * sl + 1], None, ALU.mult))
            e.wait_ge(dve_did, n)
            e.scalar_tensor_tensor(t0[:, sl, 0:N], t1[:, sl, 0:N], small[:, 3, 2 * sl + 1:2 * sl + 2],
                                   t0[:, sl, 0:N], ALU.mult, ALU.add).then_inc(nrm_ok, 1)

        def dve_out(p):
            e.wait_ge(pv_mm, 32 + 4 * p + 4)
            e.wait_ge(staged, 32 + 4 * p + 4)
            e.tensor_copy(q2[:, p, :], ps[:, 6 + p % 2, :]).then_inc(o_ok, 1)

        def act_exp(g):
            p, qt, sl = g // 4, g % 4, g % 2
            N = (qt + 1) * P
            if qt == 0:
                e.wait_ge(b_in, 16 * (p + 1))
                ge(e, s_mm, 32 + 4 * (p - 1))
                e.activation(b_hi[:, p % 2, :], b_raw[:, 0, :], ACT.Copy).then_inc(bhi_ok, 1)
            e.wait_ge(nb_ok, 32 + g + 1)
            ge(e, pt_mm, 32 + g - 1)
            for c, t in enumerate((t0, t1)):
                e.activation(t[:, sl, 0:N], ps[:, 2 * sl + c, 0:N], ACT.Exp,
                             bias=small[:, 1, 2 * sl + c:2 * sl + c + 1], scale=0.125,
                             accum_out=small[:, 2, 2 * sl + c:2 * sl + c + 1]).then_inc(exp_ok, 1)

        def act_turn(g):
            p, qt, sl = g // 4, g % 4, g % 2
            N = (qt + 1) * P
            if qt == 0:
                e.wait_ge(vt_mm, 4 + p + 1)
                e.activation(vtok[:, p % 2, :, :].rearrange("p j c -> p (j c)"), ps[:, 6 + p % 2, :], ACT.Copy)\
                    .then_inc(v2_ok, 1)
            e.wait_ge(pt_mm, 32 + g + 1)
            ge(e, pv_mm, 32 + g - 1)
            e.activation(pt2[:, sl, 0:qt + 1, :].rearrange("p j c -> p (j c)"), ps[:, 4 + sl, 0:N], ACT.Copy)\
                .then_inc(pt_ok, 1)

        for g in range(32 + 2):
            if who == "pe":
                if g < 32:
                    pe_scores(g)
                if 1 <= g < 33:
                    pe_turn(g - 1)
                if g >= 2:
                    pe_pv(g - 2)
            elif who == "dve":
                if 1 <= g < 33:
                    dve_mix(g - 1)
                if g < 32:
                    dve_top(g)
                if g >= 5 and (g - 5) % 4 == 0:
                    dve_out((g - 5) // 4)
            else:
                if g < 32:
                    act_exp(g)
                if 1 <= g < 33:
                    act_turn(g - 1)

    block = ctx.enter_context(nc.Block())

    @block.sync
    def _(sp):
        sp.dma_start(vecs[:, :], A["vecs"]).then_inc(consts_in, 16)
        sp.dma_start(h[:, 0:4, :], A["xT"][:, 0:4, :]).then_inc(h_in[0], 16)
        load_unit(sp, Unit(0))
        sp.dma_start(h[:, 4:8, :], A["xT"][:, 4:8, :]).then_inc(h_in[1], 16)
        load_unit(sp, Unit(1))
        for name, t in (("ones", ones), ("spread", spread1), ("ident", ident), ("flip", flip), ("mask", mask), ("win", win)):
            sp.dma_start(t[:, :], A[name]).then_inc(consts_in, 16)
        sp.dma_start(wf[:, :, :], A["wf"]).then_inc(consts_in, 16)
        sp.dma_start(rel[:, :], A["rel"]).then_inc(consts_in, 16)
        for s in range(2, 4):
            load_unit(sp, Unit(s))
        with sp.Fori(1, NLOAD // 4) as i:
            for s in range(4):
                load_unit(sp, Unit(s, i))
        if stop in (99, 7, 4):
            sp.wait_ge(h_fin, 8 * (2 if stop == 4 else 3))
        elif stop == 1:
            sp.wait_ge(h_fin, 8)
        else:
            sp.wait_ge(fence_at, {2: 20, 5: 32}[stop])
        sp.dma_start(out, h[:, :, REAL]).then_inc(stored, 16)
        sp.wait_ge(stored, 16)

    @block.gpsimd
    def _(e):
        e.memset(eps5[:, :], 1e-5).then_inc(consts_ok, 1)
        e.memset(eps6[:, :], 1e-6).then_inc(consts_ok, 1)
        e.memset(eps_o[:, :], 1e-6 / (1.0 - LAM) ** 2).then_inc(consts_ok, 1)
        e.memset(aug_q[:, :, :, :], 0.0).then_inc(consts_ok, 1)
        e.memset(aug_k[:, :], 0.0).then_inc(consts_ok, 1)
        e.wait_ge(consts_ok, 5)
        e.memset(aug_k[32:40, :], 1.0).then_inc(consts_ok, 1)
        system_pool(e)
        fence(e, 1)
        e.memset(qs[:, :, :, :], 0.0).then_inc(qz_ok, 1)
        e.wait_ge(qz_ok, 1)
        for i in range(2):
            stage1_pool(e, i)
        fence(e, 2)
        if stop == 1:
            return
        e.wait_ge(hn_lo, 8)
        e.dma_start(b_in_[:, :, :, :], A["ssm_bc"][:, 0:2, :, :]).then_inc(bc_in, 16)
        e.dma_start(c_raw[:, :, :, :], A["ssm_bc"][:, 2:4, :, :]).then_inc(bc_in, 16)
        tables_pool(e)
        e.drain().then_inc(tables_ok, 1)
        matrices_pool(e, 0)

        def spread(u, s):
            e.wait_ge(unit_ev, u.n(1))
            m = u.n(-U_SSM)
            for q in range(4):
                for j in (2, 3):
                    ge(e, ut_p, 8 * m + 2 * q + j - 2)
                    spread_u(e, u, m, q, j, "p").then_inc(ut_p, 1)

        units(e, U_SSM, 2, spread, 1)
        fence(e, 3)
        e.wait_ge(pads_ok, 7)
        for m in range(1, 8):
            matrices_pool(e, m)
        fence(e, 4)
        e.dma_start(spread2[:, :], A["spread"]).then_inc(tab_in, 16)
        e.dma_start(p_raw[:, :, :], A["pT"][:, 0, :, :]).then_inc(p_in, 16)
        fence(e, 5)
        if stop in (2, 4):
            return
        e.wait_ge(h_fin, 16)
        e.dma_start(onehot, A["onehot"]).then_inc(tab_in, 16)
        fence(e, 6)
        e.wait_ge(tab_ok, 2)
        e.dma_start(scratch, tab[0:8, :]).then_inc(tab_out, 16)
        e.memset(qs2[:, :, :, :], 0.0).then_inc(zz_ok, 1)
        e.wait_ge(zz_ok, 1)
        e.wait_ge(tab_out, 16)
        for p in range(8):
            bias_load(e, p)
            stage2_pool(e, p)
        fence(e, 7)
        fence(e, 8)
        e.dma_start(p_raw[:, :, :], A["pT"][:, 1, :, :]).then_inc(p_in, 16)

    @block.scalar
    def _(e):
        for m in range(KT):
            if m % 4 == 0:
                e.wait_ge(h_in[m // 4], 16)
            if m == 0:
                e.wait_ge(consts_in, 16 * 9)
            norm_act(e, 0, m, "norm_mix", TOK)
            if m in (1, 3):
                split_hi(e, Unit(m // 2))
        e.wait_ge(consts_ok, 6)
        root_act(e, 0, eps5, TOK)
        e.activation(wf_hi[:, :, :], wf[:, :, :], ACT.Copy).then_inc(wf_ok, 1)
        e.activation(ident_b[:, :], ident[:, :], ACT.Copy).then_inc(wf_ok, 1)
        e.activation(mask_b[:, :], mask[:, :], ACT.Copy).then_inc(wf_ok, 1)
        e.activation(flip_r[:, :], flip[:, :], ACT.Copy).then_inc(wf_ok, 1)
        e.activation(S(V_DT), vecs[:, COL["log_dt"]:COL["log_dt"] + 32], ACT.Exp).then_inc(dt_ok, 1)
        units(e, U_QKVB, 4, lambda u, s: split_ahead(e, u, split_hi), 1)
        e.wait_ge(par_v, 1)
        e.activation(S(V_MAG), S(V_SH), ACT.Exp).then_inc(par_a, 1)
        e.wait_ge(par_v, 2)
        e.activation(S(V_COS), S(V_R), ACT.Sin, scale=0.5).then_inc(par_a, 1)
        e.activation(S(V_SIN), S(V_R), ACT.Sin).then_inc(par_a, 1)
        f_scalar(e)
        units(e, U_CU, 2, lambda u, s: split_ahead(e, u, split_hi))
        fence(e, 1)
        for i in range(2):
            attention1_act(e, i)
        fence(e, 2)
        for m in range(8 + 1):
            if m < 8:
                head_sq(e, m, y_tile(m))
            if m == 8:
                head_root(e, 0, HD, eps5)
        for m in range(8):
            head_hi(e, m, m)
        for m in range(KT):
            u = Unit(U_OUT1 + m)
            split_ahead(e, u, split_hi)
            e.wait_ge(unit_ev, u.n(1))
            norm_act(e, 1, m, "norm_mlp")
        root_act(e, 1, eps5)

        def ff(u, s):
            split_ahead(e, u, split_hi)
            if s < 8:
                hidden_hi(e, 8 * u.i + s, s)

        units(e, U_FF, 3, ff, cycle=16)
        for s in range(16):
            u = Unit(U_FF + 48 + s)
            split_ahead(e, u, split_hi)
            if s < 8:
                hidden_hi(e, 24 + s, s)
            else:
                e.wait_ge(unit_ev, u.n(1))
                norm_act(e, 2, s - 8, None)
        root_act(e, 2, eps5)
        if stop == 1:
            return
        for m in range(KT):
            e.wait_ge(h_fin, m + 1)
            norm_act(e, 3, m, "ssm_norm")
        root_act(e, 3, eps6)

        def spread(u, s):
            split_ahead(e, u, split_hi)
            e.wait_ge(unit_ev, u.n(1))
            m = u.n(-U_SSM)
            for q in range(4):
                for j in (0, 1):
                    spread_u(e, u, m, q, j, "a").then_inc(ut_a, 1)

        units(e, U_SSM, 2, spread, 1)
        fence(e, 3)
        e.wait_ge(pads_ok, 7)
        for m in range(8 + 2):
            if m < 8:
                mixer_front_act(e, m)
            if m >= 2:
                mixer_back_act(e, m - 2)
        fence(e, 4)
        for m in range(KT):
            u = Unit(U_GLU + 2 * m)
            split_ahead(e, u, split_hi)
            split_ahead(e, u.ahead(1), split_hi)
            glu_act(e, u, m)
            e.wait_ge(unit_ev, u.n(2))
            norm_act(e, 4, m, "ffn_norm0")
        root_act(e, 4, eps6)
        fence(e, 5)
        if stop == 2:
            return
        ffn(e, "act", 0, U_FFNA, 5)
        side(e, "act", 0, U_PPA, 5)
        if stop == 4:
            return
        for m in range(KT):
            e.wait_ge(h_fin, 8 + m + 1)
            if m == 0:
                e.wait_ge(unit_mm, U_Q)
            norm_act(e, 6, m, "kv_norm")
        for m in range(KT):
            x_act(e, 6, m, "attn_norm", hi=a_hi)
        root_act(e, 6, eps6)
        e.wait_ge(lam_mm, 1)
        e.activation(small[:, 1, 0:2], ps[:, 7, 0:2], ACT.Exp).then_inc(lam_a, 1)
        for b, (u0, store) in enumerate(((U_Q, q2), (U_KV, k2), (U_KV + 8, v2)), 1):
            normed(e, "act", u0, b, store, None, None, None)
        fence(e, 6)
        attention2(e, "act")
        fence(e, 7)
        for m in range(8 + 1):
            if m < 8:
                head_sq(e, 24 + m, q2[:, m, :])
            if m == 8:
                head_root(e, 3, P * (1 - LAM) ** 2, eps_o)
        for m in range(8):
            head_hi(e, 24 + m, m)
        for m in range(KT):
            u = Unit(U_WO + m)
            split_ahead(e, u, split_hi)
            e.wait_ge(unit_ev, u.n(1))
            norm_act(e, 7, m, "ffn_norm1")
        root_act(e, 7, eps6)
        fence(e, 8)
        if stop == 5:
            return
        ffn(e, "act", 1, U_FFNB, 8)
        side(e, "act", 1, U_PPB, 8)

    @block.vector
    def _(e):
        e.wait_ge(consts_in, 16 * 9)
        n = dve.did(e.memset(t2[0:8, 0, :], 1.0))
        for m in range(KT):
            x_dve(e, 0, m, "norm_mix", TOK)
            if m in (2, 4):
                split_lo(e, Unit(m // 2 - 1))
        e.wait_ge(wf_ok, 1)
        e.tensor_tensor(wf_lo[:, :, :], wf[:, :, :], wf_hi[:, :, :], ALU.subtract).then_inc(wflo_ok, 1)
        root_dve(e, 0, TOK)

        def qkvb_dve(u, s):
            split_ahead(e, u, split_lo)
            t = u.n()
            wide_dve(e, u, tile_of(qkvb, t).rearrange("p a b -> p (a b)"))

        units(e, U_QKVB, 4, qkvb_dve, 1)
        f_dve(e)
        system_dve(e)

        def conv(u, s):
            split_ahead(e, u, split_lo)
            conv_dve(e, u, s)

        units(e, U_CU, 2, conv, counts=dve, rate=10)
        fence(e, 1)
        n = dve.did(e.memset(vp[:, :, :, :, :], 0.0))
        e.memset(vm[:, :, :, :], 0.0).then_inc(vz_ok, 1)
        for i in range(2):
            attention1_dve(e, i)
        fence(e, 2)
        head_inverse(e, 0)
        for m in range(8 + 1):
            if m < 8:
                head_scale(e, m, y_tile(m), vec("out_norm", m))
            if m:
                head_lo(e, m - 1, m - 1)
        for m in range(KT):
            u = Unit(U_OUT1 + m)
            split_ahead(e, u, split_lo)
            add_dve(e, u, m)
            if m:
                x_dve(e, 1, m - 1, "norm_mlp")
        x_dve(e, 1, KT - 1, "norm_mlp")
        root_dve(e, 1)

        def ff(u, s):
            split_ahead(e, u, split_lo)
            if s < 8:
                relu2_dve(e, u, s)
                if s:
                    hidden_lo(e, 8 * u.i + s - 1, s - 1)
                if s == 7:
                    hidden_lo(e, 8 * u.i + 7, 7)
            else:
                add_dve(e, u, s - 8)

        units(e, U_FF, 3, ff, first=1, cycle=16)
        for s in range(16):
            ff(Unit(U_FF + s, 3, 16), s)
        root_dve(e, 2)
        for m in range(KT):
            e.scalar_tensor_tensor(h[:, m, REAL], h[:, m, REAL], vec("final_norm", m), rstd[:, 0:SEQ],
                                   ALU.mult, ALU.mult).then_inc(h_fin, 1)
        if stop == 1:
            return
        for m in range(KT):
            x_dve(e, 2, m, "ssm_norm")
        root_dve(e, 3)

        def project_u(u, s):
            split_ahead(e, u, split_lo)
            e.wait_ge(unit_mm, u.n(1))
            m = u.n(-U_SSM)
            ge(e, ut_a, 8 * (m - 1))
            ge(e, ut_p, 8 * (m - 1))
            e.tensor_tensor(t0[:, s % 2, 0:SEQ], ps[:, u.slot, :], rstd[:, 0:SEQ], ALU.mult).then_inc(unit_ev, 1)

        units(e, U_SSM, 2, project_u, 1)
        fence(e, 3)
        for t in (v_b1, c_p1, c_p2):
            e.memset(t[:], 0.0).then_inc(pads_ok, 1)
        e.memset(t_l[:, :, :], 0.0).then_inc(pads_ok, 1)
        e.memset(x_s[:, :, :, 0:1], 0.0).then_inc(pads_ok, 1)
        e.wait_ge(pads_ok, 7)
        e.wait_ge(tables_ok, 1)
        for m in range(8 + 1):
            if m < 8:
                mixer_dve(e, m)
            if m >= 3:
                mixer_lo_dve(e, m - 3)
            if m:
                mixer_out_dve(e, m - 1)
        mixer_lo_dve(e, 6)
        mixer_lo_dve(e, 7)
        fence(e, 4)
        for m in range(KT):
            u = Unit(U_GLU + 2 * m)
            split_ahead(e, u, split_lo)
            split_ahead(e, u.ahead(1), split_lo)
            glu_dve(e, u, m)
            if m:
                x_dve(e, 3, m - 1, "ffn_norm0")
        x_dve(e, 3, KT - 1, "ffn_norm0")
        root_dve(e, 4)
        fence(e, 5)
        if stop == 2:
            return
        n = dve.did(e.memset(t0[:, :, 0:2], 0.0))
        e.wait_ge(dve_did, n)
        ffn(e, "dve", 0, U_FFNA, 5)
        side(e, "dve", 0, U_PPA, 5)
        if stop == 4:
            return
        for m in range(KT):
            x_dve(e, 5, m, "kv_norm")
        for m in range(KT):
            x_dve(e, 6, m, "attn_norm", hi=a_hi, lo=a_lo)
        root_dve(e, 6)
        c = COL["lambdas"]
        e.tensor_tensor(small[:, 0, 0:2], vecs[:, c:c + 4:2], vecs[:, c + 1:c + 4:2], ALU.mult).then_inc(lam_v, 1)
        normed(e, "dve", U_Q, 1, q2, None, None, None)
        normed(e, "dve", U_KV, 2, k2, (q2, vec("q_norm")), None, None)
        normed(e, "dve", U_KV + 8, 3, v2, (k2, vec("k_norm")), None, None)
        e.wait_ge(tab_mm, 1)
        for lo, n in ((0, SEQ), (SEQ, P)):
            e.tensor_scalar(tab[0:8, lo:lo + n], ps[0:8, 6 + lo // SEQ, 0:n], 8.0, None, ALU.mult)\
                .then_inc(tab_ok, 1)
        e.wait_ge(lam_a, 1)
        n = dve.did(e.tensor_tensor(small[:, 2, 0:1], small[:, 1, 1:2], small[:, 1, 0:1], ALU.subtract))
        e.wait_ge(dve_did, n)
        n = dve.did(e.tensor_scalar(neg_lam[:, :], small[:, 2, 0:1], -LAM, None, ALU.add))
        fence(e, 6)
        attention2(e, "dve")
        fence(e, 7)
        head_inverse(e, 3)
        for m in range(8 + 1):
            if m < 8:
                head_scale(e, 24 + m, q2[:, m, :], vec("subln"))
            if m:
                head_lo(e, 24 + m - 1, m - 1)
        for m in range(KT):
            u = Unit(U_WO + m)
            split_ahead(e, u, split_lo)
            add_dve(e, u, m)
            if m:
                x_dve(e, 7, m - 1, "ffn_norm1")
        x_dve(e, 7, KT - 1, "ffn_norm1")
        root_dve(e, 7)
        fence(e, 8)
        if stop == 5:
            return
        n = dve.did(e.memset(t0[:, :, 0:2], 0.0))
        e.wait_ge(dve_did, n)
        ffn(e, "dve", 1, U_FFNB, 8)
        side(e, "dve", 1, U_PPB, 8)

    @block.tensor
    def _(e):
        e.wait_ge(consts_in, 16 * 9)
        for m in range(KT):
            stat_pe(e, 0, m, TOK)
        units(e, U_QKVB, 4, lambda u, s: wide_pe(e, u), 1)
        f_pe(e)
        units(e, U_CU, 2, lambda u, s: wide_pe(e, u))
        fence(e, 1)
        for i in range(2):
            attention1_pe(e, i)
        fence(e, 2)
        for m in range(8):
            head_pe(e, m)
        for m in range(8):
            head_spread(e, m)
        e.wait_ge(unit_ev, U_OUT1)
        for m in range(KT):
            ready = (lambda e, k: e.wait_ge(hn_lo, k + 1)) if m == 0 else None
            unit_pe(e, Unit(U_OUT1 + m), a_hi, a_lo, ready)
            if m:
                stat_pe(e, 1, m - 1)
        stat_pe(e, 1, KT - 1)

        def ff(u, s):
            ready = None
            if s == 0 and isinstance(u.i, int) and u.i == 0:
                ready = lambda e, k: e.wait_ge(xlo_ok, 8 + k + 1)
            if s == 8:
                ready = lambda e, k: e.wait_ge(alo_ok, 8 * u.i + k + 1)
            if s < 8:
                unit_pe(e, u, x_hi, x_lo, ready)
            else:
                unit_pe(e, u, a_hi, a_lo, ready)

        units(e, U_FF, 3, ff, first=1, cycle=16)
        for s in range(16):
            ff(Unit(U_FF + s, 3, 16), s)
            if s > 8:
                stat_pe(e, 2, s - 9)
        stat_pe(e, 2, KT - 1)
        if stop == 1:
            return
        for m in range(KT):
            stat_pe(e, 3, m)

        def project_u(u, s):
            ready = None
            if isinstance(u.i, int) and s == 0:
                ready = lambda e, k: e.wait_ge(xlo_ok, 16 + k + 1)
            unit_pe(e, u, x_hi, x_lo, ready)

        units(e, U_SSM, 2, project_u, 1)
        fence(e, 3)
        for m in range(8 + 1):
            if m < 8:
                mixer_front_pe(e, m)
            if m:
                mixer_back_pe(e, m - 1)
        fence(e, 4)
        for m in range(2 * KT):
            ready = (lambda e, k: e.wait_ge(g_lo, k + 1)) if m == 0 else None
            unit_pe(e, Unit(U_GLU + m), a_hi, a_lo, ready)
            if m % 2 and m > 2:
                stat_pe(e, 4, m // 2 - 1)
        stat_pe(e, 4, KT - 1)
        fence(e, 5)
        if stop == 2:
            return
        ffn(e, "pe", 0, U_FFNA, 5)
        side(e, "pe", 0, U_PPA, 5)
        if stop == 4:
            return
        for m in range(KT):
            stat_pe(e, 6, m)
        e.wait_ge(lam_v, 1)
        e.matmul(ps[:, 7, 0:2], ones[:, :], small[:, 0, 0:2], start=True, stop=True).then_inc(lam_mm, 1)
        normed(e, "pe", U_Q, 1, None, None, a_hi, a_lo, lambda e, k: e.wait_ge(xlo_ok, 48 + k + 1))
        e.wait_ge(lam_a, 1)
        e.wait_ge(tab_in, 32)
        normed(e, "pe", U_KV, 2, None, None, x_hi, x_lo)
        normed(e, "pe", U_KV + 8, 3, None, None, x_hi, x_lo)
        e.wait_ge(hn_y, 24)
        e.matmul(ps[0:8, 6, :], rel[:, :], onehot[:, 0:SEQ], start=True, stop=True)
        e.matmul(ps[0:8, 7, 0:P], rel[:, :], onehot[:, SEQ:640], start=True, stop=True).then_inc(tab_mm, 1)
        fence(e, 6)
        attention2(e, "pe")
        fence(e, 7)
        for m in range(8):
            head_pe(e, 24 + m, 1)
        for m in range(8):
            head_spread(e, 24 + m)
        for m in range(KT):
            ready = (lambda e, k: e.wait_ge(hn_lo, 8 + k + 1)) if m == 0 else None
            unit_pe(e, Unit(U_WO + m), a_hi, a_lo, ready)
            if m:
                stat_pe(e, 7, m - 1)
        stat_pe(e, 7, KT - 1)
        fence(e, 8)
        if stop == 5:
            return
        ffn(e, "pe", 1, U_FFNB, 8)
        side(e, "pe", 1, U_PPB, 8)


def lay_out(x):
    f = np.float32

    def cols(v, parts=P):
        return np.ascontiguousarray(np.asarray(v, f).reshape(-1, parts).T)

    V = np.zeros((P, NCOL), f)

    def put(name, m, parts=P):
        V[:parts, COL[name]:COL[name] + m.shape[1]] = m

    put("norm_mix", cols(x["norm_mix_g"])); put("out_norm", cols(x["out_norm_g"]))
    put("norm_mlp", cols(x["norm_mlp_g"])); put("final_norm", cols(x["final_norm_g"]))
    put("conv_w", cols(x["conv_w"])); put("b_f", np.asarray(x["b_f"], f).reshape(8, 1), 8)
    put("ssm_norm", cols(x["ssm_norm_2"])); put("kv_norm", cols(x["kv_norm_2"]))
    put("attn_norm", cols(x["attn_norm_2"]))
    for n in ("k_norm", "q_norm"):
        put(n, np.tile(np.asarray(x[n + "_2"], f).reshape(1, HD), (1, 2)).T)
    put("subln", cols(x["subln_2"]))
    order = np.arange(2 * FFT).reshape(2, FFT).T.ravel()
    for n in range(2):
        put(f"ffn_norm{n}", cols(x["ffn_norm_2"][n])); put(f"ple_norm{n}", cols(x["ple_norm_2"][n]))
        for tap in range(3):
            V[:, COL[f"ffn_w{n}"] + 44 * tap:COL[f"ffn_w{n}"] + 44 * tap + 44] = \
                cols(x["ffn_conv_w_2"][n][tap])[:, order]
        V[:, COL[f"ffn_b{n}"]:COL[f"ffn_b{n}"] + 44] = cols(x["ffn_conv_b_2"][n])[:, order]
    put("lam_re", cols(x["ssm_lambda_re_2"])); put("lam_im", cols(x["ssm_lambda_im_2"]))
    put("log_dt", cols(np.repeat(np.asarray(x["ssm_log_dt_2"], f).reshape(-1), HD)))
    dsk = np.asarray(x["ssm_d_2"], f).reshape(32, 32).T
    put("ssm_d", np.tile(dsk, (4, 1)))
    put("lambdas", np.stack([np.asarray(x[n + "_2"], f).reshape(HD) for n in
                             ("lambda_q1", "lambda_k1", "lambda_q2", "lambda_k2")], 1), HD)

    def tiles(w, ks, ms):
        w = np.asarray(w, f)
        t = w.reshape(w.shape[0] // P, P, w.shape[1] // P, P)
        o = np.zeros((len(ms), P, 8, P), f)
        o[:, :, :len(ks)] = t[list(ks)][:, :, list(ms)].transpose(2, 1, 0, 3)
        return o

    w_in = np.asarray(x["w_in"], f)[0]
    q, k, v, fg, b, c, u = np.split(w_in, [512, 1024, 1536, 1544, 2056, 2568], axis=1)
    K8 = range(8)
    out = [tiles(m, K8, range(4)) for m in (q, k, v, b)]
    out.append(tiles(np.concatenate([c, u], 1), K8, [0, 4, 1, 5, 2, 6, 3, 7]))
    out.append(tiles(x["w_out"][0], K8, K8))
    for g in range(4):
        out.append(tiles(x["w_ff1"][0], K8, range(8 * g, 8 * g + 8)))
        out.append(tiles(x["w_ff2"][0], range(8 * g, 8 * g + 8), K8))
    out.append(tiles(x["ssm_w_in_2"][0], K8, K8))
    out.append(tiles(x["ssm_w_glu_2"][0], K8, [m + 8 * s for m in range(8) for s in range(2)]))

    def tail(n):
        j0 = 0
        for g in FFG:
            out.append(tiles(x["ffn_w_up_2"][n], K8, [j + FFT * s for j in range(j0, j0 + g) for s in range(2)]))
            out.append(tiles(x["ffn_w_down_2"][n], range(j0, j0 + g), K8))
            j0 += g
        side = np.asarray(x["ple_w_proj_2"][n], f).reshape(2, P, 2, 4, P)
        out.append(side.transpose(2, 1, 3, 0, 4).reshape(2, P, 8, P))
        out.append(tiles(x["ple_w_gate_2"][n], K8, K8))

    tail(0)
    out.append(tiles(x["attn_w_q_2"][0], K8, K8))
    kv = np.asarray(x["kv_w_2"], f)
    out.append(tiles(kv[:, :D], K8, K8)); out.append(tiles(kv[:, D:], K8, K8))
    out.append(tiles(x["attn_w_o_2"][0], K8, K8))
    tail(1)
    W = np.concatenate(out)
    assert W.shape[0] == NU

    hx = np.concatenate([np.asarray(x["meta_tokens"], f), np.asarray(x["x"], f)[0]], 0)
    eye = np.eye(P, dtype=f)
    grp = lambda a: np.asarray(a, f)[0].reshape(32, P, 16).transpose(1, 0, 2)
    grc = lambda a: np.asarray(a, f)[0].transpose(0, 2, 1).reshape(32, P, 16).transpose(1, 0, 2)
    dist = SEQ - np.arange(640)
    far = np.maximum(dist, 16).astype(f)
    big = 16 + (np.log(far / f(16)) / f(np.log(8.0)) * f(16)).astype(np.int32)
    bucket = np.where(dist < 16, np.maximum(dist, 0), np.minimum(big, 31))
    onehot = np.where(dist < 0, 32, bucket)[None] == np.arange(33)[:, None]
    i = np.arange(P)
    win = np.zeros((P, 64), f)
    win[:HD, 15] = win[HD:, 16] = 1
    win[:, 32 + 15:32 + 17] = 1
    return {
        "wstream": W.reshape(NU * P, 8 * P), "xT": np.ascontiguousarray(hx.T.reshape(8, P, TOK).transpose(1, 0, 2)),
        "vecs": V, "ones": np.ones((P, P), f), "ident": eye, "flip": np.ascontiguousarray(eye[::-1]), "win": win,
        "spread": np.kron(np.eye(16), np.ones((1, HD))).astype(f),
        "mask": np.where(i[None, :] > i[:, None], NEG, 0.0).astype(f),
        "wf": np.ascontiguousarray(fg.reshape(8, P, 8).transpose(1, 0, 2)),
        "ssm_bc": np.ascontiguousarray(np.stack([grp(x["ssm_b_re_2"]), grp(x["ssm_b_im_2"]),
                                                 grc(x["ssm_c_re_2"]), grc(x["ssm_c_im_2"])], 1)),
        "pT": np.ascontiguousarray(np.asarray(x["p_2"], f)[:, 0].transpose(0, 2, 1).reshape(2, 2, P, SEQ)
                                   .transpose(2, 0, 1, 3)),
        "rel": np.concatenate([np.asarray(x["rel_bias_2"], f), np.full((1, 8), NEG, f)]), "onehot": onehot.astype(f),
    }


def kernel(**inputs):
    import concourse.bacc as bacc
    from concourse.bass_utils import run_bass_kernel_spmd

    nc = bacc.Bacc("TRN2", target_bir_lowering=False, num_devices=1)
    arrays = lay_out(inputs)
    A = {n: nc.dram_tensor(f"in_{n}", a.shape, mybir.dt.from_np(a.dtype), kind="ExternalInput").ap()
         for n, a in arrays.items()}
    out = nc.dram_tensor("out", (P, KT, SEQ), F32, kind="ExternalOutput").ap()
    program(nc, A, out)
    got = run_bass_kernel_spmd(nc, [{f"in_{n}": a for n, a in arrays.items()}], core_ids=[0]).results[0]["out"]
    return np.ascontiguousarray(got.transpose(2, 1, 0).reshape(1, SEQ, D))
```

```python
from contextlib import ExitStack

import numpy as np

import concourse.bass as bass
from concourse import mybir

F32 = mybir.dt.float32
F32R = mybir.dt.float32r
BF16 = mybir.dt.bfloat16
ACT = mybir.ActivationFunctionType
ALU = mybir.AluOpType
AX_X = mybir.AxisListType.X

P = 128
D = 1024
KT = D // P
SEQ = 512
META = 16
TOK = META + SEQ
HALF = TOK // 2
HD = 64
FFT = 22
FFG = [8, 8, 6]
FFN_ORDER = [("up", 0, 0, 8), ("up", 1, 0, 2), ("down", 0, 0, 0), ("up", 1, 2, 8), ("up", 2, 0, 2), ("down", 1, 0, 0),
             ("up", 2, 2, 6), ("side", 0, 0, 0), ("down", 2, 0, 0)]
NEG = -1e30
LAM = 0.8 - 0.6 * float(np.exp(-0.3))
PI = float(np.pi)

U_QKVB = 0
U_CU = 16
U_OUT1 = 24
U_FF = 32
U_SSM = 96
U_GLU = 104
U_FFNA = 120
U_GATEA = 190
U_Q = 198
U_KV = 206
U_WO = 222
U_FFNB = 230
U_GATEB = 300
NU = 308


def column_map():
    at, cols = 0, {}
    for name, n in (
        ("norm_mix", 8), ("out_norm", 8), ("norm_mlp", 8), ("final_norm", 8), ("conv_w", 12), ("b_f", 1),
        ("ssm_norm", 8), ("kv_norm", 8), ("attn_norm", 8), ("k_norm", 1), ("q_norm", 1), ("subln", 1),
        ("ffn_norm0", 8), ("ffn_norm1", 8), ("ple_norm0", 8), ("ple_norm1", 8),
        ("ffn_w0", 132), ("ffn_w1", 132), ("ffn_b0", 44), ("ffn_b1", 44),
        ("lam_re", 32), ("lam_im", 32), ("log_dt", 32), ("ssm_d", 32), ("lambdas", 4),
    ):
        cols[name] = at
        at += n
    return cols, at


COL, NCOL = column_map()


class Unit:

    def __init__(self, c, i=0, step=4):
        self.c, self.i, self.step = c, i, step

    def n(self, k=0):
        return self.c + k + self.step * self.i

    def ahead(self, k):
        return Unit(self.c + k, self.i, self.step)

    @property
    def slot(self):
        return self.c % 4

    @property
    def round(self):
        return self.c // 2 + self.step // 2 * self.i


class Count:

    def __init__(self, sem):
        self.sem, self.base, self.i, self.rate = sem, 0, 0, 0

    def did(self, ins):
        ins.then_inc(self.sem, 1)
        self.base += 1
        return self.base + self.rate * self.i

    def loop(self, i, rate, first=0):
        self.i, self.rate, self.entered = i, rate, self.base
        self.base -= rate * first

    def leave(self, trips, first=0):
        got = self.base - self.entered + self.rate * first
        assert got == self.rate, ("rate", got, self.rate)
        self.base = self.entered + self.rate * (trips - first)
        self.i, self.rate = 0, 0


def ge(eng, sem, value):
    if not (isinstance(value, int) and value <= 0):
        eng.wait_ge(sem, value)


def one(t, k):
    return t[:, bass.ds(k, 1), :] if not isinstance(k, int) else t[:, k:k + 1, :]


def program(nc, A, out):
    with ExitStack() as ctx:
        build(nc, A, out, ctx)


def build(nc, A, out, ctx):
    def sb(name, shape, dt=F32, c=ctx):
        return c.enter_context(nc.sbuf_tensor(name, shape, dt))

    def sem(name):
        return ctx.enter_context(nc.semaphore(name))

    h = sb("h", [P, KT, TOK])
    with ExitStack() as c:
        a_hi = sb("a_hi", [P, KT, SEQ], F32R, c)
        a_lo = sb("a_lo", [P, KT, SEQ], F32R, c)
    with ExitStack() as c:
        u_t = sb("u_t", [P, 32, P], F32, c)
    with ExitStack() as c:
        qs = sb("qs", [P, 2, 2, SEQ], F32, c)
        ks = sb("ks", [P, 2, TOK], F32, c)
        vs = sb("vs", [P, 2, TOK], F32, c)
        vp = sb("vp", [P, 2, 4, 2, P], F32, c)
        vm = sb("vm", [META, 2, 2, P], F32, c)
        pt = sb("pt", [P, 2, 4, P], F32, c)
        ptm = sb("ptm", [META, 2, P], F32, c)
    with ExitStack() as c:
        qs2 = sb("qs2", [P, 2, 2, SEQ], F32, c)
        ks2 = sb("ks2", [P, 2, SEQ], F32, c)
        vs2 = sb("vs2", [P, 2, SEQ], F32, c)
        vtok = sb("vtok", [P, 2, 4, P], F32, c)
        pt2 = sb("pt2", [P, 2, 4, P], F32, c)
        b_hi = sb("b_hi", [P, 2, SEQ], F32R, c)
        b_lo = sb("b_lo", [P, 2, SEQ], F32R, c)
    sb("region_a", [P, 2 * KT * SEQ])
    state = sb("state", [P, 16, 32])
    pw_up = sb("pw_up", [P, 3, 32, 5])
    pw_dn = sb("pw_dn", [P, 2, 32, 4])
    raw = sb("raw", [P, 2, KT * P])
    w_hi = sb("w_hi", [P, 4, KT * P], F32R)
    w_lo = sb("w_lo", [P, 4, KT * P], F32R)
    vecs = sb("vecs", [P, NCOL])
    ones = sb("ones", [P, P])
    ident = sb("ident", [P, P])
    flip_r = sb("flip_r", [P, P], F32R)
    ident_b = sb("ident_b", [P, P], BF16)
    mask_b = sb("mask_b", [P, P], BF16)
    win = sb("win", [P, 64])
    eps5 = sb("eps5", [P, 1])
    eps6 = sb("eps6", [P, 1])
    eps_o = sb("eps_o", [P, 1])
    neg_lam = sb("neg_lam", [P, 1])
    rel = sb("rel", [33, 8])
    rt = sb("rt", [P, TOK])
    rstd = sb("rstd", [P, TOK])
    sq = sb("sq", [P, 2, TOK])
    t0 = sb("t0", [P, 2, TOK])
    t1 = sb("t1", [P, 2, TOK])
    t2 = sb("t2", [P, 2, TOK])
    small = sb("small", [P, 4, 8])

    with ExitStack() as c:
        x_hi = sb("x_hi", [P, KT, TOK], F32R, c)
        x_lo = sb("x_lo", [P, KT, TOK], F32R, c)
    with ExitStack() as c:
        v_b1 = sb("v_b1", [P, 2, 4, 4, 2, 16], F32, c)
        c_p1 = sb("c_p1", [P, 2, 4, 5, 2, 16], F32, c)
        c_p2 = sb("c_p2", [P, 2, 4, 5, 2, 16], F32, c)
        v_l = sb("v_l", [P, 2, 4, P], F32, c)
        t_l = sb("t_l", [P, 4, P], F32, c)
        x_s = sb("x_s", [P, 2, 4, P + 1], F32, c)
    sb("region_x", [P, 2 * KT * TOK])
    with ExitStack() as c:
        qkvb = sb("qkvb", [P, 16, TOK], F32, c)
        aug_q = sb("aug_q", [P, 2, 2, SEQ], F32, c)
        aug_k = sb("aug_k", [P, TOK], F32, c)
        cum8 = sb("cum8", [40, TOK], F32, c)
        spread1 = sb("spread1", [16, KT * P], F32, c)
        wf = sb("wf", [P, KT, 8], F32, c)
        mask = sb("mask", [P, P], F32, c)
        flip = sb("flip", [P, P], F32, c)
        wf_hi = sb("wf_hi", [P, KT, 8], F32R, c)
        wf_lo = sb("wf_lo", [P, KT, 8], F32R, c)

    with ExitStack() as c:
        e_r = sb("e_r", [P, 32, P], F32, c)
        e_i = sb("e_i", [P, 32, P], F32, c)
        c_raw = sb("c_raw", [P, 2, 32, 16], F32, c)
        bb = sb("bb", [P, 2, 32, 16], F32, c)
        with ExitStack() as cc:
            b_in_ = sb("b_in_", [P, 2, 32, 16], F32, cc)
            ctmp = sb("ctmp", [P, 4, SEQ], F32, cc)
        with ExitStack() as cc:
            v_b0 = sb("v_b0", [P, 2, 4, 4, 2, 16], F32, cc)
            c_p0 = sb("c_p0", [P, 2, 4, 5, 2, 16], F32, cc)
            mtmp = sb("mtmp", [P, 4, 320], F32, cc)
    with ExitStack() as c:
        q2 = sb("q2", [P, 8, SEQ], F32, c)
        k2 = sb("k2", [P, 8, SEQ], F32, c)
        v2 = sb("v2", [P, 8, SEQ], F32, c)
        spread2 = sb("spread2", [16, KT * P], F32, c)
        with ExitStack() as cc:
            b_raw = sb("b_raw", [P, 1, SEQ], F32, cc)
        tab = sb("tab", [8, 640], F32, c)
    with ExitStack() as c:
        with ExitStack() as cc:
            pp = sb("pp", [P, 8, SEQ], F32, cc)
        a2_hi = sb("a2_hi", [P, KT, SEQ], F32R, c)
        a2_lo = sb("a2_lo", [P, KT, SEQ], F32R, c)
        p_raw = sb("p_raw", [P, 2, SEQ], F32, c)
        p_hi = sb("p_hi", [P, 2, SEQ], F32R, c)
        p_lo = sb("p_lo", [P, 2, SEQ], F32R, c)
    V_B, C_P = (v_b0, v_b1), (c_p0, c_p1, c_p2)
    onehot = t1.rearrange("p a b -> p (a b)")[0:33, 0:640]
    scratch = nc.dram_tensor("scratch", (8, 640), F32, kind="Internal").ap()

    ps = ctx.enter_context(nc.psum_tensor("ps", [P, 8, SEQ], F32))

    consts_in = sem("consts_in")
    first_in = sem("first_in")
    h_in = [sem(f"h_in{k}") for k in range(4)]
    raw_in = [sem(f"raw_in{k}") for k in range(2)]
    hi_ok = sem("hi_ok")
    lo_ok = sem("lo_ok")
    unit_mm = sem("unit_mm")
    unit_ev = sem("unit_ev")
    h_fin = sem("h_fin")
    sq_ok = sem("sq_ok")
    stat_mm = sem("stat_mm")
    xhi_ok = sem("xhi_ok")
    xlo_ok = sem("xlo_ok")
    rt_ok = sem("rt_ok")
    rstd_ok = sem("rstd_ok")
    consts_ok = sem("consts_ok")
    wf_ok = sem("wf_ok")
    wflo_ok = sem("wflo_ok")
    f_mm = sem("f_mm")
    f_act = sem("f_act")
    f_ok = sem("f_ok")
    staged = sem("staged")
    vt_mm = sem("vt_mm")
    vt_ok = sem("vt_ok")
    s_mm = sem("s_mm")
    nb_ok = sem("nb_ok")
    exp_ok = sem("exp_ok")
    nrm_ok = sem("nrm_ok")
    vz_ok = sem("vz_ok")
    qz_ok = sem("qz_ok")
    pt_mm = sem("pt_mm")
    pt_ok = sem("pt_ok")
    ptm_ok = sem("ptm_ok")
    pv_mm = sem("pv_mm")
    y_ok = sem("y_ok")
    hn_sq = sem("hn_sq")
    hn_mm = sem("hn_mm")
    hn_rt = sem("hn_rt")
    hn_inv = sem("hn_inv")
    hn_b = sem("hn_b")
    hn_y = sem("hn_y")
    hn_hi = sem("hn_hi")
    hn_lo = sem("hn_lo")
    ay_ok = sem("ay_ok")
    ahi_ok = sem("ahi_ok")
    alo_ok = sem("alo_ok")
    dve_did = sem("dve_did")
    act_did = sem("act_did")
    pool_did = sem("pool_did")
    pool = Count(pool_did)
    dve = Count(dve_did)
    act = Count(act_did)
    ut_a = sem("ut_a")
    ut_p = sem("ut_p")
    par_v = sem("par_v")
    par_a = sem("par_a")
    bc_in = sem("bc_in")
    den_ok = sem("den_ok")
    inv_ok = sem("inv_ok")
    dt_ok = sem("dt_ok")
    pads_ok = sem("pads_ok")
    tables_ok = sem("tables_ok")
    vb_ok = sem("vb_ok")
    cp_ok = sem("cp_ok")
    vb_mm = sem("vb_mm")
    g_mm = sem("g_mm")
    vl_ok = sem("vl_ok")
    tl_ok = sem("tl_ok")
    v_mm = sem("v_mm")
    v_ev = sem("v_ev")
    xs_ok = sem("xs_ok")
    y_mm = sem("y_mm")
    ys_ok = sem("ys_ok")
    ge_ok = sem("ge_ok")
    g_hi = sem("g_hi")
    g_lo = sem("g_lo")
    sig_ok = sem("sig_ok")
    c0_ok = sem("c0_ok")
    cg_ok = sem("cg_ok")
    gel_ok = sem("gel_ok")
    p_in = sem("p_in")
    phi_ok = sem("phi_ok")
    plo_ok = sem("plo_ok")
    tab_in = sem("tab_in")
    tab_mm = sem("tab_mm")
    tab_ok = sem("tab_ok")
    tab_out = sem("tab_out")
    b_in = sem("b_in")
    bhi_ok = sem("bhi_ok")
    blo_ok = sem("blo_ok")
    lam_v = sem("lam_v")
    lam_mm = sem("lam_mm")
    lam_a = sem("lam_a")
    v2_ok = sem("v2_ok")
    qz2_ok = sem("qz2_ok")
    cv_ok = sem("cv_ok")
    sg_ok = sem("sg_ok")
    sgu_ok = sem("sgu_ok")
    o_ok = sem("o_ok")
    fence_at = sem("fence_at")
    stored = sem("stored")

    REAL = slice(META, TOK)

    def vec(name, k=0, lo=0, n=P):
        k = COL[name] + k
        return vecs[lo:lo + n, k:k + 1] if isinstance(k, int) else vecs[lo:lo + n, bass.ds(k, 1)]

    def halves(t):
        return t.rearrange("p (a b) -> p a b", a=2)

    def fence(e, k):
        e.drain().then_inc(fence_at, 1)
        e.wait_ge(fence_at, 4 * k)

    def load_unit(e, u):
        if not (isinstance(u.i, int) and u.n() < 2):
            e.wait_ge(lo_ok, u.n(-1))
        n = u.n()
        src = A["wstream"][bass.ds(n * P, P), :] if not isinstance(n, int) else A["wstream"][n * P:n * P + P, :]
        e.dma_start(raw[:, u.c % 2, :], src).then_inc(raw_in[u.c % 2], 16)

    def split_hi(e, u):
        e.wait_ge(raw_in[u.c % 2], 16 * (u.round + 1))
        if not (isinstance(u.i, int) and u.n() < 4):
            e.wait_ge(unit_mm, u.n(-3))
        e.activation(w_hi[:, u.slot, :], raw[:, u.c % 2, :], ACT.Copy).then_inc(hi_ok, 1)

    def split_lo(e, u):
        e.wait_ge(hi_ok, u.n(1))
        e.tensor_tensor(w_lo[:, u.slot, :], raw[:, u.c % 2, :], w_hi[:, u.slot, :], ALU.subtract)\
            .then_inc(lo_ok, 1)

    def split_ahead(e, u, split):
        if not (isinstance(u.i, int) and u.n() + 2 >= NU):
            split(e, u.ahead(2))

    def products(e, u, bank, hi, lo, k0=0, kt=KT, w0=0, ready=None):
        for k in range(kt):
            w = slice((w0 + k) * P, (w0 + k + 1) * P)
            if ready:
                ready(e, k)
            for n, (wt, x) in enumerate(((w_hi, hi), (w_hi, lo), (w_lo, hi))):
                last = e.matmul(ps[:, bank, :], wt[:, u.slot, w], x[:, k0 + k, 0:SEQ],
                                start=(k == 0 and n == 0), stop=(k == kt - 1 and n == 2))
        return last

    def unit_pe(e, u, hi, lo, ready=None, kt=KT):
        e.wait_ge(lo_ok, u.n(1))
        e.wait_ge(unit_ev, u.n(-3))
        products(e, u, u.slot, hi, lo, kt=kt, ready=ready).then_inc(unit_mm, 1)

    XN = {0: 0, 1: 1, 3: 2, 4: 3, 5: 4, 6: 5, 7: 7, 8: 8}

    def stat_pe(e, n, m, cols=SEQ):
        e.wait_ge(sq_ok, 8 * n + m + 1)
        if n and m == 0:
            e.wait_ge(rt_ok, n)
        for half in range(2 if cols > SEQ else 1):
            w = HALF if cols > SEQ else SEQ
            last = e.matmul(ps[:, 4 + half, 0:w], ones[:, :], sq[:, m % 2, half * HALF:half * HALF + w],
                            start=(m == 0), stop=(m == KT - 1))
        last.then_inc(stat_mm, 1)

    def norm_act(e, n, m, gain, cols=SEQ, x_hi=x_hi):
        src = h[:, m, TOK - cols:TOK]
        if 8 * n + m >= 2:
            e.wait_ge(stat_mm, 8 * n + m - 1)
        e.activation(sq[:, m % 2, 0:cols], src, ACT.Square).then_inc(sq_ok, 1)
        if gain:
            x_act(e, n, m, gain, cols)

    def x_act(e, n, m, gain, cols=SEQ, hi=x_hi):
        src = h[:, m, TOK - cols:TOK]
        e.activation(hi[:, m, 0:cols], src, ACT.Copy, scale=vec(gain, m)).then_inc(xhi_ok, 1)

    def x_dve(e, xn, m, gain, cols=SEQ, hi=x_hi, lo=x_lo):
        src = h[:, m, TOK - cols:TOK]
        e.wait_ge(xhi_ok, 8 * xn + m + 1)
        e.scalar_tensor_tensor(lo[:, m, 0:cols], src, vec(gain, m), hi[:, m, 0:cols], ALU.mult,
                               ALU.subtract).then_inc(xlo_ok, 1)

    def root_act(e, n, eps, cols=SEQ):
        e.wait_ge(stat_mm, 8 * (n + 1))
        if n:
            e.wait_ge(rstd_ok, n)
        if cols > SEQ:
            o, i = halves(rt[:, :]), ps[:, 4:6, 0:HALF]
        else:
            o, i = rt[:, 0:cols], ps[:, 4, 0:cols]
        e.activation(o, i, ACT.Sqrt, bias=eps[:, 0:1], scale=1.0 / D).then_inc(rt_ok, 1)

    def root_dve(e, n, cols=SEQ):
        e.wait_ge(rt_ok, n + 1)
        e.reciprocal(rstd[:, 0:cols], rt[:, 0:cols]).then_inc(rstd_ok, 1)
        e.wait_ge(rstd_ok, n + 1)

    roots = t2[0:16, 0, 0:SEQ]

    def head_sq(e, k, y):
        if k >= 2:
            e.wait_ge(hn_mm, k - 1)
        e.activation(sq[:, k % 2, 0:SEQ], y, ACT.Square).then_inc(hn_sq, 1)

    def head_pe(e, k, w=0):
        m = k % 8
        e.wait_ge(hn_sq, k + 1)
        if m == 0:
            ge(e, hn_rt, k // 8)
        e.matmul(ps[0:16, 5, :], win[:, 32 * w + 15 - 2 * m:32 * w + 31 - 2 * m], sq[:, k % 2, 0:SEQ],
                 start=(m == 0), stop=(m == 7)).then_inc(hn_mm, 1)

    def head_root(e, b, n, eps):
        e.wait_ge(hn_mm, 8 * b + 8)
        ge(e, hn_b, 8 * b)
        e.activation(roots, ps[0:16, 5, :], ACT.Sqrt, bias=eps[0:16, 0:1], scale=1.0 / n).then_inc(hn_rt, 1)

    def head_inverse(e, b):
        e.wait_ge(hn_rt, b + 1)
        e.reciprocal(roots, roots).then_inc(hn_inv, 1)

    def head_spread(e, k):
        m = k % 8
        e.wait_ge(hn_inv, k // 8 + 1)
        if k == 8:
            e.wait_ge(tab_ok, 2)
        ge(e, hn_y, k - 1)
        e.matmul(ps[:, 6 + k % 2, :], (spread1 if k < 8 else spread2)[:, m * P:(m + 1) * P],
                 roots, start=True, stop=True).then_inc(hn_b, 1)

    def head_scale(e, k, y, gain, to=None):
        e.wait_ge(hn_b, k + 1)
        if to is None and k >= 2:
            e.wait_ge(hn_lo, HNX(k) - 1)
        to = t0[:, k % 2, 0:SEQ] if to is None else to
        e.scalar_tensor_tensor(to, y, gain, ps[:, 6 + k % 2, :], ALU.mult, ALU.mult).then_inc(hn_y, 1)

    def HNX(k):
        return k if k < 8 else k - 16

    def head_hi(e, k, m):
        e.wait_ge(hn_y, k + 1)
        e.activation(a_hi[:, m, :], t0[:, k % 2, 0:SEQ], ACT.Copy).then_inc(hn_hi, 1)

    def head_lo(e, k, m):
        e.wait_ge(hn_hi, HNX(k) + 1)
        e.wait_ge(hn_y, k + 1)
        e.tensor_tensor(a_lo[:, m, :], t0[:, k % 2, 0:SEQ], a_hi[:, m, :], ALU.subtract).then_inc(hn_lo, 1)

    def wide_pe(e, u):
        e.wait_ge(lo_ok, u.n(1))
        if not (isinstance(u.i, int) and u.n() < 2):
            e.wait_ge(unit_ev, u.n(-1))
        b = 2 * (u.slot % 2)
        for k in range(KT):
            w = slice(k * P, (k + 1) * P)
            if isinstance(u.i, int) and u.n() == 0:
                if k < 4:
                    stat_pe(e, 0, k + 4, TOK)
                e.wait_ge(xlo_ok, k + 1)
            for n, (wt, x) in enumerate(((w_hi, x_hi), (w_hi, x_lo), (w_lo, x_hi))):
                for half in range(2):
                    last = e.matmul(ps[:, b + half, 0:HALF], wt[:, u.slot, w],
                                    x[:, k, half * HALF:(half + 1) * HALF],
                                    start=(k == 0 and n == 0), stop=(k == KT - 1 and n == 2))
        last.then_inc(unit_mm, 1)

    def wide_dve(e, u, to):
        e.wait_ge(unit_mm, u.n(1))
        b = 2 * (u.slot % 2)
        e.tensor_tensor(halves(to), ps[:, b:b + 2, 0:HALF], halves(rstd[:, :]), ALU.mult).then_inc(unit_ev, 1)

    def f_pe(e):
        e.wait_ge(wflo_ok, 1)
        for k in range(KT):
            for n, (wt, x) in enumerate(((wf_hi, x_hi), (wf_hi, x_lo), (wf_lo, x_hi))):
                for half in range(2):
                    last = e.matmul(ps[0:8, 6 + half, 0:HALF], wt[:, k, :], x[:, k, half * HALF:(half + 1) * HALF],
                                    start=(k == 0 and n == 0), stop=(k == KT - 1 and n == 2))
        last.then_inc(f_mm, 1)

    def f_dve(e):
        z, az, ls = t0[0:8, 0, :], t0[0:8, 1, :], t1[0:8, 0, :]
        e.wait_ge(f_mm, 1)
        n = dve.did(e.tensor_tensor(halves(az), ps[0:8, 6:8, 0:HALF], halves(rstd[0:8, :]), ALU.mult))
        e.wait_ge(dve_did, n)
        e.tensor_scalar(z, az, vec("b_f", 0, 0, 8), None, ALU.add).then_inc(f_ok, 1)
        e.wait_ge(f_act, 1)
        n = dve.did(e.scalar_tensor_tensor(ls, z, 0.0, t1[0:8, 1, :], ALU.min, ALU.subtract))
        e.wait_ge(dve_did, n)
        e.wait_ge(consts_ok, 1)
        n = dve.did(e.tensor_tensor_scan(cum8[0:8, :], t2[0:8, 0, :], ls, 0.0, ALU.mult, ALU.add))
        e.wait_ge(dve_did, n)
        e.tensor_scalar(aug_k[0:8, :], cum8[0:8, :], -1.0, None, ALU.mult).then_inc(f_ok, 1)
        e.tensor_copy(cum8[32:40, :], cum8[0:8, :]).then_inc(f_ok, 1)

    def f_scalar(e):
        e.wait_ge(f_ok, 1)
        n = act.did(e.activation(t0[0:8, 1, :], t0[0:8, 0, :], ACT.Abs))
        e.wait_ge(act_did, n)
        n = act.did(e.activation(t1[0:8, 0, :], t0[0:8, 1, :], ACT.Exp, scale=-1.0))
        e.wait_ge(act_did, n)
        e.activation(t1[0:8, 1, :], t1[0:8, 0, :], ACT.Ln, bias=1.0).then_inc(f_act, 1)

    def conv_dve(e, u, s):
        k = s // 2
        if s % 2 == 0:
            wide_dve(e, u, t0[:, k, :])
            return
        wide_dve(e, u, t1[:, k, :])
        j = 2 * u.i + k
        e.wait_ge(unit_ev, u.n(1))
        n = dve.did(e.tensor_tensor(t2[:, k, :], t0[:, k, :], t1[:, k, :], ALU.mult))
        e.wait_ge(dve_did, n)
        n = dve.did(e.tensor_scalar(t0[:, k, 0:SEQ], t2[:, k, 16:528], vec("conv_w", 8 + j), None, ALU.mult))
        e.wait_ge(dve_did, n)
        n = dve.did(e.scalar_tensor_tensor(t1[:, k, 0:SEQ], t2[:, k, 15:527], vec("conv_w", 4 + j),
                                           t0[:, k, 0:SEQ], ALU.mult, ALU.add))
        e.wait_ge(dve_did, n)
        n = dve.did(e.scalar_tensor_tensor(t0[:, k, 0:SEQ], t2[:, k, 14:526], vec("conv_w", j),
                                           t1[:, k, 0:SEQ], ALU.mult, ALU.add))
        e.wait_ge(dve_did, n)
        b = qkvb[:, bass.ds(12 + j, 1), REAL] if not isinstance(j, int) else qkvb[:, 12 + j:13 + j, REAL]
        n = dve.did(e.tensor_tensor(b, b, t0[:, k:k + 1, 0:SEQ], ALU.mult))

    def tile_of(t, k, cols=slice(None), rows=slice(None)):
        return t[rows, k:k + 1, cols] if isinstance(k, int) else t[rows, bass.ds(k, 1), cols]

    def stage1_pool(e, i):
        for par in range(2):
            p = 2 * i + par
            if p >= 2:
                e.wait_ge(s_mm, 8 * (p - 1))
                e.wait_ge(vt_mm, p - 1)
            k = 8 * p
            for hh in range(2):
                r = slice(HD * hh, HD * hh + HD)
                ge(e, staged, k + hh)
                e.tensor_scalar(qs[r, par, hh:hh + 1, :], tile_of(qkvb, p, REAL, r), HD ** -0.5, None, ALU.mult)\
                    .then_inc(staged, 1)
            e.wait_ge(staged, k + 2)
            e.tensor_copy(ks[:, par:par + 1, :], tile_of(qkvb, 4 + p)).then_inc(staged, 1)
            e.wait_ge(staged, k + 3)
            e.tensor_copy(vs[:, par:par + 1, :], tile_of(qkvb, 8 + p)).then_inc(staged, 1)
            for hh in range(2):
                hd = 2 * p + hh
                pick = lambda lo, c: (ident[lo:lo + 8, c:c + 1] if isinstance(c, int)
                                      else ident[lo:lo + 8, bass.ds(c, 1)]).to_broadcast([8, SEQ])
                e.wait_ge(staged, k + 4 + 2 * hh)
                e.tensor_copy(aug_q[0:8, par, hh, :], pick(0, hd)).then_inc(staged, 1)
                e.wait_ge(staged, k + 5 + 2 * hh)
                e.tensor_tensor(aug_q[32:40, par, hh, :], cum8[32:40, REAL], pick(32, 32 + hd), ALU.mult)\
                    .then_inc(staged, 1)

    def values_pe(e, p):
        par = p % 2
        e.wait_ge(staged, 8 * p + 8)
        ge(e, y_ok, p - 1)
        ge(e, vt_ok, 4 * p)
        ge(e, ptm_ok, 8 * p - 1)
        for j in range(4):
            e.transpose(ps[:, 6 + par, j * P:(j + 1) * P], vs[:, par, META + j * P:META + (j + 1) * P], ident[:, :])
        e.transpose(ps[0:META, 0, P:2 * P], vs[:, par, 0:META], ident[:, :]).then_inc(vt_mm, 1)

    def values_act(e, p):
        par = p % 2
        e.wait_ge(vt_mm, p + 1)
        ge(e, pv_mm, 8 * (p - 1))
        t = ps[:, 6 + par, :].rearrange("p (j c) -> p j c", j=4)
        for hh in range(2):
            c = slice(HD * hh, HD * hh + HD)
            e.activation(vm[:, par, hh, c], ps[0:META, 0, P + HD * hh:P + HD * hh + HD], ACT.Copy).then_inc(vt_ok, 1)
        for hh in range(2):
            c = slice(HD * hh, HD * hh + HD)
            e.activation(vp[:, par, :, hh, c], t[:, :, c], ACT.Copy).then_inc(vt_ok, 1)

    def scores1_pe(e, g):
        p, w = g // 8, g % 8
        par, qt, hh, sl = p % 2, w // 2, w % 2, w % 2
        ge(e, exp_ok, g - 1)
        if w == 0:
            e.wait_ge(vt_ok, 4 * p + 2)
        ge(e, ptm_ok, g - 1)
        A_, B = 2 * sl, 2 * sl + 1
        q = qs[:, par, hh, qt * P:(qt + 1) * P]
        aq = aug_q[:, par, hh, qt * P:(qt + 1) * P]
        N = (qt + 1) * P
        e.matmul(ps[:, A_, SEQ - META:SEQ], q, ks[:, par, 0:META], start=True, stop=False)
        e.matmul(ps[:, A_, SEQ - META:SEQ], aq, aug_k[:, 0:META], start=False, stop=True)
        e.matmul(ps[:, B, 0:N], q, ks[:, par, META:META + N], start=True, stop=False)
        e.matmul(ps[:, B, 0:N], aq, aug_k[:, META:META + N], start=False, stop=False)
        e.matmul(ps[:, B, N - P:N], ident_b[:, :], mask_b[:, :], start=False, stop=True).then_inc(s_mm, 1)

    def turn1_pe(e, g):
        qt, sl = g % 8 // 2, g % 2
        e.wait_ge(nrm_ok, g + 1)
        for j in range(qt + 1):
            e.transpose(ps[:, 4 + sl, j * P:(j + 1) * P], t0[:, sl, META + j * P:META + (j + 1) * P], ident[:, :])
        e.transpose(ps[0:META, 2 * sl, 0:P], t0[:, sl, 0:META], ident[:, :]).then_inc(pt_mm, 1)

    def pv1_pe(e, g):
        p, w = g // 8, g % 8
        par, qt, hh, sl = p % 2, w // 2, w % 2, w % 2
        e.wait_ge(pt_ok, g + 1)
        e.wait_ge(ptm_ok, g + 1)
        if w == 0:
            e.wait_ge(vt_ok, 4 * p + 4)
        o = ps[:, 6 + par, qt * P:(qt + 1) * P]
        for j in range(qt + 1):
            e.matmul(o, vp[:, par, j, hh, :], pt[:, sl, j, :], start=(hh == 0 and j == 0), stop=False)
        e.matmul(o, vm[:, par, hh, :], ptm[:, sl, :], start=False, stop=(hh == 1)).then_inc(pv_mm, 1)

    def attention1_pe(e):
        for g in range(32 + 2):
            if g < 32:
                if g % 8 == 0:
                    values_pe(e, g // 8)
                scores1_pe(e, g)
            if 1 <= g < 33:
                turn1_pe(e, g - 1)
            if g >= 2:
                pv1_pe(e, g - 2)

    def scores_flat(sl):
        return ps[:, 2 * sl:2 * sl + 2, :].rearrange("p a b -> p (a b)")

    def attention1_dve(e):
        def top(g):
            qt, sl = g % 8 // 2, g % 2
            e.wait_ge(s_mm, g + 1)
            s = scores_flat(sl)[:, SEQ - META:SEQ + (qt + 1) * P]
            e.reduce_max(small[:, 1, sl:sl + 1], s, AX_X, negate=True).then_inc(nb_ok, 1)

        def normalise(g):
            qt, sl = g % 8 // 2, g % 2
            N = META + (qt + 1) * P
            e.wait_ge(exp_ok, g + 1)
            n = dve.did(e.reciprocal(small[:, 3, sl:sl + 1], small[:, 2, sl:sl + 1]))
            e.wait_ge(dve_did, n)
            e.tensor_scalar(t0[:, sl, 0:N], t0[:, sl, 0:N], small[:, 3, sl:sl + 1], None, ALU.mult)\
                .then_inc(nrm_ok, 1)

        for g in range(32 + 2):
            if 1 <= g < 33:
                normalise(g - 1)
            if g < 32:
                top(g)
            if 1 <= g < 33:
                k = g - 1
                e.wait_ge(pt_mm, k + 1)
                ge(e, pv_mm, k - 1)
                e.tensor_copy(ptm[:, k % 2, :], ps[0:META, 2 * (k % 2), 0:P]).then_inc(ptm_ok, 1)
            if g >= 9 and g % 8 == 1:
                p = g // 8 - 1
                e.wait_ge(pv_mm, 8 * p + 8)
                e.tensor_copy(qkvb[:, p, REAL], ps[:, 6 + p % 2, :]).then_inc(y_ok, 1)

    def attention1_act(e):
        def exps(g):
            qt, sl = g % 8 // 2, g % 2
            e.wait_ge(nb_ok, g + 1)
            ge(e, pt_mm, g - 1)
            ge(e, nrm_ok, g - 1)
            N = META + (qt + 1) * P
            e.activation(t0[:, sl, 0:N], scores_flat(sl)[:, SEQ - META:SEQ + (qt + 1) * P], ACT.Exp,
                         bias=small[:, 1, sl:sl + 1], accum_out=small[:, 2, sl:sl + 1]).then_inc(exp_ok, 1)

        def turned(g):
            qt, sl = g % 8 // 2, g % 2
            N = (qt + 1) * P
            e.wait_ge(pt_mm, g + 1)
            ge(e, pv_mm, g - 1)
            e.activation(pt[:, sl, 0:qt + 1, :].rearrange("p j c -> p (j c)"), ps[:, 4 + sl, 0:N], ACT.Copy)\
                .then_inc(pt_ok, 1)

        for g in range(32 + 1):
            if g < 32:
                if g % 8 == 0:
                    values_act(e, g // 8)
                exps(g)
            if g >= 1:
                turned(g - 1)

    def y_tile(m):
        return qkvb[:, m if m < 4 else m + 8, REAL]

    def relu2_dve(e, u, s):
        e.wait_ge(unit_mm, u.n(1))
        k = s % 2
        e.tensor_tensor(t0[:, k, 0:SEQ], ps[:, u.slot, :], rstd[:, 0:SEQ], ALU.mult).then_inc(unit_ev, 1)
        ge(e, alo_ok, 8 * u.i + s - 1)
        e.wait_ge(unit_ev, u.n(1))
        e.scalar_tensor_tensor(t1[:, k, 0:SEQ], t0[:, k, 0:SEQ], 0.0, t0[:, k, 0:SEQ], ALU.max, ALU.mult)\
            .then_inc(ay_ok, 1)

    def hidden_hi(e, n, m):
        e.wait_ge(ay_ok, n + 1)
        e.activation(a_hi[:, m, :], t1[:, m % 2, 0:SEQ], ACT.Copy).then_inc(ahi_ok, 1)

    def hidden_lo(e, n, m):
        e.wait_ge(ahi_ok, n + 1)
        e.tensor_tensor(a_lo[:, m, :], t1[:, m % 2, 0:SEQ], a_hi[:, m, :], ALU.subtract).then_inc(alo_ok, 1)

    def add_dve(e, u, m, final=False):
        e.wait_ge(unit_mm, u.n(1))
        e.wait_ge(unit_ev, u.n())
        i = e.tensor_tensor(h[:, m, REAL], h[:, m, REAL], ps[:, u.slot, :], ALU.add)
        i.then_inc(unit_ev, 1)


    def units(e, u0, trips, body, first=0, cycle=4, counts=None, rate=0):
        for i in range(first):
            for s in range(cycle):
                body(Unit(u0 + s, i, cycle), s)
        if trips > first:
            with e.Fori(first, trips) as i:
                if counts:
                    counts.loop(i, rate, first)
                for s in range(cycle):
                    body(Unit(u0 + s, i, cycle), s)
            if counts:
                counts.leave(trips, first)

    def spread_u(e, u, m, q, j, who):
        src = t0[32 * q:32 * q + 32, m % 2 if isinstance(m, int) else u.slot % 2, 0:SEQ]
        src = src.rearrange("p (c j) -> p j c", j=4)[:, j:j + 1, :]
        k = 4 * m + q
        dst = u_t[32 * j:32 * j + 32, bass.ds(k, 1), :] if not isinstance(k, int) else u_t[32 * j:32 * j + 32, k:k + 1, :]
        return (e.activation(dst, src, ACT.Copy) if who == "a" else e.tensor_copy(dst, src))

    def cmul(e, n, out_r, out_i, a, b, tmp, sign=1):
        ar, ai = a
        br, bi = b
        ta, tb, tc, td = tmp
        n.did(e.tensor_tensor(ta, ar, br, ALU.mult))
        n.did(e.tensor_tensor(tb, ai, bi, ALU.mult))
        n.did(e.tensor_tensor(tc, ar, bi, ALU.mult))
        k = n.did(e.tensor_tensor(td, ai, br, ALU.mult))
        e.wait_ge(n.sem, k)
        n.did(e.tensor_tensor(out_r, ta, tb, ALU.subtract if sign > 0 else ALU.add))
        k = n.did(e.tensor_tensor(out_i, tc, td, ALU.add if sign > 0 else ALU.subtract))
        e.wait_ge(n.sem, k)

    S = lambda k: state[:, k, :]
    T4 = lambda w: [t[:, s, 0:w] for t in (t0, t1) for s in range(2)]
    V_DT, V_MAG, V_TH, V_K, V_R, V_SH, V_SIN, V_COS, V_AR, V_AI, V_FR, V_FI, V_M4, V_T, V_W, V_Z = range(16)

    def system_dve(e):
        e.wait_ge(den_ok, 1)
        e.reciprocal(S(V_Z), S(V_T)).then_inc(inv_ok, 1)

    def system_pool(e):
        lr = vecs[:, COL["lam_re"]:COL["lam_re"] + 32]
        li = vecs[:, COL["lam_im"]:COL["lam_im"] + 32]

        def do(ins):
            e.wait_ge(pool_did, pool.did(ins))

        tt = lambda o, a, b, op: do(e.tensor_tensor(o, a, b, op))
        ts = lambda o, a, x, y, op0, op1: do(e.tensor_scalar(o, a, x, y, op0, op1))
        e.wait_ge(first_in, 32)
        e.wait_ge(consts_ok, 6)
        tt(S(V_T), lr, lr, ALU.mult)
        tt(S(V_W), li, li, ALU.mult)
        e.tensor_tensor(S(V_T), S(V_T), S(V_W), ALU.add).then_inc(den_ok, 1)
        e.wait_ge(dt_ok, 1)
        e.tensor_tensor(S(V_SH), lr, S(V_DT), ALU.mult).then_inc(par_v, 1)
        tt(S(V_TH), li, S(V_DT), ALU.mult)
        magic = 1.5 * 2.0 ** 23
        ts(S(V_K), S(V_TH), 1.0 / (2 * PI), magic, ALU.mult, ALU.add)
        ts(S(V_K), S(V_K), magic, None, ALU.subtract, ALU.bypass)
        c1 = 6.28125
        c2 = float((np.float32(2 * np.pi - c1).view(np.uint32) & np.uint32(0xFFFFF000)).view(np.float32))
        c3 = float(np.float32(2 * np.pi - c1 - c2))
        do(e.tensor_copy(S(V_R), S(V_TH)))
        for c in (c1, c2, c3):
            ts(S(V_W), S(V_K), -c, None, ALU.mult, ALU.bypass)
            tt(S(V_R), S(V_R), S(V_W), ALU.add)
        lim = float(np.nextafter(np.float32(np.pi), np.float32(0)))
        e.tensor_scalar(S(V_R), S(V_R), lim, -lim, ALU.min, ALU.max).then_inc(par_v, 1)
        e.wait_ge(par_a, 3)
        tt(S(V_COS), S(V_COS), S(V_COS), ALU.mult)
        ts(S(V_COS), S(V_COS), -2.0, 1.0, ALU.mult, ALU.add)
        tt(S(V_AR), S(V_MAG), S(V_COS), ALU.mult)
        tt(S(V_AI), S(V_MAG), S(V_SIN), ALU.mult)
        e.wait_ge(inv_ok, 1)
        ts(S(V_W), S(V_AR), -1.0, None, ALU.add, ALU.bypass)
        tt(S(V_FR), S(V_W), lr, ALU.mult)
        tt(S(V_T), S(V_AI), li, ALU.mult)
        tt(S(V_FR), S(V_FR), S(V_T), ALU.add)
        tt(S(V_FR), S(V_FR), S(V_Z), ALU.mult)
        tt(S(V_FI), S(V_AI), lr, ALU.mult)
        tt(S(V_T), S(V_W), li, ALU.mult)
        tt(S(V_FI), S(V_FI), S(V_T), ALU.subtract)
        tt(S(V_FI), S(V_FI), S(V_Z), ALU.mult)
        tt(S(V_T), S(V_MAG), S(V_MAG), ALU.mult)
        tt(S(V_M4), S(V_T), S(V_T), ALU.mult)
        up = lambda k, n: pw_up[:, k, :, n]
        do(e.memset(up(0, 0), 1.0))
        do(e.memset(up(1, 0), 0.0))
        do(e.tensor_copy(up(0, 1), S(V_AR)))
        do(e.tensor_copy(up(1, 1), S(V_AI)))
        small4 = [S(k) for k in (V_TH, V_K, V_R, V_SH)]
        for n, (a, b) in {2: (1, 1), 3: (2, 1), 4: (2, 2)}.items():
            cmul(e, pool, up(0, n), up(1, n), (up(0, a), up(1, a)), (up(0, b), up(1, b)), small4)
        ts(pw_up[:, 2, :, :], pw_up[:, 1, :, :], -1.0, None, ALU.mult, ALU.bypass)
        for j in range(4):
            do(e.tensor_copy(pw_dn[:, :, :, j], pw_up[:, 0:2, :, 3 - j]))

    def tables_pool(e):
        small4 = [S(k) for k in (V_TH, V_K, V_R, V_SH)]

        def do(ins):
            e.wait_ge(pool_did, pool.did(ins))

        e.wait_ge(bc_in, 32)
        bc = lambda k: S(k).unsqueeze(2).to_broadcast([P, 32, 16])
        cmul(e, pool, bb[:, 0, :, :], bb[:, 1, :, :], (bc(V_FR), bc(V_FI)), (b_in_[:, 0, :, :], b_in_[:, 1, :, :]),
             [ctmp[:, k, :].rearrange("p (q c) -> p q c", c=16) for k in range(4)])

        def square():
            c, i = S(V_COS), S(V_SIN)
            cmul(e, pool, S(V_T), S(V_W), (c, i), (c, i), small4)
            unit_length(e, S(V_T), S(V_W), S(V_Z), S(V_K))
            do(e.tensor_copy(c, S(V_T)))
            do(e.tensor_copy(i, S(V_W)))

        square()
        square()
        do(e.memset(e_r[:, :, 0:1], 1.0))
        do(e.memset(e_i[:, :, 0:1], 0.0))
        n = 1
        while n < P:
            per = min(32, SEQ // n)
            for q in range(0, 32, per):
                w = [ctmp[:, k, 0:per * n].rearrange("p (q c) -> p q c", c=n) for k in range(4)]
                b = [S(k)[:, q:q + per].unsqueeze(2).to_broadcast([P, per, n]) for k in (V_COS, V_SIN)]
                cmul(e, pool, e_r[:, q:q + per, n:2 * n], e_i[:, q:q + per, n:2 * n],
                     (e_r[:, q:q + per, 0:n], e_i[:, q:q + per, 0:n]), b, w)
            n *= 2
            if n < P:
                square()
        e.memset(v_b0[:, :, :, :, :, :], 0.0).then_inc(pads_ok, 1)
        e.memset(c_p0[:, :, :, :, :, :], 0.0).then_inc(pads_ok, 1)
        e.wait_ge(pads_ok, 2)

    def unit_length(e, r, i, s, w):
        def do(ins):
            e.wait_ge(pool_did, pool.did(ins))
        do(e.tensor_tensor(s, r, r, ALU.mult))
        do(e.tensor_tensor(w, i, i, ALU.mult))
        do(e.tensor_tensor(s, s, w, ALU.add))
        do(e.tensor_scalar(s, s, -0.5, 1.5, ALU.mult, ALU.add))
        do(e.tensor_tensor(r, r, s, ALU.mult))
        do(e.tensor_tensor(i, i, s, ALU.mult))

    def matrices_pool(e, m):
        b = m % 2
        pr_ = slice(4 * m, 4 * m + 4)
        ge(e, g_mm, m - 1)
        ge(e, y_mm, m - 2)
        for dst, src, pw, n, done in ((V_B[b], bb, pw_dn, 4, vb_ok), (C_P[m % 3], c_raw, pw_up, 5, cp_ok)):
            w = [mtmp[:, k, 0:64 * n].rearrange("p (q j c) -> p q j c", q=4, j=n) for k in range(4)]
            x = [src[:, k, pr_, :].unsqueeze(2).to_broadcast([P, 4, n, 16]) for k in range(2)]
            y = [pw[:, k, pr_, :].unsqueeze(3).to_broadcast([P, 4, n, 16]) for k in range(3 if n == 5 else 2)]
            im = 2 if n == 5 else 1

            def do(ins):
                e.wait_ge(pool_did, pool.did(ins))

            do(e.tensor_tensor(w[0], x[0], y[0], ALU.mult))
            do(e.tensor_tensor(w[1], x[1], y[1], ALU.mult))
            do(e.tensor_tensor(w[2], x[0], y[im], ALU.mult))
            do(e.tensor_tensor(w[3], x[1], y[0], ALU.mult))
            for g in range(2):
                r = slice(HD * g, HD * g + HD)
                do(e.tensor_tensor(dst[r, 0, :, :, g, :], w[0][r], w[1][r], ALU.subtract))
                do(e.tensor_tensor(dst[r, 1, :, :, g, :], w[2][r], w[3][r],
                                   ALU.subtract if n == 5 else ALU.add))
            e.drain().then_inc(done, 1)

    VB = ((0, 1), (3, 7))

    def mixer_front_pe(e, m):
        b = m % 2
        e.wait_ge(vb_ok, m + 1)
        ge(e, vl_ok, 2 * m)
        for k in range(2):
            for q in range(4):
                last = e.transpose(ps[:, 4 + k, q * P:(q + 1) * P],
                                   V_B[b][:, k, q, :, :, :].rearrange("p j g c -> p (j g c)"), ident[:, :])
        last.then_inc(vb_mm, 1)
        e.wait_ge(cp_ok, m + 1)
        ge(e, tl_ok, 4 * m)
        for q in range(4):
            for k in range(2):
                last = e.matmul(ps[0:32, 6, q * P:(q + 1) * P], V_B[b][:, k, q, 3, :, :].rearrange("p g c -> p (g c)"),
                                C_P[m % 3][:, k, q, 0:4, :, :].rearrange("p j g c -> p (j g c)"),
                                start=(k == 0), stop=(k == 1))
        last.then_inc(g_mm, 1)
        e.wait_ge(vl_ok, 2 * m + 2)
        ge(e, v_ev, m - 1)
        for k in range(2):
            for q in range(4):
                last = e.matmul(ps[:, VB[m % 2][k], q * P:(q + 1) * P], v_l[:, k, q, :], u_t[:, 4 * m + q, :],
                                start=True, stop=True)
        last.then_inc(v_mm, 1)

    def mixer_back_pe(e, m):
        b = m % 2
        e.wait_ge(tl_ok, 4 * m + 4)
        e.wait_ge(xs_ok, m + 1)
        ge(e, ys_ok, 4 * m)
        for q in range(4):
            o = ps[:, 2, q * P:(q + 1) * P]
            e.matmul(o, t_l[:, q, :], u_t[:, 4 * m + q, :], start=True, stop=False)
            for k in range(2):
                last = e.matmul(o, C_P[m % 3][:, k, q, 1:5, :, :].rearrange("p j g c -> p (j g c)"),
                                x_s[:, k, q, 0:P], start=False, stop=(k == 1))
        last.then_inc(y_mm, 1)

    def mixer_front_act(e, m):
        e.wait_ge(vb_mm, m + 1)
        ge(e, v_mm, m)
        for k in range(2):
            e.activation(v_l[:, k, :, :].rearrange("p q c -> p (q c)"), ps[:, 4 + k, :], ACT.Copy).then_inc(vl_ok, 1)
        e.wait_ge(g_mm, m + 1)
        ge(e, y_mm, m)
        g = ps[0:32, 6, :].rearrange("p (q c) -> p q c", q=4)
        for j in range(4):
            e.activation(t_l[32 * j:32 * j + 32, :, 32 * j:P], g[:, :, 0:P - 32 * j], ACT.Copy).then_inc(tl_ok, 1)

    def mixer_back_act(e, m):
        e.wait_ge(ys_ok, 4 * m + 4)
        ge(e, g_lo, m - 1)
        for q in range(4):
            for j in range(4):
                dst = sq[32 * q:32 * q + 32, m % 2, 0:SEQ].rearrange("p (c j) -> p j c", j=4)[:, j, :]
                e.activation(dst, u_t[32 * j:32 * j + 32, 4 * m + q, :], ACT.Gelu_apprx_tanh).then_inc(ge_ok, 1)
        e.wait_ge(ge_ok, 16 * m + 16)
        e.activation(a_hi[:, m, :], sq[:, m % 2, 0:SEQ], ACT.Copy).then_inc(g_hi, 1)

    def mixer_dve(e, m):
        e.wait_ge(v_mm, m + 1)
        er, ei = (t[:, 4 * m:4 * m + 4, :].rearrange("p q c -> p (q c)") for t in (e_r, e_i))
        z = [t2[:, k, 0:SEQ] for k in range(2)]
        w = T4(SEQ)
        cmul(e, dve, z[0], z[1], (er, ei), (ps[:, VB[m % 2][0], :], ps[:, VB[m % 2][1], :]), w, -1)
        e.drain().then_inc(v_ev, 1)
        for k in range(2):
            for q in range(4):
                c = slice(q * P, (q + 1) * P)
                n = dve.did(e.tensor_tensor_scan(t0[:, k, c], S(V_M4)[:, 4 * m + q:4 * m + q + 1].to_broadcast([P, P]),
                                                 t2[:, k, c], 0.0, ALU.mult, ALU.add))
        e.wait_ge(dve_did, n)
        ge(e, y_mm, m)
        q4 = lambda t: t.rearrange("p (q c) -> p q c", q=4)
        x = [x_s[:, k, :, 1:P + 1] for k in range(2)]
        cmul(e, dve, x[0], x[1], (q4(er), q4(ei)), (q4(t0[:, 0, 0:SEQ]), q4(t0[:, 1, 0:SEQ])),
             [q4(t) for t in (t1[:, 0, 0:SEQ], t1[:, 1, 0:SEQ], t2[:, 0, 0:SEQ], t2[:, 1, 0:SEQ])])
        e.drain().then_inc(xs_ok, 1)

    def mixer_out_dve(e, m):
        e.wait_ge(y_mm, m + 1)
        for q in range(4):
            e.scalar_tensor_tensor(u_t[:, 4 * m + q, :], u_t[:, 4 * m + q, :], vec("ssm_d", 4 * m + q),
                                   ps[:, 2, q * P:(q + 1) * P], ALU.mult, ALU.add).then_inc(ys_ok, 1)

    def mixer_lo_dve(e, m):
        e.wait_ge(g_hi, m + 1)
        e.tensor_tensor(a_lo[:, m, :], sq[:, m % 2, 0:SEQ], a_hi[:, m, :], ALU.subtract).then_inc(g_lo, 1)

    def glu_act(e, u, m):
        e.wait_ge(unit_mm, u.n(2))
        e.activation(t0[:, m % 2, 0:SEQ], ps[:, (u.slot + 1) % 4, :], ACT.Sigmoid).then_inc(sig_ok, 1)

    def glu_dve(e, u, m):
        e.wait_ge(sig_ok, m + 1)
        e.tensor_tensor(t1[:, m % 2, 0:SEQ], ps[:, u.slot, :], t0[:, m % 2, 0:SEQ], ALU.mult).then_inc(unit_ev, 1)
        e.wait_ge(unit_ev, u.n(1))
        e.tensor_tensor(h[:, m, REAL], h[:, m, REAL], t1[:, m % 2, 0:SEQ], ALU.add).then_inc(unit_ev, 1)

    A0 = 32

    def pair_n(layer, j):
        return FFT * layer + j

    def hidden(g):
        return (a2_hi, a2_lo) if g % 2 else (a_hi, a_lo)

    def up_act(e, layer, g, p0, u, s):
        k = s // 2
        at = p0 + 2 * u.i + k
        j = 8 * g + at
        G = pair_n(layer, j)
        if s % 2 == 0:
            ge(e, gel_ok, G)
        else:
            e.wait_ge(alo_ok, A0 + G)
        e.wait_ge(unit_ev, u.n(1))
        c = 2 * j + s % 2
        e.activation(t1[:, s % 2, 0:SEQ], t0[:, s % 2, 2:SEQ + 2], ACT.Identity, bias=vec(f"ffn_b{layer}", c),
                     scale=vec(f"ffn_w{layer}", 88 + c)).then_inc(c0_ok, 1)
        split_ahead(e, u, split_hi)
        if s % 2 == 0:
            e.wait_ge(cg_ok, G + 1)
            e.activation(t2[:, k, 0:SEQ], t1[:, 0, 0:SEQ], ACT.Gelu_apprx_tanh).then_inc(gel_ok, 1)
        else:
            e.wait_ge(ay_ok, A0 + G + 1)
            e.activation(tile_of(hidden(g)[0], at), t1[:, 1:2, 0:SEQ], ACT.Copy).then_inc(ahi_ok, 1)

    def up_lo(e, layer, g, at):
        n = A0 + pair_n(layer, 8 * g + at) + 1
        hi, lo = hidden(g)
        e.wait_ge(ahi_ok, n)
        e.wait_ge(ay_ok, n)
        e.tensor_tensor(tile_of(lo, at), t1[:, 1:2, 0:SEQ], tile_of(hi, at), ALU.subtract).then_inc(alo_ok, 1)

    def up_dve(e, layer, g, p0, u, s):
        k = s // 2
        at = p0 + 2 * u.i + k
        j = 8 * g + at
        G = pair_n(layer, j)
        c = 2 * j + s % 2
        e.wait_ge(unit_mm, u.n(1))
        e.tensor_tensor(t0[:, s % 2, 2:SEQ + 2], ps[:, u.slot, :], rstd[:, 0:SEQ], ALU.mult).then_inc(unit_ev, 1)
        if s % 2 == 0 and not (k == 0 and isinstance(u.i, int) and u.i == 0):
            up_lo(e, layer, g, at - 1)
        e.wait_ge(c0_ok, 2 * G + s % 2 + 1)
        e.wait_ge(unit_ev, u.n(1))
        y = t1[:, s % 2, 0:SEQ]
        n = dve.did(e.scalar_tensor_tensor(y, t0[:, s % 2, 1:SEQ + 1], vec(f"ffn_w{layer}", 44 + c), y,
                                           ALU.mult, ALU.add))
        e.wait_ge(dve_did, n)
        e.scalar_tensor_tensor(y, t0[:, s % 2, 0:SEQ], vec(f"ffn_w{layer}", c), y, ALU.mult, ALU.add)\
            .then_inc(cg_ok if s % 2 == 0 else cv_ok, 1)
        if s % 2 == 0:
            split_ahead(e, u, split_lo)
            e.wait_ge(cg_ok, G + 1)
        else:
            e.wait_ge(cv_ok, G + 1)
            e.wait_ge(gel_ok, G + 1)
            e.tensor_tensor(y, y, t2[:, k, 0:SEQ], ALU.mult).then_inc(ay_ok, 1)
            split_ahead(e, u, split_lo)

    def ffn(e, who, layer, u0, n):
        gain = f"ple_norm{layer}"
        u = u0
        for kind, g, p0, p1 in FFN_ORDER:
            if kind == "down" and g == 1:
                side_operands(e, who, layer)
            if kind == "side":
                side_projection(e, who, layer, u)
                u += 2
            elif kind == "up":
                start = g == 0 and p0 == 0

                def up(v, s):
                    if who == "act":
                        up_act(e, layer, g, p0, v, s)
                    elif who == "dve":
                        up_dve(e, layer, g, p0, v, s)
                    else:
                        ready = None
                        if start and isinstance(v.i, int) and v.i == 0 and s == 0:
                            ready = lambda e, k: e.wait_ge(xlo_ok, 8 * XN[n - 1] + k + 1)
                        unit_pe(e, v, x_hi, x_lo, ready)

                if who == "dve":
                    units(e, u, (p1 - p0) // 2, up, 1, counts=dve, rate=4)
                    up_lo(e, layer, g, p1 - 1)
                else:
                    units(e, u, (p1 - p0) // 2, up, 1 if start else 0)
                u += 2 * (p1 - p0)
            else:
                last = g == len(FFG) - 1
                for m in range(KT):
                    v = Unit(u + m)
                    if who == "act":
                        split_ahead(e, v, split_hi)
                        if last:
                            e.wait_ge(unit_ev, v.n(1))
                            norm_act(e, n, m, None)
                            x_act(e, n, m, gain)
                    elif who == "dve":
                        split_ahead(e, v, split_lo)
                        add_dve(e, v, m)
                        if last and m:
                            x_dve(e, XN[n], m - 1, gain)
                    else:
                        hi, lo = hidden(g)
                        ready = (lambda e, k: e.wait_ge(alo_ok, A0 + pair_n(layer, 8 * g) + k + 1)) if m == 0 else None
                        unit_pe(e, v, hi, lo, ready, kt=FFG[g])
                        if last and m:
                            stat_pe(e, n, m - 1)
                u += KT
        if who == "act":
            root_act(e, n, eps6)
        elif who == "dve":
            x_dve(e, XN[n], KT - 1, gain)
            root_dve(e, n)
        else:
            stat_pe(e, n, KT - 1)

    def side_operands(e, who, layer):
        if who == "act":
            e.wait_ge(p_in, 16 * (layer + 1))
            e.activation(p_hi[:, :, :], p_raw[:, :, :], ACT.Copy).then_inc(phi_ok, 1)
        elif who == "dve":
            e.wait_ge(phi_ok, layer + 1)
            e.tensor_tensor(p_lo[:, :, :], p_raw[:, :, :], p_hi[:, :, :], ALU.subtract).then_inc(plo_ok, 1)

    def side_projection(e, who, layer, u0):
        if who == "act":
            for s in range(2):
                split_ahead(e, Unit(u0 + s), split_hi)
        elif who == "dve":
            for s in range(2):
                u = Unit(u0 + s)
                e.wait_ge(unit_mm, u.n(1))
                e.tensor_copy(pp[:, 4 * s:4 * s + 4, :], ps[:, 0:4, :]).then_inc(unit_ev, 1)
                split_ahead(e, u, split_lo)
        else:
            e.wait_ge(plo_ok, layer + 1)
            for s in range(2):
                u = Unit(u0 + s)
                e.wait_ge(lo_ok, u.n(1))
                e.wait_ge(unit_ev, u.n())
                for q in range(4):
                    last = products(e, u, q, p_hi, p_lo, kt=2, w0=2 * q)
                last.then_inc(unit_mm, 1)
            e.wait_ge(unit_ev, u0 + 2)

    def side(e, who, layer, u0, n, after=None, lag=0):
        if who == "act":
            for m in range(KT):
                u = Unit(u0 + m)
                split_ahead(e, u, split_hi)
                e.wait_ge(unit_ev, u.n(1))
                ge(e, sgu_ok, 8 * layer + m - 1)
                e.activation(t1[:, m % 2, 0:SEQ], t0[:, m % 2, 0:SEQ], ACT.Sigmoid).then_inc(sg_ok, 1)
                if after and m >= lag:
                    after(m - lag)
        elif who == "dve":
            for m in range(KT + 1):
                if m < KT:
                    u = Unit(u0 + m)
                    split_ahead(e, u, split_lo)
                    e.wait_ge(unit_mm, u.n(1))
                    ge(e, sg_ok, 8 * layer + m - 1)
                    e.tensor_tensor(t0[:, m % 2, 0:SEQ], ps[:, u.slot, :], rstd[:, 0:SEQ], ALU.mult).then_inc(unit_ev, 1)
                if after and m > lag:
                    after(m - 1 - lag)
                if m:
                    j = m - 1
                    e.wait_ge(sg_ok, 8 * layer + j + 1)
                    e.tensor_tensor(t2[:, j % 2, 0:SEQ], t1[:, j % 2, 0:SEQ], pp[:, j, :], ALU.mult).then_inc(sgu_ok, 1)
                    e.wait_ge(sgu_ok, 8 * layer + j + 1)
                    e.tensor_tensor(h[:, j, REAL], h[:, j, REAL], t2[:, j % 2, 0:SEQ], ALU.add).then_inc(h_fin, 1)
        else:
            for m in range(KT):
                ready = (lambda e, k: e.wait_ge(xlo_ok, 8 * XN[n] + k + 1)) if m == 0 else None
                unit_pe(e, Unit(u0 + m), x_hi, x_lo, ready)
                if after and m >= lag:
                    after(m - lag)
        if after:
            for m in range(KT - lag, KT):
                after(m)


    def normed(e, who, u0, b, store, gain, hi, lo, ready=None):
        def last(m):
            if b > 1:
                k = 8 * (b - 1) + m
                if who == "dve":
                    if m == 0:
                        head_inverse(e, b - 1)
                    head_scale(e, k, gain[0][:, m, :], gain[1], gain[0][:, m, :])
                elif who == "pe":
                    head_spread(e, k)

        if b > 1 and who == "act":
            head_root(e, b - 1, HD, eps6)
        for m in range(8 + 1):
            if m < 8:
                u = Unit(u0 + m)
                if who == "act":
                    split_ahead(e, u, split_hi)
                    if b < 3:
                        e.wait_ge(unit_ev, u.n(1))
                        head_sq(e, 8 * b + m, store[:, m, :])
                elif who == "dve":
                    split_ahead(e, u, split_lo)
                    e.wait_ge(unit_mm, u.n(1))
                    e.tensor_tensor(store[:, m, :], ps[:, u.slot, :], rstd[:, 0:SEQ], ALU.mult).then_inc(unit_ev, 1)
                else:
                    unit_pe(e, u, hi, lo, ready if m == 0 else None)
            if m:
                if who == "pe" and b < 3:
                    head_pe(e, 8 * b + m - 1)
                last(m - 1)

    def stage2_pool(e, p):
        par = p % 2
        k = 4 * p
        if p >= 2:
            e.wait_ge(s_mm, 32 + 4 * (p - 1))
            e.wait_ge(vt_mm, 4 + p - 1)
        for c in range(2):
            r = slice(HD * c, HD * c + HD)
            e.wait_ge(staged, 32 + k + c)
            e.tensor_scalar(qs2[r, par, c, :], q2[r, p, :], HD ** -0.5, None, ALU.mult).then_inc(staged, 1)
        e.wait_ge(staged, 32 + k + 2)
        e.tensor_copy(ks2[:, par, :], k2[:, p, :]).then_inc(staged, 1)
        e.wait_ge(staged, 32 + k + 3)
        e.tensor_copy(vs2[:, par, :], v2[:, p, :]).then_inc(staged, 1)

    def bias_load(e, p):
        ge(e, blo_ok, p)
        src = bass.AP(scratch.tensor, scratch.offset + p * 640 + 1, [[1, P], [1, SEQ]])
        e.dma_start(b_raw[:, 0, :], src).then_inc(b_in, 16)

    def attention2(e, who):
        def pe_scores(g):
            p, qt, sl = g // 4, g % 4, g % 2
            N = (qt + 1) * P
            if qt == 0:
                e.wait_ge(staged, 32 + 4 * p + 4)
                e.wait_ge(blo_ok, p + 1)
                ge(e, o_ok, p - 1)
                for j in range(4):
                    last = e.transpose(ps[:, 6 + p % 2, j * P:(j + 1) * P], vs2[:, p % 2, j * P:(j + 1) * P], ident[:, :])
                last.then_inc(vt_mm, 1)
            ge(e, exp_ok, 32 + 2 * (g - 1))
            for c in range(2):
                o = ps[:, 2 * sl + c, 0:N]
                e.matmul(o, qs2[:, p % 2, c, qt * P:(qt + 1) * P], ks2[:, p % 2, 0:N], start=True, stop=False)
                for n, t in enumerate((b_hi, b_lo)):
                    last = e.matmul(o, flip_r[:, :], t[:, p % 2, SEQ - N:SEQ], start=False, stop=(n == 1))
            last.then_inc(s_mm, 1)

        def pe_turn(g):
            p, qt, sl = g // 4, g % 4, g % 2
            e.wait_ge(nrm_ok, 32 + g + 1)
            if qt == 0:
                e.wait_ge(v2_ok, p + 1)
            for j in range(qt + 1):
                last = e.transpose(ps[:, 4 + sl, j * P:(j + 1) * P], t0[:, sl, j * P:(j + 1) * P], ident[:, :])
            last.then_inc(pt_mm, 1)

        def pe_pv(g):
            p, qt, sl = g // 4, g % 4, g % 2
            e.wait_ge(pt_ok, 32 + g + 1)
            if qt == 0:
                ge(e, o_ok, p - 1)
            for j in range(qt + 1):
                last = e.matmul(ps[:, 6 + p % 2, qt * P:(qt + 1) * P], vtok[:, p % 2, j, :], pt2[:, sl, j, :],
                                start=(j == 0), stop=(j == qt))
            last.then_inc(pv_mm, 1)

        def dve_top(g):
            p, qt, sl = g // 4, g % 4, g % 2
            N = (qt + 1) * P
            e.wait_ge(s_mm, 32 + g + 1)
            for c in range(2):
                e.reduce_max(small[:, 1, 2 * sl + c:2 * sl + c + 1], ps[:, 2 * sl + c, 0:N], AX_X, negate=True)\
                    .then_inc(nb_ok, 1)

        def dve_bias(p):
            e.wait_ge(bhi_ok, p + 1)
            e.tensor_tensor(b_lo[:, p % 2, :], b_raw[:, 0, :], b_hi[:, p % 2, :], ALU.subtract).then_inc(blo_ok, 1)

        def act_bias(p):
            e.wait_ge(b_in, 16 * (p + 1))
            ge(e, s_mm, 32 + 4 * (p - 1))
            e.activation(b_hi[:, p % 2, :], b_raw[:, 0, :], ACT.Copy).then_inc(bhi_ok, 1)

        def dve_mix(g):
            p, qt, sl = g // 4, g % 4, g % 2
            N = (qt + 1) * P
            r = [small[:, 3, 2 * sl + c:2 * sl + c + 1] for c in range(2)]
            e.wait_ge(exp_ok, 32 + 2 * g + 1)
            n = dve.did(e.reciprocal(r[0], small[:, 2, 2 * sl:2 * sl + 1]))
            e.wait_ge(dve_did, n)
            dve.did(e.tensor_scalar(t0[:, sl, 0:N], t0[:, sl, 0:N], r[0], None, ALU.mult))
            e.wait_ge(exp_ok, 32 + 2 * g + 2)
            n = dve.did(e.reciprocal(r[1], small[:, 2, 2 * sl + 1:2 * sl + 2]))
            e.wait_ge(dve_did, n)
            n = dve.did(e.tensor_tensor(r[1], r[1], neg_lam[:, :], ALU.mult))
            e.wait_ge(dve_did, n)
            e.scalar_tensor_tensor(t0[:, sl, 0:N], t1[:, sl, 0:N], small[:, 3, 2 * sl + 1:2 * sl + 2],
                                   t0[:, sl, 0:N], ALU.mult, ALU.add).then_inc(nrm_ok, 1)

        def dve_out(p):
            e.wait_ge(pv_mm, 32 + 4 * p + 4)
            e.wait_ge(staged, 32 + 4 * p + 4)
            e.tensor_copy(q2[:, p, :], ps[:, 6 + p % 2, :]).then_inc(o_ok, 1)

        def act_exp(g):
            p, qt, sl = g // 4, g % 4, g % 2
            N = (qt + 1) * P
            ge(e, pt_mm, 32 + g - 1)
            for c, t in enumerate((t0, t1)):
                e.wait_ge(nb_ok, 32 + 2 * g + c + 1)
                e.activation(t[:, sl, 0:N], ps[:, 2 * sl + c, 0:N], ACT.Exp,
                             bias=small[:, 1, 2 * sl + c:2 * sl + c + 1],
                             accum_out=small[:, 2, 2 * sl + c:2 * sl + c + 1]).then_inc(exp_ok, 1)

        def act_turn(g):
            p, qt, sl = g // 4, g % 4, g % 2
            N = (qt + 1) * P
            if qt == 0:
                e.wait_ge(vt_mm, 4 + p + 1)
                e.activation(vtok[:, p % 2, :, :].rearrange("p j c -> p (j c)"), ps[:, 6 + p % 2, :], ACT.Copy)\
                    .then_inc(v2_ok, 1)
            e.wait_ge(pt_mm, 32 + g + 1)
            ge(e, pv_mm, 32 + g - 1)
            e.activation(pt2[:, sl, 0:qt + 1, :].rearrange("p j c -> p (j c)"), ps[:, 4 + sl, 0:N], ACT.Copy)\
                .then_inc(pt_ok, 1)

        for g in range(32 + 2):
            if who == "pe":
                if g < 32:
                    pe_scores(g)
                if 1 <= g < 33:
                    pe_turn(g - 1)
                if g >= 2:
                    pe_pv(g - 2)
            elif who == "dve":
                if 1 <= g < 33:
                    dve_mix(g - 1)
                if g == 0:
                    dve_bias(0)
                if g < 32:
                    dve_top(g)
                if g % 4 == 2 and g < 30:
                    dve_bias(g // 4 + 1)
                if g >= 5 and (g - 5) % 4 == 0:
                    dve_out((g - 5) // 4)
            else:
                if g == 0:
                    act_bias(0)
                if g < 32:
                    act_exp(g)
                if 1 <= g < 33:
                    act_turn(g - 1)
                if g % 4 == 1 and g < 29:
                    act_bias(g // 4 + 1)

    block = ctx.enter_context(nc.Block())

    @block.sync
    def _(sp):
        for n in range(4):
            sp.dma_start(h[:, 2 * n:2 * n + 2, :], A["xT"][:, 2 * n:2 * n + 2, :]).then_inc(h_in[n], 16)
            if n == 0:
                sp.dma_start(vecs[:, :], A["vecs"]).then_inc(first_in, 16)
                sp.dma_start(ones[:, :], A["ones"]).then_inc(first_in, 16)
            if n == 1:
                load_unit(sp, Unit(0))
        load_unit(sp, Unit(1))
        for name, t in (("spread", spread1), ("ident", ident), ("flip", flip), ("mask", mask), ("win", win)):
            sp.dma_start(t[:, :], A[name]).then_inc(consts_in, 16)
        sp.dma_start(wf[:, :, :], A["wf"]).then_inc(consts_in, 16)
        sp.dma_start(rel[:, :], A["rel"]).then_inc(consts_in, 16)
        for s in range(2, 4):
            load_unit(sp, Unit(s))
        with sp.Fori(1, NU // 4) as i:
            for s in range(4):
                load_unit(sp, Unit(s, i))
        for m in range(KT):
            sp.wait_ge(h_fin, 16 + m + 1)
            sp.dma_start(out[:, m, :], h[:, m, REAL]).then_inc(stored, 16)
        sp.wait_ge(stored, 16 * KT)

    @block.gpsimd
    def _(e):
        e.memset(eps5[:, :], 1e-5).then_inc(consts_ok, 1)
        e.memset(eps6[:, :], 1e-6).then_inc(consts_ok, 1)
        e.memset(eps_o[:, :], 1e-6 / (1.0 - LAM) ** 2).then_inc(consts_ok, 1)
        e.wait_ge(consts_ok, 3)
        for m in range(KT):
            e.wait_ge(h_in[m // 2], 16)
            if m:
                e.wait_ge(sq_ok, m)
            ge(e, stat_mm, m - 1)
            e.tensor_tensor(sq[:, m % 2, :], h[:, m, :], h[:, m, :], ALU.mult).then_inc(sq_ok, 1)
        e.wait_ge(sq_ok, 8)
        e.memset(aug_q[:, :, :, :], 0.0).then_inc(consts_ok, 1)
        e.memset(aug_k[:, :], 0.0).then_inc(consts_ok, 1)
        e.wait_ge(consts_ok, 5)
        e.memset(aug_k[32:40, :], 1.0).then_inc(consts_ok, 1)
        e.wait_ge(consts_ok, 6)
        e.memset(qs[:, :, :, :], 0.0).then_inc(qz_ok, 1)
        e.memset(vp[:, :, :, :, :], 0.0).then_inc(vz_ok, 1)
        e.memset(vm[:, :, :, :], 0.0).then_inc(vz_ok, 1)
        e.wait_ge(qz_ok, 1)
        e.wait_ge(vz_ok, 2)
        system_pool(e)
        e.wait_ge(unit_ev, 12)
        e.wait_ge(f_ok, 3)
        stage1_pool(e, 0)
        fence(e, 1)
        stage1_pool(e, 1)
        fence(e, 2)
        e.wait_ge(hn_lo, 8)
        e.dma_start(b_in_[:, :, :, :], A["ssm_bc"][:, 0:2, :, :]).then_inc(bc_in, 16)
        e.dma_start(c_raw[:, :, :, :], A["ssm_bc"][:, 2:4, :, :]).then_inc(bc_in, 16)
        tables_pool(e)
        e.drain().then_inc(tables_ok, 1)
        matrices_pool(e, 0)

        def spread(u, s):
            e.wait_ge(unit_ev, u.n(1))
            m = u.n(-U_SSM)
            for q in range(4):
                for j in (2, 3):
                    ge(e, ut_p, 8 * m + 2 * q + j - 2)
                    spread_u(e, u, m, q, j, "p").then_inc(ut_p, 1)

        units(e, U_SSM, 2, spread, 1)
        fence(e, 3)
        e.wait_ge(pads_ok, 7)
        for m in range(1, 8):
            matrices_pool(e, m)
        fence(e, 4)
        e.dma_start(spread2[:, :], A["spread"]).then_inc(tab_in, 16)
        e.dma_start(p_raw[:, :, :], A["pT"][:, 0, :, :]).then_inc(p_in, 16)
        fence(e, 5)
        e.wait_ge(h_fin, 16)
        e.dma_start(onehot, A["onehot"]).then_inc(tab_in, 16)
        e.wait_ge(tab_ok, 2)
        e.dma_start(scratch, tab[0:8, :]).then_inc(tab_out, 16)
        e.memset(qs2[:, :, :, :], 0.0).then_inc(qz2_ok, 1)
        e.wait_ge(qz2_ok, 1)
        e.wait_ge(tab_out, 16)
        for p in range(8):
            bias_load(e, p)
            if p == 0:
                e.wait_ge(hn_y, 17)
                e.wait_ge(unit_ev, U_KV + 9)
            stage2_pool(e, p)
            if p == 0:
                fence(e, 6)
        fence(e, 7)
        fence(e, 8)
        e.dma_start(p_raw[:, :, :], A["pT"][:, 1, :, :]).then_inc(p_in, 16)

    @block.scalar
    def _(e):
        e.wait_ge(first_in, 32)
        for m in range(KT):
            e.wait_ge(h_in[m // 2], 16)
            x_act(e, 0, m, "norm_mix", TOK)
            if m in (1, 3):
                split_hi(e, Unit(m // 2))
        e.wait_ge(consts_in, 16 * 7)
        e.wait_ge(consts_ok, 6)
        root_act(e, 0, eps5, TOK)
        e.activation(wf_hi[:, :, :], wf[:, :, :], ACT.Copy).then_inc(wf_ok, 1)
        e.activation(ident_b[:, :], ident[:, :], ACT.Copy).then_inc(wf_ok, 1)
        e.activation(mask_b[:, :], mask[:, :], ACT.Copy).then_inc(wf_ok, 1)
        e.activation(flip_r[:, :], flip[:, :], ACT.Copy).then_inc(wf_ok, 1)
        e.activation(S(V_DT), vecs[:, COL["log_dt"]:COL["log_dt"] + 32], ACT.Exp).then_inc(dt_ok, 1)
        units(e, U_QKVB, 4, lambda u, s: split_ahead(e, u, split_hi), 1)
        e.wait_ge(par_v, 1)
        e.activation(S(V_MAG), S(V_SH), ACT.Exp).then_inc(par_a, 1)
        e.wait_ge(par_v, 2)
        e.activation(S(V_COS), S(V_R), ACT.Sin, scale=0.5).then_inc(par_a, 1)
        e.activation(S(V_SIN), S(V_R), ACT.Sin).then_inc(par_a, 1)
        f_scalar(e)
        units(e, U_CU, 2, lambda u, s: split_ahead(e, u, split_hi))
        fence(e, 1)
        attention1_act(e)
        fence(e, 2)
        for m in range(8 + 1):
            if m < 8:
                head_sq(e, m, y_tile(m))
            if m == 8:
                head_root(e, 0, HD, eps5)
        for m in range(8):
            head_hi(e, m, m)
        for m in range(KT):
            u = Unit(U_OUT1 + m)
            split_ahead(e, u, split_hi)
            e.wait_ge(unit_ev, u.n(1))
            norm_act(e, 1, m, "norm_mlp")
        root_act(e, 1, eps5)

        def ff(u, s):
            split_ahead(e, u, split_hi)
            if s < 8:
                hidden_hi(e, 8 * u.i + s, s)

        units(e, U_FF, 3, ff, cycle=16)
        for s in range(16):
            u = Unit(U_FF + 48 + s)
            split_ahead(e, u, split_hi)
            if s < 8:
                hidden_hi(e, 24 + s, s)
            else:
                e.wait_ge(unit_ev, u.n(1))
                norm_act(e, 2, s - 8, None)
        root_act(e, 2, eps5)
        for m in range(KT):
            e.wait_ge(h_fin, m + 1)
            norm_act(e, 3, m, "ssm_norm")
        root_act(e, 3, eps6)

        def spread(u, s):
            split_ahead(e, u, split_hi)
            e.wait_ge(unit_ev, u.n(1))
            m = u.n(-U_SSM)
            for q in range(4):
                for j in (0, 1):
                    spread_u(e, u, m, q, j, "a").then_inc(ut_a, 1)

        units(e, U_SSM, 2, spread, 1)
        fence(e, 3)
        e.wait_ge(pads_ok, 7)
        for m in range(8 + 2):
            if m < 8:
                mixer_front_act(e, m)
            if m >= 2:
                mixer_back_act(e, m - 2)
        fence(e, 4)
        for m in range(KT):
            u = Unit(U_GLU + 2 * m)
            split_ahead(e, u, split_hi)
            split_ahead(e, u.ahead(1), split_hi)
            glu_act(e, u, m)
            e.wait_ge(unit_ev, u.n(2))
            norm_act(e, 4, m, "ffn_norm0")
        root_act(e, 4, eps6)
        fence(e, 5)
        ffn(e, "act", 0, U_FFNA, 5)

        def attn_form(m):
            e.wait_ge(h_fin, 8 + m + 1)
            norm_act(e, 6, m, None)
            x_act(e, 6, m, "attn_norm", hi=a_hi)

        side(e, "act", 0, U_GATEA, 5, attn_form, 2)
        root_act(e, 6, eps6)
        e.wait_ge(unit_mm, U_Q)
        for m in range(KT):
            x_act(e, 6, m, "kv_norm")
        e.wait_ge(lam_mm, 1)
        e.activation(small[:, 1, 0:2], ps[:, 7, 0:2], ACT.Exp).then_inc(lam_a, 1)
        for b, (u0, store) in enumerate(((U_Q, q2), (U_KV, k2), (U_KV + 8, v2)), 1):
            normed(e, "act", u0, b, store, None, None, None)
        fence(e, 6)
        attention2(e, "act")
        fence(e, 7)
        for m in range(8 + 1):
            if m < 8:
                head_sq(e, 24 + m, q2[:, m, :])
            if m == 8:
                head_root(e, 3, P * (1 - LAM) ** 2, eps_o)
        for m in range(8):
            head_hi(e, 24 + m, m)
        for m in range(KT):
            u = Unit(U_WO + m)
            split_ahead(e, u, split_hi)
            e.wait_ge(unit_ev, u.n(1))
            norm_act(e, 7, m, "ffn_norm1")
        root_act(e, 7, eps6)
        fence(e, 8)
        ffn(e, "act", 1, U_FFNB, 8)
        side(e, "act", 1, U_GATEB, 8)

    @block.vector
    def _(e):
        e.wait_ge(first_in, 32)
        n = dve.did(e.memset(t2[0:8, 0, :], 1.0))
        for m in range(KT):
            x_dve(e, 0, m, "norm_mix", TOK)
            if m in (2, 4):
                split_lo(e, Unit(m // 2 - 1))
        e.wait_ge(wf_ok, 1)
        e.tensor_tensor(wf_lo[:, :, :], wf[:, :, :], wf_hi[:, :, :], ALU.subtract).then_inc(wflo_ok, 1)
        root_dve(e, 0, TOK)

        def qkvb_dve(u, s):
            split_ahead(e, u, split_lo)
            t = u.n()
            wide_dve(e, u, tile_of(qkvb, t).rearrange("p a b -> p (a b)"))

        units(e, U_QKVB, 4, qkvb_dve, 1)
        f_dve(e)
        system_dve(e)

        def conv(u, s):
            split_ahead(e, u, split_lo)
            conv_dve(e, u, s)

        units(e, U_CU, 2, conv, counts=dve, rate=10)
        fence(e, 1)
        attention1_dve(e)
        fence(e, 2)
        head_inverse(e, 0)
        for m in range(8 + 1):
            if m < 8:
                head_scale(e, m, y_tile(m), vec("out_norm", m))
            if m:
                head_lo(e, m - 1, m - 1)
        for m in range(KT):
            u = Unit(U_OUT1 + m)
            split_ahead(e, u, split_lo)
            add_dve(e, u, m)
            if m:
                x_dve(e, 1, m - 1, "norm_mlp")
        x_dve(e, 1, KT - 1, "norm_mlp")
        root_dve(e, 1)

        def ff(u, s):
            split_ahead(e, u, split_lo)
            if s < 8:
                relu2_dve(e, u, s)
                if s:
                    hidden_lo(e, 8 * u.i + s - 1, s - 1)
                if s == 7:
                    hidden_lo(e, 8 * u.i + 7, 7)
            else:
                add_dve(e, u, s - 8)

        units(e, U_FF, 3, ff, first=1, cycle=16)
        for s in range(16):
            ff(Unit(U_FF + s, 3, 16), s)
        root_dve(e, 2)
        for m in range(KT):
            e.scalar_tensor_tensor(h[:, m, REAL], h[:, m, REAL], vec("final_norm", m), rstd[:, 0:SEQ],
                                   ALU.mult, ALU.mult).then_inc(h_fin, 1)
            if m > 1:
                x_dve(e, 2, m - 2, "ssm_norm")
        x_dve(e, 2, 6, "ssm_norm")
        x_dve(e, 2, 7, "ssm_norm")
        root_dve(e, 3)

        def project_u(u, s):
            split_ahead(e, u, split_lo)
            e.wait_ge(unit_mm, u.n(1))
            m = u.n(-U_SSM)
            ge(e, ut_a, 8 * (m - 1))
            ge(e, ut_p, 8 * (m - 1))
            e.tensor_tensor(t0[:, s % 2, 0:SEQ], ps[:, u.slot, :], rstd[:, 0:SEQ], ALU.mult).then_inc(unit_ev, 1)

        units(e, U_SSM, 2, project_u, 1)
        fence(e, 3)
        for t in (v_b1, c_p1, c_p2):
            e.memset(t[:], 0.0).then_inc(pads_ok, 1)
        e.memset(t_l[:, :, :], 0.0).then_inc(pads_ok, 1)
        e.memset(x_s[:, :, :, 0:1], 0.0).then_inc(pads_ok, 1)
        e.wait_ge(pads_ok, 7)
        e.wait_ge(tables_ok, 1)
        for m in range(8 + 1):
            if m < 8:
                mixer_dve(e, m)
            if m >= 3:
                mixer_lo_dve(e, m - 3)
            if m:
                mixer_out_dve(e, m - 1)
        mixer_lo_dve(e, 6)
        mixer_lo_dve(e, 7)
        fence(e, 4)
        for m in range(KT):
            u = Unit(U_GLU + 2 * m)
            split_ahead(e, u, split_lo)
            split_ahead(e, u.ahead(1), split_lo)
            glu_dve(e, u, m)
            if m:
                x_dve(e, 3, m - 1, "ffn_norm0")
        x_dve(e, 3, KT - 1, "ffn_norm0")
        root_dve(e, 4)
        fence(e, 5)
        n = dve.did(e.memset(t0[:, :, 0:2], 0.0))
        e.wait_ge(dve_did, n)
        ffn(e, "dve", 0, U_FFNA, 5)
        side(e, "dve", 0, U_GATEA, 5,
             lambda m: x_dve(e, 5, m, "attn_norm", hi=a_hi, lo=a_lo), 2)
        root_dve(e, 6)
        for m in range(KT):
            x_dve(e, 6, m, "kv_norm")
        c = COL["lambdas"]
        e.tensor_tensor(small[:, 0, 0:2], vecs[:, c:c + 4:2], vecs[:, c + 1:c + 4:2], ALU.mult).then_inc(lam_v, 1)
        normed(e, "dve", U_Q, 1, q2, None, None, None)
        e.wait_ge(tab_mm, 1)
        for lo, n in ((0, SEQ), (SEQ, P)):
            e.tensor_copy(tab[0:8, lo:lo + n], ps[0:8, 6 + lo // SEQ, 0:n]).then_inc(tab_ok, 1)
        normed(e, "dve", U_KV, 2, k2, (q2, vec("q_norm")), None, None)
        normed(e, "dve", U_KV + 8, 3, v2, (k2, vec("k_norm")), None, None)
        e.wait_ge(lam_a, 1)
        n = dve.did(e.tensor_tensor(small[:, 2, 0:1], small[:, 1, 1:2], small[:, 1, 0:1], ALU.subtract))
        e.wait_ge(dve_did, n)
        n = dve.did(e.tensor_scalar(neg_lam[:, :], small[:, 2, 0:1], -LAM, None, ALU.add))
        fence(e, 6)
        attention2(e, "dve")
        fence(e, 7)
        head_inverse(e, 3)
        for m in range(8 + 1):
            if m < 8:
                head_scale(e, 24 + m, q2[:, m, :], vec("subln"))
            if m:
                head_lo(e, 24 + m - 1, m - 1)
        for m in range(KT):
            u = Unit(U_WO + m)
            split_ahead(e, u, split_lo)
            add_dve(e, u, m)
            if m:
                x_dve(e, 7, m - 1, "ffn_norm1")
        x_dve(e, 7, KT - 1, "ffn_norm1")
        root_dve(e, 7)
        fence(e, 8)
        n = dve.did(e.memset(t0[:, :, 0:2], 0.0))
        e.wait_ge(dve_did, n)
        ffn(e, "dve", 1, U_FFNB, 8)
        side(e, "dve", 1, U_GATEB, 8)

    @block.tensor
    def _(e):
        e.wait_ge(first_in, 32)
        for m in range(4):
            stat_pe(e, 0, m, TOK)
        units(e, U_QKVB, 4, lambda u, s: wide_pe(e, u), 1)
        f_pe(e)
        units(e, U_CU, 2, lambda u, s: wide_pe(e, u))
        fence(e, 1)
        attention1_pe(e)
        fence(e, 2)
        for m in range(8):
            head_pe(e, m)
        for m in range(8):
            head_spread(e, m)
        e.wait_ge(unit_ev, U_OUT1)
        for m in range(KT):
            ready = (lambda e, k: e.wait_ge(hn_lo, k + 1)) if m == 0 else None
            unit_pe(e, Unit(U_OUT1 + m), a_hi, a_lo, ready)
            if m:
                stat_pe(e, 1, m - 1)
        stat_pe(e, 1, KT - 1)

        def ff(u, s):
            ready = None
            if s == 0 and isinstance(u.i, int) and u.i == 0:
                ready = lambda e, k: e.wait_ge(xlo_ok, 8 + k + 1)
            if s == 8:
                ready = lambda e, k: e.wait_ge(alo_ok, 8 * u.i + k + 1)
            if s < 8:
                unit_pe(e, u, x_hi, x_lo, ready)
            else:
                unit_pe(e, u, a_hi, a_lo, ready)

        units(e, U_FF, 3, ff, first=1, cycle=16)
        for s in range(16):
            ff(Unit(U_FF + s, 3, 16), s)
            if s > 8:
                stat_pe(e, 2, s - 9)
        stat_pe(e, 2, KT - 1)
        for m in range(KT):
            stat_pe(e, 3, m)

        def project_u(u, s):
            ready = None
            if isinstance(u.i, int) and s == 0:
                ready = lambda e, k: e.wait_ge(xlo_ok, 16 + k + 1)
            unit_pe(e, u, x_hi, x_lo, ready)

        units(e, U_SSM, 2, project_u, 1)
        fence(e, 3)
        for m in range(8 + 1):
            if m < 8:
                mixer_front_pe(e, m)
            if m:
                mixer_back_pe(e, m - 1)
        fence(e, 4)
        for m in range(2 * KT):
            ready = (lambda e, k: e.wait_ge(g_lo, k + 1)) if m == 0 else None
            unit_pe(e, Unit(U_GLU + m), a_hi, a_lo, ready)
            if m % 2 and m > 2:
                stat_pe(e, 4, m // 2 - 1)
        stat_pe(e, 4, KT - 1)
        fence(e, 5)
        ffn(e, "pe", 0, U_FFNA, 5)
        side(e, "pe", 0, U_GATEA, 5, lambda m: stat_pe(e, 6, m), 3)
        e.wait_ge(lam_v, 1)
        e.matmul(ps[:, 7, 0:2], ones[:, :], small[:, 0, 0:2], start=True, stop=True).then_inc(lam_mm, 1)
        normed(e, "pe", U_Q, 1, None, None, a_hi, a_lo, lambda e, k: e.wait_ge(xlo_ok, 40 + k + 1))
        e.wait_ge(lam_a, 1)
        e.wait_ge(tab_in, 32)
        e.matmul(ps[0:8, 6, :], rel[:, :], onehot[:, 0:SEQ], start=True, stop=True)
        e.matmul(ps[0:8, 7, 0:P], rel[:, :], onehot[:, SEQ:640], start=True, stop=True).then_inc(tab_mm, 1)
        normed(e, "pe", U_KV, 2, None, None, x_hi, x_lo, lambda e, k: e.wait_ge(xlo_ok, 48 + k + 1))
        normed(e, "pe", U_KV + 8, 3, None, None, x_hi, x_lo)
        fence(e, 6)
        attention2(e, "pe")
        fence(e, 7)
        for m in range(8):
            head_pe(e, 24 + m, 1)
        for m in range(8):
            head_spread(e, 24 + m)
        for m in range(KT):
            ready = (lambda e, k: e.wait_ge(hn_lo, 8 + k + 1)) if m == 0 else None
            unit_pe(e, Unit(U_WO + m), a_hi, a_lo, ready)
            if m:
                stat_pe(e, 7, m - 1)
        stat_pe(e, 7, KT - 1)
        fence(e, 8)
        ffn(e, "pe", 1, U_FFNB, 8)
        side(e, "pe", 1, U_GATEB, 8)


def lay_out(x):
    f = np.float32

    def cols(v, parts=P):
        return np.ascontiguousarray(np.asarray(v, f).reshape(-1, parts).T)

    V = np.zeros((P, NCOL), f)

    def put(name, m, parts=P):
        V[:parts, COL[name]:COL[name] + m.shape[1]] = m

    put("norm_mix", cols(x["norm_mix_g"])); put("out_norm", cols(x["out_norm_g"]))
    put("norm_mlp", cols(x["norm_mlp_g"])); put("final_norm", cols(x["final_norm_g"]))
    put("conv_w", cols(x["conv_w"])); put("b_f", np.asarray(x["b_f"], f).reshape(8, 1), 8)
    put("ssm_norm", cols(x["ssm_norm_2"])); put("kv_norm", cols(x["kv_norm_2"]))
    put("attn_norm", cols(x["attn_norm_2"]))
    for n in ("k_norm", "q_norm"):
        put(n, np.tile(np.asarray(x[n + "_2"], f).reshape(1, HD), (1, 2)).T)
    put("subln", cols(x["subln_2"]))
    order = np.arange(2 * FFT).reshape(2, FFT).T.ravel()
    for n in range(2):
        put(f"ffn_norm{n}", cols(x["ffn_norm_2"][n])); put(f"ple_norm{n}", cols(x["ple_norm_2"][n]))
        for tap in range(3):
            V[:, COL[f"ffn_w{n}"] + 44 * tap:COL[f"ffn_w{n}"] + 44 * tap + 44] = \
                cols(x["ffn_conv_w_2"][n][tap])[:, order]
        V[:, COL[f"ffn_b{n}"]:COL[f"ffn_b{n}"] + 44] = cols(x["ffn_conv_b_2"][n])[:, order]
    put("lam_re", cols(x["ssm_lambda_re_2"])); put("lam_im", cols(x["ssm_lambda_im_2"]))
    put("log_dt", cols(np.repeat(np.asarray(x["ssm_log_dt_2"], f).reshape(-1), HD)))
    dsk = np.asarray(x["ssm_d_2"], f).reshape(32, 32).T
    put("ssm_d", np.tile(dsk, (4, 1)))
    put("lambdas", np.stack([np.asarray(x[n + "_2"], f).reshape(HD) for n in
                             ("lambda_q1", "lambda_k1", "lambda_q2", "lambda_k2")], 1), HD)

    def tiles(w, ks, ms):
        w = np.asarray(w, f)
        t = w.reshape(w.shape[0] // P, P, w.shape[1] // P, P)
        o = np.zeros((len(ms), P, 8, P), f)
        o[:, :, :len(ks)] = t[list(ks)][:, :, list(ms)].transpose(2, 1, 0, 3)
        return o

    w_in = np.asarray(x["w_in"], f)[0]
    q, k, v, fg, b, c, u = np.split(w_in, [512, 1024, 1536, 1544, 2056, 2568], axis=1)
    K8 = range(8)
    out = [tiles(m, K8, range(4)) for m in (q, k, v, b)]
    out.append(tiles(np.concatenate([c, u], 1), K8, [0, 4, 1, 5, 2, 6, 3, 7]))
    out.append(tiles(x["w_out"][0], K8, K8))
    for g in range(4):
        out.append(tiles(x["w_ff1"][0], K8, range(8 * g, 8 * g + 8)))
        out.append(tiles(x["w_ff2"][0], range(8 * g, 8 * g + 8), K8))
    out.append(tiles(x["ssm_w_in_2"][0], K8, K8))
    out.append(tiles(x["ssm_w_glu_2"][0], K8, [m + 8 * s for m in range(8) for s in range(2)]))

    def tail(n):
        for kind, g, p0, p1 in FFN_ORDER:
            if kind == "up":
                out.append(tiles(x["ffn_w_up_2"][n], K8, [8 * g + j + FFT * s for j in range(p0, p1) for s in range(2)]))
            elif kind == "down":
                out.append(tiles(x["ffn_w_down_2"][n], range(8 * g, 8 * g + FFG[g]), K8))
            else:
                side = np.asarray(x["ple_w_proj_2"][n], f).reshape(2, P, 2, 4, P)
                out.append(side.transpose(2, 1, 3, 0, 4).reshape(2, P, 8, P))
        out.append(tiles(x["ple_w_gate_2"][n], K8, K8))

    tail(0)
    out.append(tiles(x["attn_w_q_2"][0], K8, K8))
    kv = np.asarray(x["kv_w_2"], f)
    out.append(tiles(kv[:, :D], K8, K8)); out.append(tiles(kv[:, D:], K8, K8))
    out.append(tiles(x["attn_w_o_2"][0], K8, K8))
    tail(1)
    W = np.concatenate(out)
    assert W.shape[0] == NU

    hx = np.concatenate([np.asarray(x["meta_tokens"], f), np.asarray(x["x"], f)[0]], 0)
    eye = np.eye(P, dtype=f)
    grp = lambda a: np.asarray(a, f)[0].reshape(32, P, 16).transpose(1, 0, 2)
    grc = lambda a: np.asarray(a, f)[0].transpose(0, 2, 1).reshape(32, P, 16).transpose(1, 0, 2)
    dist = SEQ - np.arange(640)
    far = np.maximum(dist, 16).astype(f)
    big = 16 + (np.log(far / f(16)) / f(np.log(8.0)) * f(16)).astype(np.int32)
    bucket = np.where(dist < 16, np.maximum(dist, 0), np.minimum(big, 31))
    onehot = np.where(dist < 0, 32, bucket)[None] == np.arange(33)[:, None]
    i = np.arange(P)
    win = np.zeros((P, 64), f)
    win[:HD, 15] = win[HD:, 16] = 1
    win[:, 32 + 15:32 + 17] = 1
    return {
        "wstream": W.reshape(NU * P, 8 * P), "xT": np.ascontiguousarray(hx.T.reshape(8, P, TOK).transpose(1, 0, 2)),
        "vecs": V, "ones": np.ones((P, P), f), "ident": eye, "flip": np.ascontiguousarray(eye[::-1]), "win": win,
        "spread": np.kron(np.eye(16), np.ones((1, HD))).astype(f),
        "mask": np.where(i[None, :] > i[:, None], NEG, 0.0).astype(f),
        "wf": np.ascontiguousarray(fg.reshape(8, P, 8).transpose(1, 0, 2)),
        "ssm_bc": np.ascontiguousarray(np.stack([grp(x["ssm_b_re_2"]), grp(x["ssm_b_im_2"]),
                                                 grc(x["ssm_c_re_2"]), grc(x["ssm_c_im_2"])], 1)),
        "pT": np.ascontiguousarray(np.asarray(x["p_2"], f)[:, 0].transpose(0, 2, 1).reshape(2, 2, P, SEQ)
                                   .transpose(2, 0, 1, 3)),
        "rel": np.concatenate([np.asarray(x["rel_bias_2"], f), np.full((1, 8), NEG, f)]), "onehot": onehot.astype(f),
    }


def kernel(**inputs):
    import concourse.bacc as bacc
    from concourse.bass_utils import run_bass_kernel_spmd

    nc = bacc.Bacc("TRN2", target_bir_lowering=False, num_devices=1)
    arrays = lay_out(inputs)
    A = {n: nc.dram_tensor(f"in_{n}", a.shape, mybir.dt.from_np(a.dtype), kind="ExternalInput").ap()
         for n, a in arrays.items()}
    out = nc.dram_tensor("out", (P, KT, SEQ), F32, kind="ExternalOutput").ap()
    program(nc, A, out)
    got = run_bass_kernel_spmd(nc, [{f"in_{n}": a for n, a in arrays.items()}], core_ids=[0]).results[0]["out"]
    return np.ascontiguousarray(got.transpose(2, 1, 0).reshape(1, SEQ, D))
```
